# Optimizing a Trainium2 kernel written in Bass

```python
import math
import jax, jax.numpy as jnp
from jax import lax
import numpy as np

D_MODEL = 1024
BATCH = 1
SEQ = 256
DEPTH = 1

HEAD_DIM = 64
FOX_HEADS = 8
FOX_WIDTH = FOX_HEADS * HEAD_DIM
DIFF_HEADS = 4
DIFF_QK_WIDTH = DIFF_HEADS * 2 * HEAD_DIM
DIFF_V_DIM = 2 * HEAD_DIM
DIFF_V_WIDTH = DIFF_HEADS * DIFF_V_DIM
IN_WIDTH = 3 * FOX_WIDTH + FOX_HEADS + 2 * DIFF_QK_WIDTH + DIFF_V_WIDTH + 2 * D_MODEL
MEM_LEN = 256
CROSS_HEADS = 4
CROSS_WIDTH = CROSS_HEADS * HEAD_DIM
N_GROUPS = 4
EXPERTS_PER_GROUP = 8
N_EXPERTS = N_GROUPS * EXPERTS_PER_GROUP
TOP_K = 2
D_FF_EXPERT = 512
MOE_BLOCK = 256
Q_BLOCK = 128
ROPE_THETA = 10000.0
NORM_EPS = 1e-6
SUBLN_EPS = 1e-5
FGATE_BIAS_INIT = 3.0


def _rms_norm(t, g, eps=NORM_EPS):
    tf = t.astype(jnp.float32)
    tf = tf * lax.rsqrt(jnp.mean(tf * tf, axis=-1, keepdims=True) + eps)
    return (tf * g.astype(jnp.float32)).astype(t.dtype)

def _split_heads(t, n):
    b, s, w = t.shape
    return t.reshape(b, s, n, w // n).transpose(0, 2, 1, 3)

def _merge_heads(t):
    b, h, s, d = t.shape
    return t.transpose(0, 2, 1, 3).reshape(b, s, h * d)

def _in_offsets():
    sizes = (FOX_WIDTH, FOX_WIDTH, FOX_WIDTH, FOX_HEADS, DIFF_QK_WIDTH, DIFF_QK_WIDTH,
             DIFF_V_WIDTH, D_MODEL, D_MODEL)
    return [int(o) for o in np.cumsum(sizes)[:-1]]

def _rope_tables(positions, dtype):
    half = HEAD_DIM // 2
    inv_freq = ROPE_THETA ** (-jnp.arange(half, dtype=jnp.float32) * 2.0 / HEAD_DIM)
    ang = positions.astype(jnp.float32)[..., None] * inv_freq
    cos = jnp.cos(ang)[:, :, None, None, :].astype(dtype)
    sin = jnp.sin(ang)[:, :, None, None, :].astype(dtype)
    return cos, sin

def _rope(t, cos, sin):
    half = t.shape[-1] // 2
    t1, t2 = t[..., :half], t[..., half:]
    return jnp.concatenate([t1 * cos - t2 * sin, t2 * cos + t1 * sin], axis=-1)

def _causal_mask(q0, q1):
    qpos = q0 + jnp.arange(q1 - q0)
    kpos = jnp.arange(q1)
    return qpos[:, None] >= kpos[None, :]

def _fox_attention(q, k, v, log_f):
    c = jnp.cumsum(log_f, axis=-1)
    scale = HEAD_DIM ** -0.5
    n_q = q.shape[2]
    outs = []
    for blk in range(n_q // Q_BLOCK):
        q0, q1 = blk * Q_BLOCK, (blk + 1) * Q_BLOCK
        s = jnp.einsum('bhqd,bhkd->bhqk', q[:, :, q0:q1], k[:, :, :q1]).astype(jnp.float32) * scale
        s = s + c[:, :, q0:q1, None] - c[:, :, None, :q1]
        s = jnp.where(_causal_mask(q0, q1), s, -jnp.inf)
        p = jax.nn.softmax(s, axis=-1).astype(v.dtype)
        outs.append(jnp.einsum('bhqk,bhkd->bhqd', p, v[:, :, :q1]))
    return jnp.concatenate(outs, axis=2)

def _diff_attention(q1, q2, k1, k2, v, lam):
    scale = HEAD_DIM ** -0.5
    n_q = q1.shape[2]
    outs = []
    for blk in range(n_q // Q_BLOCK):
        q0, qe = blk * Q_BLOCK, (blk + 1) * Q_BLOCK
        mask = _causal_mask(q0, qe)
        s1 = jnp.einsum('bhqd,bhkd->bhqk', q1[:, :, q0:qe], k1[:, :, :qe]).astype(jnp.float32) * scale
        s2 = jnp.einsum('bhqd,bhkd->bhqk', q2[:, :, q0:qe], k2[:, :, :qe]).astype(jnp.float32) * scale
        p1 = jax.nn.softmax(jnp.where(mask, s1, -jnp.inf), axis=-1)
        p2 = jax.nn.softmax(jnp.where(mask, s2, -jnp.inf), axis=-1)
        a = (p1 - lam * p2).astype(v.dtype)
        outs.append(jnp.einsum('bhqk,bhkd->bhqd', a, v[:, :, :qe]))
    return jnp.concatenate(outs, axis=2)

def _cross_attention(hx, hm, w_q, w_kv, w_o):
    b, m = hm.shape[0], hm.shape[1]
    q = _split_heads(hx @ w_q, CROSS_HEADS)
    kv = (hm @ w_kv).reshape(b, m, 2, CROSS_HEADS, HEAD_DIM)
    k = kv[:, :, 0].transpose(0, 2, 1, 3)
    v = kv[:, :, 1].transpose(0, 2, 1, 3)
    s = jnp.einsum('bhsd,bhmd->bhsm', q, k).astype(jnp.float32) * HEAD_DIM ** -0.5
    p = jax.nn.softmax(s, axis=-1).astype(v.dtype)
    return _merge_heads(jnp.einsum('bhsm,bhmd->bhsd', p, v)) @ w_o

def _routed_experts(t, expert_ids, gate_w, w_gate, w_up, w_down):
    n_tok, d = t.shape
    n_assign = n_tok * TOP_K
    flat_e = expert_ids.reshape(n_assign).astype(jnp.int32)
    flat_tok = jnp.arange(n_assign, dtype=jnp.int32) // TOP_K
    flat_w = gate_w.reshape(n_assign)
    order = jnp.argsort(flat_e)
    e_sorted = flat_e[order]
    counts = jnp.zeros((N_EXPERTS,), jnp.int32).at[flat_e].add(1)
    padded = (counts + MOE_BLOCK - 1) // MOE_BLOCK * MOE_BLOCK
    pad_end = jnp.cumsum(padded)
    pad_start = pad_end - padded
    seg_start = jnp.cumsum(counts) - counts
    dest = pad_start[e_sorted] + jnp.arange(n_assign, dtype=jnp.int32) - seg_start[e_sorted]
    n_blocks = -(-n_assign // MOE_BLOCK) + N_EXPERTS
    n_rows = n_blocks * MOE_BLOCK
    row_tok = jnp.full((n_rows,), n_tok, jnp.int32).at[dest].set(flat_tok[order])
    row_w = jnp.zeros((n_rows,), t.dtype).at[dest].set(flat_w[order])
    block_start = jnp.arange(n_blocks, dtype=jnp.int32) * MOE_BLOCK
    block_expert = jnp.minimum(jnp.searchsorted(pad_end, block_start, side='right'), N_EXPERTS - 1)
    t_pad = jnp.concatenate([t, jnp.zeros((1, d), t.dtype)], axis=0)
    xs = t_pad[row_tok].reshape(n_blocks, MOE_BLOCK, d)

    def expert_block(args):
        xb, e = args
        hb = jax.nn.silu(xb @ w_gate[e]) * (xb @ w_up[e])
        return hb @ w_down[e]

    ys = lax.map(expert_block, (xs, block_expert)).reshape(n_rows, d)
    out = jnp.zeros((n_tok + 1, d), t.dtype).at[row_tok].add(ys * row_w[:, None])
    return out[:n_tok]

def _hier_moe(t, w_group, b_group, w_expert, b_expert, w_gate, w_up, w_down):
    n_tok = t.shape[0]
    group_logits = (t @ w_group + b_group).astype(jnp.float32)
    group_prob = jax.nn.softmax(group_logits, axis=-1)
    g_sel = jnp.argmax(group_logits, axis=-1)
    g_w = jnp.take_along_axis(group_prob, g_sel[:, None], axis=-1)
    exp_logits = (t @ w_expert + b_expert).astype(jnp.float32).reshape(n_tok, N_GROUPS, EXPERTS_PER_GROUP)
    sel_logits = jnp.take_along_axis(exp_logits, g_sel[:, None, None], axis=1)[:, 0]
    top_vals, top_idx = lax.top_k(sel_logits, TOP_K)
    weights = jax.nn.softmax(top_vals, axis=-1) * g_w
    expert_ids = g_sel[:, None].astype(jnp.int32) * EXPERTS_PER_GROUP + top_idx.astype(jnp.int32)
    return _routed_experts(t, expert_ids, weights.astype(t.dtype), w_gate, w_up, w_down)

def first_inputs(seed: int = 0) -> dict:
    key = jax.random.key(seed)
    ks = jax.random.split(key, 32)
    f32 = jnp.float32
    L = DEPTH

    def nrm(k, shape, fan_in):
        return jax.random.normal(k, shape, f32) * fan_in ** -0.5

    def gain(k, shape):
        return 1.0 + 0.02 * jax.random.normal(k, shape, f32)

    return {
        'x': jax.random.normal(ks[0], (BATCH, SEQ, D_MODEL), f32),
        'mem': jax.random.normal(ks[1], (BATCH, MEM_LEN, D_MODEL), f32),
        'positions': jnp.broadcast_to(jnp.arange(SEQ, dtype=jnp.int32), (BATCH, SEQ)),
        'g_mix': gain(ks[2], (L, D_MODEL)),
        'w_in': nrm(ks[3], (L, D_MODEL, IN_WIDTH), D_MODEL),
        'b_fgate': FGATE_BIAS_INIT + 0.1 * jax.random.normal(ks[4], (L, FOX_HEADS), f32),
        'w_branch_a': nrm(ks[5], (L, FOX_WIDTH, D_MODEL), FOX_WIDTH),
        'w_branch_b': nrm(ks[6], (L, DIFF_V_WIDTH, D_MODEL), DIFF_V_WIDTH),
        'w_out': nrm(ks[7], (L, D_MODEL, D_MODEL), D_MODEL),
        'lambda_q1': 0.1 * jax.random.normal(ks[8], (L, HEAD_DIM), f32),
        'lambda_k1': 0.1 * jax.random.normal(ks[9], (L, HEAD_DIM), f32),
        'lambda_q2': 0.1 * jax.random.normal(ks[10], (L, HEAD_DIM), f32),
        'lambda_k2': 0.1 * jax.random.normal(ks[11], (L, HEAD_DIM), f32),
        'g_diff_sub': gain(ks[12], (L, DIFF_V_DIM)),
        'g_cross': gain(ks[13], (L, D_MODEL)),
        'g_mem': gain(ks[14], (L, D_MODEL)),
        'w_cq': nrm(ks[15], (L, D_MODEL, CROSS_WIDTH), D_MODEL),
        'w_ckv': nrm(ks[16], (L, D_MODEL, 2 * CROSS_WIDTH), D_MODEL),
        'w_co': nrm(ks[17], (L, CROSS_WIDTH, D_MODEL), CROSS_WIDTH),
        'g_ffn': gain(ks[18], (L, D_MODEL)),
        'w_group': nrm(ks[19], (L, D_MODEL, N_GROUPS), D_MODEL),
        'b_group': 0.01 * jax.random.normal(ks[20], (L, N_GROUPS), f32),
        'w_expert': nrm(ks[21], (L, D_MODEL, N_EXPERTS), D_MODEL),
        'b_expert': 0.01 * jax.random.normal(ks[22], (L, N_EXPERTS), f32),
        'w_exp_gate': nrm(ks[23], (L, N_EXPERTS, D_MODEL, D_FF_EXPERT), D_MODEL),
        'w_exp_up': nrm(ks[24], (L, N_EXPERTS, D_MODEL, D_FF_EXPERT), D_MODEL),
        'w_exp_down': nrm(ks[25], (L, N_EXPERTS, D_FF_EXPERT, D_MODEL), D_FF_EXPERT),
        'g_final': gain(ks[26], (D_MODEL,)),
    }

def first_block(x, mem, positions, g_mix, w_in, b_fgate, w_branch_a, w_branch_b, w_out,
              lambda_q1, lambda_k1, lambda_q2, lambda_k2, g_diff_sub, g_cross, g_mem,
              w_cq, w_ckv, w_co, g_ffn, w_group, b_group, w_expert, b_expert,
              w_exp_gate, w_exp_up, w_exp_down, g_final):
    b, s, d = x.shape
    cos, sin = _rope_tables(positions, x.dtype)
    offsets = _in_offsets()
    for l in range(DEPTH):
        lambda_init = 0.8 - 0.6 * math.exp(-0.3 * l)
        h = _rms_norm(x, g_mix[l])
        fq, fk, fv, f_logit, dq, dk, dv, gate_a, gate_b = jnp.split(h @ w_in[l], offsets, axis=-1)
        log_f = jax.nn.log_sigmoid((f_logit + b_fgate[l]).astype(jnp.float32)).transpose(0, 2, 1)
        y_a = _fox_attention(_split_heads(fq, FOX_HEADS), _split_heads(fk, FOX_HEADS),
                             _split_heads(fv, FOX_HEADS), log_f)
        y_a = _merge_heads(y_a)
        dq = _rope(dq.reshape(b, s, DIFF_HEADS, 2, HEAD_DIM), cos, sin)
        dk = _rope(dk.reshape(b, s, DIFF_HEADS, 2, HEAD_DIM), cos, sin)
        lam = (jnp.exp(jnp.sum(lambda_q1[l].astype(jnp.float32) * lambda_k1[l].astype(jnp.float32)))
               - jnp.exp(jnp.sum(lambda_q2[l].astype(jnp.float32) * lambda_k2[l].astype(jnp.float32)))
               + lambda_init)
        y_b = _diff_attention(dq[:, :, :, 0].transpose(0, 2, 1, 3), dq[:, :, :, 1].transpose(0, 2, 1, 3),
                              dk[:, :, :, 0].transpose(0, 2, 1, 3), dk[:, :, :, 1].transpose(0, 2, 1, 3),
                              _split_heads(dv, DIFF_HEADS), lam)
        y_b = _merge_heads(_rms_norm(y_b, g_diff_sub[l], SUBLN_EPS) * (1.0 - lambda_init))
        merged = (jax.nn.sigmoid(gate_a) * (y_a @ w_branch_a[l])
                  + jax.nn.sigmoid(gate_b) * (y_b @ w_branch_b[l]))
        x = x + merged @ w_out[l]
        x = x + _cross_attention(_rms_norm(x, g_cross[l]), _rms_norm(mem, g_mem[l]),
                                 w_cq[l], w_ckv[l], w_co[l])
        hm = _rms_norm(x, g_ffn[l]).reshape(b * s, d)
        x = x + _hier_moe(hm, w_group[l], b_group[l], w_expert[l], b_expert[l],
                          w_exp_gate[l], w_exp_up[l], w_exp_down[l]).reshape(b, s, d)
    return _rms_norm(x, g_final)


DEPTH_2 = 2

CTX_LEN = 256
GRID_W = 64
N_MOD = 9
D_FF = 2816
EPS = 1e-6
A_HEADS = 4
A_HEAD_DIM = 128
A_WIDTH = A_HEADS * A_HEAD_DIM
MLSTM_CHUNK = 128
CONV_W = 3
B_GROUPS = 4
B_GROUP_DIM = 128
B_WIDTH = B_GROUPS * B_GROUP_DIM
SGU_CHUNK = 128
EVEN_IN = 4 * A_WIDTH + 4 * A_HEADS + 2 * B_WIDTH
EVEN_MIX = A_WIDTH + B_WIDTH
C_HEADS = 16
C_KV_HEADS = 4
C_GROUP = C_HEADS // C_KV_HEADS
C_HEAD_DIM = 64
WINDOW = 128
ATTN_BLOCK = 128
ODD_QKV = (C_HEADS + 2 * C_KV_HEADS) * C_HEAD_DIM
ROPE_BASE = 10000.0
N_EVEN = (DEPTH_2 + 1) // 2
N_ODD = DEPTH_2 // 2


f32 = jnp.float32

def _rms_norm_2(t):
    tf = t.astype(f32)
    return (tf * lax.rsqrt(jnp.mean(tf * tf, axis=-1, keepdims=True) + EPS)).astype(t.dtype)

def _modulation(s, w, b):
    m = s @ w + b
    return m.reshape(s.shape[0], N_MOD, 1, D_MODEL)

def _modulate(h, shift, scale):
    return _rms_norm_2(h) * (1.0 + scale) + shift

def _swiglu(h, w_in, w_out):
    g, u = jnp.split(h @ w_in, 2, axis=-1)
    return (jax.nn.silu(g) * u) @ w_out

def _axial_rope_tables(T):
    rows = T // GRID_W
    row, col = jnp.meshgrid(jnp.arange(rows), jnp.arange(GRID_W), indexing='ij')
    n_freq = C_HEAD_DIM // 4
    inv = ROPE_BASE ** (-jnp.arange(n_freq, dtype=f32) / n_freq)
    ang = jnp.concatenate([row.reshape(-1, 1).astype(f32) * inv,
                           col.reshape(-1, 1).astype(f32) * inv], axis=-1)
    return jnp.cos(ang), jnp.sin(ang)

def _apply_rope(t, cos, sin):
    x1, x2 = t[..., 0::2], t[..., 1::2]
    cs = cos[None, :, None, :].astype(t.dtype)
    sn = sin[None, :, None, :].astype(t.dtype)
    return jnp.stack([x1 * cs - x2 * sn, x1 * sn + x2 * cs], axis=-1).reshape(t.shape)

def _centred_depthwise_conv(x, w):
    C = x.shape[-1]
    return lax.conv_general_dilated(x, w[:, None, :].astype(x.dtype), window_strides=(1,),
                                    padding=[(CONV_W // 2, CONV_W // 2)],
                                    dimension_numbers=('NWC', 'WIO', 'NWC'),
                                    feature_group_count=C)

def _zero_state(B_):
    return (jnp.zeros((B_, A_HEADS, A_HEAD_DIM, A_HEAD_DIM), f32),
            jnp.zeros((B_, A_HEADS, A_HEAD_DIM), f32),
            jnp.zeros((B_, A_HEADS), f32))

def _mlstm_chunkwise(q, k, v, ig, lf, state):
    B_, H, T, d = q.shape
    L = MLSTM_CHUNK
    N = T // L
    q = q.reshape(B_, H, N, L, d)
    k = k.reshape(B_, H, N, L, d)
    v = v.reshape(B_, H, N, L, d)
    ig = ig.reshape(B_, H, N, L)
    b = jnp.cumsum(lf.reshape(B_, H, N, L), axis=-1)
    g = b[..., -1]
    a = g[..., None] - b + ig
    m_loc = jnp.max(a, axis=-1)
    w = jnp.exp(a - m_loc[..., None])
    C_loc = jnp.einsum('bhnl,bhnld,bhnle->bhnde', w, k, v)
    n_loc = jnp.einsum('bhnl,bhnld->bhnd', w, k)

    def step(carry, xs):
        C, n, m = carry
        g_j, m_loc_j, C_loc_j, n_loc_j = xs
        m_new = jnp.maximum(g_j + m, m_loc_j)
        dec = jnp.exp(g_j + m - m_new)
        add = jnp.exp(m_loc_j - m_new)
        C_new = dec[..., None, None] * C + add[..., None, None] * C_loc_j
        n_new = dec[..., None] * n + add[..., None] * n_loc_j
        return (C_new, n_new, m_new), (C, n, m)

    xs = (jnp.moveaxis(g, 2, 0), jnp.moveaxis(m_loc, 2, 0),
          jnp.moveaxis(C_loc, 2, 0), jnp.moveaxis(n_loc, 2, 0))
    final, (C_prev, n_prev, m_prev) = lax.scan(step, state, xs)
    C_prev = jnp.moveaxis(C_prev, 0, 2)
    n_prev = jnp.moveaxis(n_prev, 0, 2)
    m_prev = jnp.moveaxis(m_prev, 0, 2)

    e = b + m_prev[..., None]
    tril = jnp.tril(jnp.ones((L, L), dtype=bool))
    Dm = jnp.where(tril, b[..., :, None] - b[..., None, :] + ig[..., None, :], -jnp.inf)
    m_t = jnp.maximum(e, jnp.max(Dm, axis=-1))
    S = jnp.einsum('bhntd,bhnsd->bhnts', q, k) * jnp.exp(Dm - m_t[..., None])
    inter = jnp.exp(e - m_t)
    num = (jnp.einsum('bhnts,bhnse->bhnte', S, v)
           + inter[..., None] * jnp.einsum('bhntd,bhnde->bhnte', q, C_prev))
    den = jnp.sum(S, axis=-1) + inter * jnp.einsum('bhntd,bhnd->bhnt', q, n_prev)
    h = num / jnp.maximum(jnp.abs(den), jnp.exp(-m_t))[..., None]
    return h.reshape(B_, H, T, d), final

def _flip(ts):
    return tuple(jnp.flip(t, axis=2) for t in ts)

def _even_stream_inputs(n, w_in, conv_w, gate_b):
    B_, T, _ = n.shape
    p = n @ w_in
    qk, v, o, gates, uv = jnp.split(
        p, [2 * A_WIDTH, 3 * A_WIDTH, 4 * A_WIDTH, 4 * A_WIDTH + 4 * A_HEADS], axis=-1)
    q, k = jnp.split(jax.nn.silu(_centred_depthwise_conv(qk, conv_w)), 2, axis=-1)

    def heads(t):
        return t.reshape(B_, T, A_HEADS, A_HEAD_DIM).transpose(0, 2, 1, 3).astype(f32)

    q, k, v = heads(q), heads(k) * (A_HEAD_DIM ** -0.5), heads(v)
    gt = (gates.astype(f32) + gate_b.reshape(-1).astype(f32)).reshape(B_, T, 4, A_HEADS).transpose(2, 0, 3, 1)
    fwd = (gt[0], jax.nn.log_sigmoid(gt[1]))
    bwd = (gt[2], jax.nn.log_sigmoid(gt[3]))
    return (q, k, v), fwd, bwd, o, uv

def _spatial_gating(uv, norm_g, ws, sb):
    u, v = jnp.split(jax.nn.gelu(uv), 2, axis=-1)
    v = _rms_norm_2(v) * norm_g
    B_, T, _ = v.shape
    vb = v.reshape(B_, T // SGU_CHUNK, SGU_CHUNK, B_GROUPS, B_GROUP_DIM)
    mixed = jnp.einsum('gpq,bnqgc->bnpgc', ws, vb) + sb.T[:, :, None]
    return u * mixed.reshape(B_, T, B_WIDTH)

def _even_output(hsum, o, uv, mnorm, sgu_g, ws, sb, w_out):
    B_, H, T, d = hsum.shape
    hn = hsum * lax.rsqrt(jnp.mean(hsum * hsum, axis=-1, keepdims=True) + EPS) * mnorm[None, :, None, :].astype(f32)
    h_a = jax.nn.sigmoid(o) * hn.transpose(0, 2, 1, 3).reshape(B_, T, A_WIDTH).astype(o.dtype)
    h_b = _spatial_gating(uv, sgu_g, ws, sb)
    return jnp.concatenate([h_a, h_b], axis=-1) @ w_out

def _even_mixer(nx, nc, w_in, w_out, conv_w, gate_b, mnorm, sgu_g, ws, sb, need_ctx):
    qkv_c, fw_c, bw_c, o_c, uv_c = _even_stream_inputs(nc, w_in, conv_w, gate_b)
    qkv_x, fw_x, bw_x, o_x, uv_x = _even_stream_inputs(nx, w_in, conv_w, gate_b)
    zero = _zero_state(nx.shape[0])
    hc_f, st_f = _mlstm_chunkwise(*qkv_c, *fw_c, zero)
    hc_b, st_b = _mlstm_chunkwise(*_flip(qkv_c), *_flip(bw_c), zero)
    hx_f, _ = _mlstm_chunkwise(*qkv_x, *fw_x, st_f)
    hx_b, _ = _mlstm_chunkwise(*_flip(qkv_x), *_flip(bw_x), st_b)
    yx = _even_output(hx_f + jnp.flip(hx_b, axis=2), o_x, uv_x, mnorm, sgu_g, ws, sb, w_out)
    yc = None
    if need_ctx:
        yc = _even_output(hc_f + jnp.flip(hc_b, axis=2), o_c, uv_c, mnorm, sgu_g, ws, sb, w_out)
    return yx, yc

def _softmax_with_sink(sink, *scores):
    ref = scores[0]
    s0 = jnp.broadcast_to(sink[None, :, :, None, None].astype(f32), ref.shape[:-1] + (1,))
    p = jax.nn.softmax(jnp.concatenate([s0] + [s.astype(f32) for s in scores], axis=-1), axis=-1)
    parts = []
    off = 1
    for s in scores:
        parts.append(p[..., off:off + s.shape[-1]])
        off += s.shape[-1]
    return parts

def _window_attention(q, k, v, kc, vc, sink):
    B_, T, _, _ = q.shape
    nb = T // ATTN_BLOCK
    scale = C_HEAD_DIM ** -0.5
    qb = (q * scale).reshape(B_, nb, ATTN_BLOCK, C_KV_HEADS, C_GROUP, C_HEAD_DIM).transpose(1, 0, 2, 3, 4, 5)
    pad = ((0, 0), (ATTN_BLOCK, ATTN_BLOCK), (0, 0), (0, 0))
    kp, vp = jnp.pad(k, pad), jnp.pad(v, pad)
    offs = jnp.arange(ATTN_BLOCK)
    band_offs = jnp.arange(3 * ATTN_BLOCK) - ATTN_BLOCK

    def block(args):
        qj, j = args
        start = j * ATTN_BLOCK
        kj = lax.dynamic_slice_in_dim(kp, start, 3 * ATTN_BLOCK, axis=1)
        vj = lax.dynamic_slice_in_dim(vp, start, 3 * ATTN_BLOCK, axis=1)
        qpos = start + offs
        kpos = start + band_offs
        valid = (jnp.abs(qpos[:, None] - kpos[None, :]) <= WINDOW) & (kpos[None, :] >= 0) & (kpos[None, :] < T)
        s_band = jnp.where(valid, jnp.einsum('bqhgd,bkhd->bhgqk', qj, kj).astype(f32), -jnp.inf)
        s_ctx = jnp.einsum('bqhgd,bkhd->bhgqk', qj, kc)
        p_ctx, p_band = _softmax_with_sink(sink, s_ctx, s_band)
        return (jnp.einsum('bhgqk,bkhd->bqhgd', p_ctx.astype(vc.dtype), vc)
                + jnp.einsum('bhgqk,bkhd->bqhgd', p_band.astype(vj.dtype), vj))

    out = lax.map(block, (qb, jnp.arange(nb)))
    return out.transpose(1, 0, 2, 3, 4, 5).reshape(B_, T, C_HEADS * C_HEAD_DIM)

def _context_attention(qc, kc, vc, sink):
    B_, Tc = qc.shape[:2]
    q = (qc * (C_HEAD_DIM ** -0.5)).reshape(B_, Tc, C_KV_HEADS, C_GROUP, C_HEAD_DIM)
    (p,) = _softmax_with_sink(sink, jnp.einsum('bqhgd,bkhd->bhgqk', q, kc))
    return jnp.einsum('bhgqk,bkhd->bqhgd', p.astype(vc.dtype), vc).reshape(B_, Tc, C_HEADS * C_HEAD_DIM)

def _odd_mixer(nx, nc, w_qkv, w_out, sink, cos, sin, need_ctx):
    B_, T, _ = nx.shape
    Tc = nc.shape[1]
    qdim = C_HEADS * C_HEAD_DIM
    kvdim = C_KV_HEADS * C_HEAD_DIM
    q, k, v = jnp.split(nx @ w_qkv, [qdim, qdim + kvdim], axis=-1)
    q = _apply_rope(q.reshape(B_, T, C_HEADS, C_HEAD_DIM), cos, sin)
    k = _apply_rope(k.reshape(B_, T, C_KV_HEADS, C_HEAD_DIM), cos, sin)
    v = v.reshape(B_, T, C_KV_HEADS, C_HEAD_DIM)
    kc, vc = jnp.split(nc @ w_qkv[:, qdim:], 2, axis=-1)
    kc = kc.reshape(B_, Tc, C_KV_HEADS, C_HEAD_DIM)
    vc = vc.reshape(B_, Tc, C_KV_HEADS, C_HEAD_DIM)
    sink = sink.reshape(C_KV_HEADS, C_GROUP)
    yx = _window_attention(q, k, v, kc, vc, sink) @ w_out
    yc = None
    if need_ctx:
        qc = (nc @ w_qkv[:, :qdim]).reshape(B_, Tc, C_HEADS, C_HEAD_DIM)
        yc = _context_attention(qc, kc, vc, sink) @ w_out
    return yx, yc

def second_inputs(seed: int = 0) -> dict:
    key = jax.random.key(seed)
    ks = jax.random.split(key, 20)
    D = D_MODEL

    def nrm(k, shape, scale):
        return jax.random.normal(k, shape, jnp.float32) * scale

    is_forget = jnp.array([0.0, 1.0, 0.0, 1.0], jnp.float32)[:, None]
    forget_lin = jnp.linspace(3.0, 6.0, A_HEADS, dtype=jnp.float32)[None, :]
    return {
        'x': nrm(ks[0], (BATCH, SEQ, D), 1.0),
        'c': nrm(ks[1], (BATCH, D), 1.0),
        'ctx': nrm(ks[2], (BATCH, CTX_LEN, D), 1.0),
        'c_ctx': nrm(ks[3], (D,), 1.0),
        'ada_w': nrm(ks[4], (DEPTH_2, D, N_MOD * D), 0.5 * D ** -0.5),
        'ada_b': nrm(ks[5], (DEPTH_2, N_MOD * D), 0.02),
        'ffn_w_in': nrm(ks[6], (DEPTH_2, 2, D, 2 * D_FF), D ** -0.5),
        'ffn_w_out': nrm(ks[7], (DEPTH_2, 2, D_FF, D), D_FF ** -0.5),
        'even_w_in': nrm(ks[8], (N_EVEN, D, EVEN_IN), D ** -0.5),
        'even_w_out': nrm(ks[9], (N_EVEN, EVEN_MIX, D), EVEN_MIX ** -0.5),
        'mlstm_conv': nrm(ks[10], (N_EVEN, CONV_W, 2 * A_WIDTH), CONV_W ** -0.5),
        'mlstm_gate_b': is_forget * forget_lin + nrm(ks[11], (N_EVEN, 4, A_HEADS), 0.1),
        'mlstm_norm': 1.0 + nrm(ks[12], (N_EVEN, A_HEADS, A_HEAD_DIM), 0.05),
        'sgu_norm': 1.0 + nrm(ks[13], (N_EVEN, B_WIDTH), 0.05),
        'sgu_ws': nrm(ks[14], (N_EVEN, B_GROUPS, SGU_CHUNK, SGU_CHUNK), SGU_CHUNK ** -0.5),
        'sgu_b': 1.0 + nrm(ks[15], (N_EVEN, B_GROUPS, SGU_CHUNK), 0.1),
        'odd_w_qkv': nrm(ks[16], (N_ODD, D, ODD_QKV), D ** -0.5),
        'odd_w_out': nrm(ks[17], (N_ODD, C_HEADS * C_HEAD_DIM, D), (C_HEADS * C_HEAD_DIM) ** -0.5),
        'attn_sink': nrm(ks[18], (N_ODD, C_HEADS), 0.5),
        'final_norm': 1.0 + nrm(ks[19], (D,), 0.05),
    }

def second_block(x, c, ctx, c_ctx, ada_w, ada_b, ffn_w_in, ffn_w_out, even_w_in, even_w_out,
              mlstm_conv, mlstm_gate_b, mlstm_norm, sgu_norm, sgu_ws, sgu_b,
              odd_w_qkv, odd_w_out, attn_sink, final_norm):
    cos, sin = _axial_rope_tables(x.shape[1])
    sc = jax.nn.silu(c)
    scc = jax.nn.silu(c_ctx)[None]
    h, hc = x, ctx
    for layer in range(DEPTH_2):
        last = layer == DEPTH_2 - 1
        mod = _modulation(sc, ada_w[layer], ada_b[layer])
        modc = _modulation(scc, ada_w[layer], ada_b[layer])
        h = h + 0.5 * mod[:, 2] * _swiglu(_modulate(h, mod[:, 0], mod[:, 1]),
                                          ffn_w_in[layer, 0], ffn_w_out[layer, 0])
        hc = hc + 0.5 * modc[:, 2] * _swiglu(_modulate(hc, modc[:, 0], modc[:, 1]),
                                             ffn_w_in[layer, 0], ffn_w_out[layer, 0])
        nx = _modulate(h, mod[:, 3], mod[:, 4])
        nc = _modulate(hc, modc[:, 3], modc[:, 4])
        if layer % 2 == 0:
            e = layer // 2
            yx, yc = _even_mixer(nx, nc, even_w_in[e], even_w_out[e], mlstm_conv[e], mlstm_gate_b[e],
                                 mlstm_norm[e], sgu_norm[e], sgu_ws[e], sgu_b[e], not last)
        else:
            o = layer // 2
            yx, yc = _odd_mixer(nx, nc, odd_w_qkv[o], odd_w_out[o], attn_sink[o], cos, sin, not last)
        h = h + mod[:, 5] * yx
        h = h + 0.5 * mod[:, 8] * _swiglu(_modulate(h, mod[:, 6], mod[:, 7]),
                                          ffn_w_in[layer, 1], ffn_w_out[layer, 1])
        if not last:
            hc = hc + modc[:, 5] * yc
            hc = hc + 0.5 * modc[:, 8] * _swiglu(_modulate(hc, modc[:, 6], modc[:, 7]),
                                                 ffn_w_in[layer, 1], ffn_w_out[layer, 1])
    return _rms_norm_2(h) * final_norm


def setup_inputs(seed=0):
    out = dict(first_inputs(seed))
    for name, value in second_inputs(seed + 1).items():
        if name != "x":
            out[name + "_2"] = value
    return out


def reference(
    x, mem, positions, g_mix, w_in, b_fgate, w_branch_a, w_branch_b, w_out, lambda_q1,
    lambda_k1, lambda_q2, lambda_k2, g_diff_sub, g_cross, g_mem, w_cq, w_ckv, w_co, g_ffn,
    w_group, b_group, w_expert, b_expert, w_exp_gate, w_exp_up, w_exp_down, g_final, c_2, ctx_2,
    c_ctx_2, ada_w_2, ada_b_2, ffn_w_in_2, ffn_w_out_2, even_w_in_2, even_w_out_2, mlstm_conv_2,
    mlstm_gate_b_2, mlstm_norm_2, sgu_norm_2, sgu_ws_2, sgu_b_2, odd_w_qkv_2, odd_w_out_2,
    attn_sink_2, final_norm_2,
):
    x = first_block(
        x, mem, positions, g_mix, w_in, b_fgate, w_branch_a, w_branch_b, w_out, lambda_q1,
        lambda_k1, lambda_q2, lambda_k2, g_diff_sub, g_cross, g_mem, w_cq, w_ckv, w_co, g_ffn,
        w_group, b_group, w_expert, b_expert, w_exp_gate, w_exp_up, w_exp_down, g_final,
    )
    return second_block(
        x, c_2, ctx_2, c_ctx_2, ada_w_2, ada_b_2, ffn_w_in_2, ffn_w_out_2, even_w_in_2,
        even_w_out_2, mlstm_conv_2, mlstm_gate_b_2, mlstm_norm_2, sgu_norm_2, sgu_ws_2, sgu_b_2,
        odd_w_qkv_2, odd_w_out_2, attn_sink_2, final_norm_2,
    )


_drawn_inputs = setup_inputs


def setup_inputs(seed=0):
    import zlib

    import numpy as np

    out = dict(_drawn_inputs(seed))
    spreads = {}
    factors = {'lambda_k1': 8.0,
     'lambda_q2': 8.0,
     'g_diff_sub': 3.488,
     'g_cross': 8.0,
     'g_mem': 8.0,
     'b_group': 32.344,
     'b_expert': 46.104,
     'g_final': 2.71,
     'mlstm_norm_2': 28.962,
     'sgu_norm_2': 23.516,
     'sgu_b_2': 11.827,
     'attn_sink_2': 200.0,
     'g_ffn': 8.0,
     'odd_w_out_2': 2.967}
    for name, (base, spread) in spreads.items():
        noise = np.random.default_rng([zlib.crc32(name.encode()), seed]).standard_normal(out[name].shape)
        drawn = base * np.exp(spread * noise) if base else spread * noise
        out[name] = __import__('jax').numpy.asarray(drawn.astype(out[name].dtype))
    for name, factor in factors.items():
        out[name] = (out[name] * factor).astype(out[name].dtype)
    return out
```

```python
from contextlib import ExitStack

import numpy as np

import concourse.bass as bass
from concourse import mybir

F32 = mybir.dt.float32
F32R = mybir.dt.float32r
I32 = mybir.dt.int32
ALU = mybir.AluOpType
ACT = mybir.ActivationFunctionType
AX = mybir.AxisListType

P = 128
D = 1024
KC = D // P
TOK = 256
HD = 64
PIECE = 2048
RAW_SLOTS = 4
SPLIT_SLOTS = 2
EXPERTS = 32
GROUPS = 4
FF_CHUNKS = 22
NEG = -1.0e30
EPS = 1e-6
MAGIC = 1.5 * 2.0 ** 23
LAMBDA_INIT = 0.8 - 0.6 * float(np.exp(0.0))
GELU_C = float(np.sqrt(2.0 / np.pi))

N_FIRST, N_EXPERT, N_UP, N_DOWN, N_EVEN, N_ODD = 32, 6 * EXPERTS, 22, 11, 16, 10
N_ADA, ADA_LOCAL = 72, 32
QKV_PIECES, EVEN_IN_PIECES = 12, 12

PARAM_FIELDS = [("g_mix", 8), ("g_cross", 8), ("g_mem", 8), ("g_ffn", 8), ("g_final", 8),
                ("final_norm", 8), ("g_sub", 1), ("lam_a", 128), ("lam_b", 128),
                ("w_fgate", 64), ("w_router", 288), ("w_gates", 128), ("b_fgate", 8),
                ("b_router", 36), ("ada_b", 144), ("conv_w", 24), ("gate_b", 16), ("mnorm", 4),
                ("sgu_norm", 512), ("sgu_ws", 512), ("sgu_b", 512), ("sink", 16), ("cond", 16)]
CONST_FIELDS = [("ident", 128), ("mask", 384), ("upto", 128), ("from", 128), ("turn_half", 128),
                ("turn_pair", 128), ("cos_x", 256), ("sin_x", 256), ("inv_freq", 1),
                ("one_over", 2), ("down4", 4), ("down32", 32)]


def columns(fields):
    at, out = 0, {}
    for name, n in fields:
        out[name] = (at, at + n)
        at += n
    return out, at


PARAM_AT, N_PARAM = columns(PARAM_FIELDS)
CONST_AT, N_CONST = columns(CONST_FIELDS)


def shape_constants():
    i = np.arange(P)
    c = {}
    c["ident"] = np.eye(P)
    zero = np.zeros((P, P))
    c["mask"] = np.concatenate([np.where(i[None, :] >= i[:, None], 0.0, NEG), zero,
                                np.where(i[None, :] <= i[:, None], 0.0, NEG)], 1)
    c["upto"] = (i[:, None] <= i[None, :]) * 1.0
    c["from"] = (i[:, None] >= i[None, :]) * 1.0
    half = np.zeros((P, P))
    pair = np.zeros((P, P))
    for p in range(P):
        half[p + 32 if p % 64 < 32 else p - 32, p] = -1.0 if p % 64 < 32 else 1.0
        pair[p + 1 if p % 2 == 0 else p - 1, p] = -1.0 if p % 2 == 0 else 1.0
    c["turn_half"], c["turn_pair"] = half, pair
    t = np.arange(TOK)
    freq = (np.float32(10000.0) ** (-np.arange(16, dtype=np.float32) / np.float32(16))).astype(np.float32)
    ang = np.concatenate([(t // 64).astype(np.float32)[:, None] * freq,
                          (t % 64).astype(np.float32)[:, None] * freq], 1)
    which = (i % 64) // 2
    c["cos_x"] = np.cos(ang.astype(np.float64))[:, which].T
    c["sin_x"] = np.sin(ang.astype(np.float64))[:, which].T
    inv = np.float32(10000.0) ** (-np.arange(32, dtype=np.float32) * np.float32(2.0) / np.float32(64))
    c["inv_freq"] = inv[i % 32][:, None]
    c["one_over"] = np.broadcast_to([1.0 / D, 1.0 / P], (P, 2))
    c["down4"] = np.broadcast_to(np.arange(4, 0, -1), (P, 4))
    c["down32"] = np.broadcast_to(np.arange(32, 0, -1), (P, 32))
    return np.concatenate([np.asarray(c[n], np.float32) for n, _ in CONST_FIELDS], 1)


class Steps:

    def __init__(self, known):
        self.known, self.made, self.sems, self.count = known, {}, {}, {}
        self.make = None

    def sem(self, key):
        if key not in self.sems:
            self.sems[key] = self.make(key)
        return self.sems[key]

    def did(self, key, label):
        self.count[key] = self.count.get(key, 0) + 1
        assert (key, label) not in self.made, (key, label)
        self.made[(key, label)] = self.count[key]
        return self.sem(key), 1

    def after(self, key, label):
        if self.known is None:
            return self.sem(key), 1
        return self.sem(key), self.known[(key, label)]


def build(nc, A, known=None, upto=99):
    ctx = ExitStack()
    steps = Steps(known)
    did, after = steps.did, steps.after

    def sb(name, shape, dt=F32):
        return ctx.enter_context(nc.sbuf_tensor(name, shape, dt))

    def sem(name):
        return ctx.enter_context(nc.semaphore(name))

    steps.make = sem
    PS = ctx.enter_context(nc.psum_tensor("PS", [P, 8, 512], F32))
    X = sb("X", [P, KC, 512])
    NH = sb("NH", [P, KC, 512], F32R)
    NL = sb("NL", [P, KC, 512], F32R)
    RAW = sb("RAW", [P, RAW_SLOTS, PIECE])
    SH = sb("SH", [P, SPLIT_SLOTS, PIECE], F32R)
    SL = sb("SL", [P, SPLIT_SLOTS, PIECE], F32R)
    ARENA = sb("ARENA", [P, 12304])
    PARAM = sb("PARAM", [P, N_PARAM])
    CONST = sb("CONST", [P, N_CONST])
    ONES = sb("ONES", [P, P])
    SWH = sb("SWH", [P, 480], F32R)
    SWL = sb("SWL", [P, 480], F32R)
    WORK = sb("WORK", [P, 2048])
    TA = sb("TA", [P, 2, 512])
    TB = sb("TB", [P, 2, 512])
    PB = sb("PB", [P, 2, 512])
    PT = sb("PT", [P, 2, 512])
    MOD = sb("MOD", [P, 2, 72, 2])
    SM = sb("SM", [P, 320])
    scratch = nc.dram_tensor("gate_scratch", [EXPERTS * TOK], F32, kind="Internal").ap()

    sm_at = [0]

    def small(n):
        a = sm_at[0]
        sm_at[0] += n
        assert sm_at[0] <= 318
        return SM[:, a:a + n]

    def param(name):
        a, b = PARAM_AT[name]
        return PARAM[:, a:b]

    def const(name):
        a, b = CONST_AT[name]
        return CONST[:, a:b]

    ident = const("ident")
    mask_from, mask_upto = const("mask")[:, 0:128], const("mask")[:, 256:384]
    SQ = WORK[:, 0:1024]
    TMP = WORK[:, 1024:2048].rearrange("p (a n) -> p a n", a=2)
    ROW = TA[0:1, :, :].rearrange("p a n -> p (a n)")

    def arena(at, *shape):
        n = int(np.prod(shape))
        v = ARENA[:, at:at + n]
        if len(shape) == 2:
            return v.rearrange("p (a b) -> p a b", a=shape[0])
        if len(shape) == 3:
            return v.rearrange("p (a b c) -> p a b c", a=shape[0], b=shape[1])
        return v

    FQ, FK, FV = arena(0, 4, 256), arena(1024, 4, 256), arena(2048, 2, 512)
    DQ, DK, DV = arena(3072, 4, 256), arena(4096, 4, 256), arena(5120, 2, 512)
    YD = arena(6144, 4, 256)
    COSD, SIND, ANG, ANGR = arena(7168, 256), arena(7424, 256), arena(7680, 256), arena(7936, 256)
    ANGK = arena(8192, 256)
    GA, GB, MG = arena(0, 8, 256), arena(2048, 8, 256), arena(4096, 8, 256)
    CQ, CK, CV = arena(0, 2, 256), arena(512, 2, 256), arena(1024, 2, 256)
    GBC = arena(0, EXPERTS, TOK)
    HID = arena(0, FF_CHUNKS, 512)
    QT, KT, KTOK = arena(0, 4, 512), arena(2048, 4, 512), arena(4096, 4, 512)
    VV = arena(4096, 4, 512)
    VA = arena(6144, 4, 4 * 129)
    SO, UT, HS = arena(8208, 4, 512), arena(10256, 4, 512), arena(10256, 4, 512)
    OQ, OK, OV = arena(0, 8, 256), arena(2048, 2, 512), arena(3072, 4, 256)
    C8, NC8 = TB[0:8, 0, 0:256], TB[0:8, 0, 256:512]

    NEGH, VAR, RS = small(16), small(16), small(16)
    ZERO = small(1)
    NM, RSUM, RI, ES = small(4), small(4), small(4), small(2)
    LAM, LE = small(1), small(2)
    NSINK = small(16)
    MLS = small(200)

    piece_loaded = [sem(f"piece_loaded{i}") for i in range(RAW_SLOTS)]
    high_made, low_made, piece_used = sem("high_made"), sem("low_made"), sem("piece_used")
    evacuated = sem("evacuated")
    params_in, consts_in, x_in, pos_in, mem_in, ctx_in = (
        sem(n) for n in ("params_in", "consts_in", "x_in", "pos_in", "mem_in", "ctx_in"))
    gate_out, gate_in, result_out = sem("gate_out"), sem("gate_in"), sem("result_out")
    hid_high, hid_low = sem("hid_high"), sem("hid_low")
    exp_gated, exp_high, exp_low = sem("exp_gated"), sem("exp_high"), sem("exp_low")
    act_tanh = sem("act_tanh")
    ffn_mid = sem("ffn_mid")
    ada_turned, ada_done = sem("ada_turned"), sem("ada_done")

    M = {}
    at = 0
    for name, n in (("first", QKV_PIECES), ("ada_local", ADA_LOCAL), ("second", N_FIRST - QKV_PIECES),
                    ("expert", N_EXPERT), ("up0", N_UP), ("down0", N_DOWN), ("even", EVEN_IN_PIECES),
                    ("ada_even", N_ADA - ADA_LOCAL), ("even_out", N_EVEN - EVEN_IN_PIECES),
                    ("up1", N_UP), ("down1", N_DOWN), ("up2", N_UP), ("down2", N_DOWN),
                    ("odd", N_ODD), ("up3", N_UP), ("down3", N_DOWN)):
        M[name] = at
        at += n
    N_PIECES = at
    Q = {"first": 0, "expert": N_FIRST}
    Q["up0"] = Q["expert"] + 4 * EXPERTS
    Q["even"] = Q["up0"] + N_UP
    Q["up1"] = Q["even"] + N_EVEN
    Q["up2"] = Q["up1"] + N_UP
    Q["odd"] = Q["up2"] + N_UP
    Q["up3"] = Q["odd"] + N_ODD
    n_pieces = {1: M["second"], 2: M["second"] + 12, 3: M["second"] + 16, 4: M["expert"],
                5: M["up0"] + 1, 7: M["even"] + 1, 8: M["up1"] + 1,
                9: M["up2"] + 1, 10: M["odd"] + 1, 11: M["up3"] + 1}.get(upto, N_PIECES)

    def first(i):
        return M["first"] + i if i < QKV_PIECES else M["second"] + i - QKV_PIECES

    def even(i):
        return M["even"] + i if i < EVEN_IN_PIECES else M["even_out"] + i - EVEN_IN_PIECES

    def ada(j):
        return M["ada_local"] + j if j < ADA_LOCAL else M["ada_even"] + j - ADA_LOCAL

    def unsplit_before(m):
        return sum(ada(j) < m for j in (range(N_ADA)))

    def val(c, it=None, per=4):
        return c if it is None else it * per + c

    def load_piece(sp, src, index, m, it=None, per=4, i_per=4):
        if m >= RAW_SLOTS:
            sp.wait_ge(low_made, val(m - RAW_SLOTS + 1, it, per))
        if it is None:
            s = src[index]
        else:
            s = src[bass.ds(it * i_per + index, 1)].rearrange("a p n -> p (a n)")
        sp.dma_start(RAW[:, m % RAW_SLOTS, :], s).then_inc(piece_loaded[m % RAW_SLOTS], 16)

    def make_high(act, m, it=None, per=4):
        if m >= n_pieces:
            return
        act.wait_ge(piece_loaded[m % RAW_SLOTS], val(16 * (m // RAW_SLOTS + 1), it, 16 * per // RAW_SLOTS))
        if m >= SPLIT_SLOTS:
            act.wait_ge(piece_used, val(m - SPLIT_SLOTS + 1, it, per))
        nc.scalar.activation(SH[:, m % SPLIT_SLOTS, :], RAW[:, m % RAW_SLOTS, :], ACT.Copy
                             ).then_inc(high_made, 1)

    def make_low(dve, m, it=None, per=4):
        if m >= n_pieces:
            return
        dve.wait_ge(high_made, val(m + 1 - unsplit_before(m), it, per))
        nc.vector.tensor_tensor(SL[:, m % SPLIT_SLOTS, :], RAW[:, m % RAW_SLOTS, :],
                                SH[:, m % SPLIT_SLOTS, :].bitcast(F32), ALU.subtract
                                ).then_inc(low_made, 1)

    def weights(m, a, b, c=None):
        if c is None:
            return [t[:, m % SPLIT_SLOTS, :].rearrange("p (a b) -> p a b", a=a) for t in (SH, SL)]
        return [t[:, m % SPLIT_SLOTS, :].rearrange("p (a b c) -> p a b c", a=a, b=b) for t in (SH, SL)]

    def mm3(out, w, x, start, stop, **kw):
        nc.tensor.matmul(out, w[0], x[0], start=start, stop=False, **kw)
        nc.tensor.matmul(out, w[0], x[1], start=False, stop=False, **kw)
        return nc.tensor.matmul(out, w[1], x[0], start=False, stop=stop, **kw)

    def bank(q):
        return 2 * (q % 2)

    def pe_claim(pe, m, q, it=None, per=4, qper=4):
        pe.wait_ge(low_made, val(m + 1, it, per))
        if q is not None and q >= 2:
            pe.wait_ge(evacuated, val(q - 1, it, qper))

    def pe_feature_major(pe, m, q, T, xs=None, kc=KC, cols=256, off=0, **loop):
        pe_claim(pe, m, q, **loop)
        w = weights(m, kc, cols)
        n = cols // P
        per_bank = n // 2
        for c in range(n):
            o = PS[:, bank(q) + c // per_bank, (c % per_bank) * T:(c % per_bank) * T + T]
            for k in range(kc):
                x = xs(k) if xs else [NH[:, k, off:off + T], NL[:, k, off:off + T]]
                last = mm3(o, [v[:, k, c * P:(c + 1) * P] for v in w], x, k == 0, k == kc - 1)
        last.then_inc(piece_used, 1)

    def pe_token_major(pe, m, q, T, off=0):
        pe_claim(pe, m, q)
        w = weights(m, KC, 256)
        per_bank = T // P // 2
        for b in range(T // P):
            o = PS[:, bank(q) + b // per_bank, (b % per_bank) * 256:(b % per_bank) * 256 + 256]
            for k in range(KC):
                t = slice(off + b * P, off + (b + 1) * P)
                last = mm3(o, [NH[:, k, t], NL[:, k, t]], [v[:, k, :] for v in w], k == 0, k == KC - 1)
        last.then_inc(piece_used, 1)

    def act_squares(act, n, src, T, *ready):
        for r in ready:
            act.wait_ge(*r)
        for k in range(KC):
            if k >= 2:
                act.wait_ge(*after("norm.pe", f"{n} sum {k - 2}"))
            nc.scalar.activation(SQ[:, (k % 2) * 512:(k % 2) * 512 + T], src(k), ACT.Square
                                 ).then_inc(*did("norm.act", f"{n} square {k}"))

    def pe_sums(pe, n, T):
        for k in range(KC):
            pe.wait_ge(*after("norm.act", f"{n} square {k}"))
            nc.tensor.matmul(PS[:, 4, 0:T], ONES[:, :], SQ[:, (k % 2) * 512:(k % 2) * 512 + T],
                             start=k == 0, stop=k == KC - 1).then_inc(*did("norm.pe", f"{n} sum {k}"))

    def act_row(act, n, T, last):
        act.wait_ge(*after("norm.pe", f"{n} sum {last}"))
        for i in range(0, T, 512):
            w = min(512, T - i)
            ins = nc.scalar.copy(ROW[:, i:i + w], PS[0:1, 4 + i // 512, 0:w])
        ins.then_inc(*did("norm.act", f"{n} row"))

    def pe_compact(pe, n, T, width):
        pe.wait_ge(*after("norm.act", f"{n} row"))
        for j in range(T // P):
            last = nc.tensor.matmul(PS[:, 6, j:j + 1], ROW[:, j * P:(j + 1) * P],
                                    const("one_over")[0:1, width:width + 1], start=True, stop=True)
        last.then_inc(*did("norm.pe", f"{n} compact"))

    def dve_variance(dve, n, T, eps):
        dve.wait_ge(*after("norm.pe", f"{n} compact"))
        nc.vector.tensor_scalar(VAR[:, 0:T // P], PS[:, 6, 0:T // P], eps, None, ALU.add
                                ).then_inc(*did("norm.dve", f"{n} var"))

    def pool_rstd(pool, n, T):
        pool.wait_ge(*after("norm.dve", f"{n} var"))
        nc.gpsimd.tensor_tensor(RS[:, 0:T // P], VAR[:, 0:T // P], NEGH[:, 0:T // P], ALU.pow
                                ).then_inc(*did("norm.pool", f"{n} rstd"))

    def dve_diagonal(dve, n, T):
        dve.wait_ge(*after("norm.pool", f"{n} rstd"))
        J = T // P
        nc.vector.tensor_tensor(SQ[:, 0:T].rearrange("p (j n) -> p j n", j=J),
                                ident.unsqueeze(1).to_broadcast([P, J, P]),
                                RS[:, 0:J].unsqueeze(2).to_broadcast([P, J, P]), ALU.mult
                                ).then_inc(*did("norm.dve", f"{n} diag"))

    def pe_broadcast(pe, n, T):
        pe.wait_ge(*after("norm.dve", f"{n} diag"))
        for i in range(0, T, 512):
            w = min(512, T - i)
            last = nc.tensor.matmul(PS[:, 4 + i // 512, 0:w], ONES[:, :], SQ[:, i:i + w],
                                    start=True, stop=True)
        last.then_inc(*did("norm.pe", f"{n} bcast"))

    def act_norm(act, n, T, src, *ready):
        act_squares(act, n, src, T, *ready)
        act_row(act, n, T, KC - 1)

    def pe_norm(pe, n, T):
        pe_sums(pe, n, T)
        pe_compact(pe, n, T, 0)
        pe_broadcast(pe, n, T)

    def dve_norm(dve, n, T):
        dve_variance(dve, n, T, EPS)
        dve_diagonal(dve, n, T)
        dve.wait_ge(*after("norm.pe", f"{n} bcast"))

    def dve_apply(dve, n, halves, mul, add):
        def low(k):
            dve.wait_ge(*after("norm.act", f"{n} high {k}"))
            for h in halves:
                t = slice(h * 256, h * 256 + 256)
                ins = nc.vector.scalar_tensor_tensor(NL[:, k, t], TMP[:, k % 2, t], add(k, h),
                                                     NH[:, k, t].bitcast(F32), ALU.add, ALU.subtract)
            ins.then_inc(*did("norm.dve", f"{n} low {k}"))
        for k in range(KC):
            if k >= 2:
                dve.wait_ge(*after("norm.dve", f"{n} low {k - 2}"))
            for h in halves:
                t = slice(h * 256, h * 256 + 256)
                ins = nc.vector.scalar_tensor_tensor(TMP[:, k % 2, t], X[:, k, t], mul(k, h),
                                                     PS[:, 4, t], ALU.mult, ALU.mult)
            ins.then_inc(*did("norm.dve", f"{n} scaled {k}"))
            if k >= 1:
                low(k - 1)
        low(KC - 1)

    def act_apply(act, n, halves, add):
        for k in range(KC):
            act.wait_ge(*after("norm.dve", f"{n} scaled {k}"))
            for h in halves:
                t = slice(h * 256, h * 256 + 256)
                ins = nc.scalar.activation(NH[:, k, t], TMP[:, k % 2, t], ACT.Identity, bias=add(k, h))
            ins.then_inc(*did("norm.act", f"{n} high {k}"))

    def pe_applied(pe, n):
        pe.wait_ge(*after("norm.dve", f"{n} low {KC - 1}"))

    def gain(*names):
        return lambda k, h: param(names[h])[:, k:k + 1]

    def no_shift(k, h):
        return ZERO

    def mod_col(layer, index):
        return lambda k, h: MOD[:, layer, 8 * index + k, h:h + 1]

    def fox_unit(h):
        pb, c = slice(64 * (h % 2), 64 * (h % 2) + 64), h // 2
        return dict(kind="fox", segs=[(0, 128), (128, 256)], h=h, pb=pb, c=c,
                    turns=[(0, 0), (128, 128), (256, 256)],
                    pv=[(FV[:, 0, h * 64:h * 64 + 64], 0, 128, 0, True, True),
                        (FV[:, 0, h * 64:h * 64 + 64], 128, 128, 128, True, False),
                        (FV[:, 1, h * 64:h * 64 + 64], 256, 128, 128, False, True)],
                    out=(pb, 256), dst=(NH[pb, c, 256:512], NL[pb, c, 256:512]))

    def diff_unit(h, qb):
        w = P * (qb + 1)
        return dict(kind="diff", segs=[(0, w), (w, w)], h=h, qb=qb, w=w,
                    turns=[(P * j, P * j) for j in range(qb + 1)],
                    pv=[(DV[:, j, h * P:(h + 1) * P], P * j, P, 0, j == 0, j == qb)
                        for j in range(qb + 1)],
                    out=(slice(0, P), P), dst=(YD[:, h, qb * P:(qb + 1) * P],))

    def cross_unit(h):
        pb, c = slice(64 * (h % 2), 64 * (h % 2) + 64), h // 2
        return dict(kind="cross", segs=[(0, 256), (256, 256)], h=h, pb=pb, c=c,
                    turns=[(qb * 256 + kb * P, kb * 256 + qb * P) for qb in range(2) for kb in range(2)],
                    pv=[(CV[:, kb, h * 64:h * 64 + 64], kb * 256, 256, 0, kb == 0, kb == 1)
                        for kb in range(2)],
                    out=(pb, 256), dst=(NH[pb, c, 0:256], NL[pb, c, 0:256]))

    def odd_unit(c, side, qb):
        kv = 2 * (c // 4) + side
        pb = slice(64 * side, 64 * side + 64)
        t = slice(qb * P, (qb + 1) * P)
        return dict(kind="odd", segs=[(0, 512)], h=4 * kv + c % 4, pb=pb, c=c, kc=c // 4, qb=qb,
                    turns=[(P * j, P * j) for j in range(4)],
                    pv=[(OV[:, j, kv * 64:kv * 64 + 64], P * j, P, 0, j == 0, j == 3) for j in range(4)],
                    out=(pb, P), dst=(NH[pb, c, t], NL[pb, c, t]))

    LOCAL = [fox_unit(h) for h in range(8)] + [diff_unit(h, qb) for h in range(4) for qb in range(2)]
    CROSS = [cross_unit(h) for h in range(4)]
    ODD = [odd_unit(c, side, qb) for c in range(8) for side in range(2) for qb in range(2)]

    def pe_scores(pe, u, b):
        if u["kind"] == "fox":
            for qb, (c0, w) in enumerate(u["segs"]):
                o = PS[:, b, c0:c0 + w]
                pick = ident[0:8, u["h"]:u["h"] + 1]
                q = slice(qb * P, (qb + 1) * P)
                nc.tensor.matmul(o, FQ[u["pb"], u["c"], q], FK[u["pb"], u["c"], 0:w], start=True, stop=False)
                nc.tensor.matmul(o, ident, const("mask")[:, 384 - w:384], start=False, stop=False)
                nc.tensor.matmul(o, C8[:, q], pick.to_broadcast([8, w]), start=False, stop=False)
                last = nc.tensor.matmul(o, pick.to_broadcast([8, P]), NC8[:, 0:w], start=False, stop=True)
        elif u["kind"] == "diff":
            for r, (c0, w) in enumerate(u["segs"]):
                o = PS[:, b, c0:c0 + w]
                pb = slice(64 * r, 64 * r + 64)
                nc.tensor.matmul(o, DQ[pb, u["h"], u["qb"] * P:(u["qb"] + 1) * P], DK[pb, u["h"], 0:w],
                                 start=True, stop=False)
                last = nc.tensor.matmul(o, ident, const("mask")[:, 384 - w:384], start=False, stop=True)
                if r == 0:
                    last.then_inc(*did("local.pe", f"first half {u['h']} {u['qb']}"))
                    pe.wait_ge(*after("local.pe", f"first half {u['h']} {u['qb']}"))
        elif u["kind"] == "cross":
            for qb, (c0, w) in enumerate(u["segs"]):
                last = nc.tensor.matmul(PS[:, b, c0:c0 + w], CQ[u["pb"], u["c"], qb * P:(qb + 1) * P],
                                        CK[u["pb"], u["c"], :], start=True, stop=True)
        else:
            t = slice(u["qb"] * P, (u["qb"] + 1) * P)
            m0 = 128 if u["qb"] == 0 else 0
            nc.tensor.matmul(PS[:, b, 0:256], OQ[u["pb"], u["c"], t], OK[u["pb"], u["kc"], 0:256],
                             start=True, stop=False)
            nc.tensor.matmul(PS[:, b, 0:256], ident, const("mask")[:, m0:m0 + 256], start=False, stop=True)
            last = nc.tensor.matmul(PS[:, b, 256:512], OQ[u["pb"], u["c"], t], OK[u["pb"], u["kc"], 256:512],
                                    start=True, stop=True)
        return last

    def pe_attention(pe, st, units):
        n = len(units)
        for i in range(n + 3):
            if i < n:
                if i >= 2:
                    pe.wait_ge(*after(f"{st}.act", f"exp {i - 2}"))
                pe_scores(pe, units[i], 4 + i % 2).then_inc(*did(f"{st}.pe", f"scores {i}"))
                if st == "local":
                    pe_ada(pe, local_fill(i, 0))
            if 2 <= i < n + 2:
                u = i - 2
                pe.wait_ge(*after(f"{st}.dve", f"scaled {u}"))
                if u >= 1:
                    pe.wait_ge(*after(f"{st}.act", f"turned {u - 1}"))
                for p0, t0 in units[u]["turns"]:
                    last = nc.tensor.transpose(PS[:, 6, t0:t0 + P], PB[:, u % 2, p0:p0 + P], ident)
                last.then_inc(*did(f"{st}.pe", f"turn {u}"))
            if i >= 3:
                u = i - 3
                pe.wait_ge(*after(f"{st}.act", f"turned {u}"))
                if u >= 1:
                    last_reader = "act" if units[u - 1]["kind"] == "diff" else "dve"
                    pe.wait_ge(*after(f"{st}.{last_reader}", f"out {u - 1}"))
                o = units[u]["out"][0]
                for v, p0, w, o0, start, stop in units[u]["pv"]:
                    last = nc.tensor.matmul(PS[o, 7, o0:o0 + w], v, PT[:, u % 2, p0:p0 + w],
                                            start=start, stop=stop)
                last.then_inc(*did(f"{st}.pe", f"pv {u}"))
            if i < n and st == "local":
                pe_ada(pe, local_fill(i, 1))

    def dve_attention(dve, st, units):
        n = len(units)
        for i in range(n + 4):
            if i < n:
                u, s = units[i], 2 * (i % 2)
                dve.wait_ge(*after(f"{st}.pe", f"scores {i}"))
                for j, (c0, w) in enumerate(u["segs"]):
                    ins = nc.vector.tensor_reduce(NM[:, s + j:s + j + 1], PS[:, 4 + i % 2, c0:c0 + w],
                                                  AX.X, ALU.max, negate=True)
                ins.then_inc(*did(f"{st}.dve", f"max {i}"))
                if i and st == "local":
                    dve_ada(dve, local_fill(i - 1, 1))
                if u["kind"] == "odd":
                    dve.wait_ge(*after(f"{st}.dve", f"max {i}"))
                    nc.vector.tensor_tensor(NM[:, s:s + 1], NM[:, s:s + 1], NSINK[:, u["h"]:u["h"] + 1],
                                            ALU.min).then_inc(*did(f"{st}.dve", f"shift {i}"))
            if 1 <= i <= n:
                k = i - 1
                u, s = units[k], 2 * (k % 2)
                dve.wait_ge(*after(f"{st}.act", f"exp {k}"))
                m = len(u["segs"])
                total = RSUM[:, s:s + m]
                if u["kind"] == "odd":
                    dve.wait_ge(*after(f"{st}.act", f"sink {k}"))
                    nc.vector.tensor_tensor(total, total, ES[:, k % 2:k % 2 + 1], ALU.add
                                            ).then_inc(*did(f"{st}.dve", f"total {k}"))
                    dve.wait_ge(*after(f"{st}.dve", f"total {k}"))
                nc.vector.reciprocal(RI[:, s:s + m], total).then_inc(*did(f"{st}.dve", f"recip {k}"))
                dve.wait_ge(*after(f"{st}.dve", f"recip {k}"))
                if u["kind"] == "diff":
                    w = u["w"]
                    nc.vector.tensor_scalar(PB[:, k % 2, w:2 * w], PB[:, k % 2, w:2 * w], RI[:, s + 1:s + 2],
                                            LAM, ALU.mult, ALU.mult
                                            ).then_inc(*did(f"{st}.dve", f"second {k}"))
                    dve.wait_ge(*after(f"{st}.dve", f"second {k}"))
                    ins = nc.vector.scalar_tensor_tensor(PB[:, k % 2, 0:w], PB[:, k % 2, 0:w], RI[:, s:s + 1],
                                                         PB[:, k % 2, w:2 * w], ALU.mult, ALU.subtract)
                else:
                    for j, (c0, w) in enumerate(u["segs"]):
                        ins = nc.vector.tensor_scalar(PB[:, k % 2, c0:c0 + w], PB[:, k % 2, c0:c0 + w],
                                                      RI[:, s + j:s + j + 1], None, ALU.mult)
                ins.then_inc(*did(f"{st}.dve", f"scaled {k}"))
            if i >= 4:
                k = i - 4
                u = units[k]
                o, w = u["out"]
                if u["kind"] != "diff":
                    dve.wait_ge(*after(f"{st}.act", f"out {k}"))
                if u["kind"] != "diff":
                    nc.vector.tensor_tensor(u["dst"][1], PS[o, 7, 0:w], u["dst"][0].bitcast(F32),
                                            ALU.subtract).then_inc(*did(f"{st}.dve", f"out {k}"))
            if i < n and st == "local":
                dve_ada(dve, local_fill(i, 0))

    def act_attention(act, st, units):
        n = len(units)
        for i in range(n + 4):
            if i < n:
                u, s = units[i], 2 * (i % 2)
                act.wait_ge(*after(f"{st}.dve", (f"shift {i}" if u["kind"] == "odd" else f"max {i}")))
                if i >= 2:
                    act.wait_ge(*after(f"{st}.pe", f"turn {i - 2}"))
                for j, (c0, w) in enumerate(u["segs"]):
                    ins = nc.scalar.activation(PB[:, i % 2, c0:c0 + w], PS[:, 4 + i % 2, c0:c0 + w], ACT.Exp,
                                               bias=NM[:, s + j:s + j + 1],
                                               accum_out=RSUM[:, s + j:s + j + 1])
                ins.then_inc(*did(f"{st}.act", f"exp {i}"))
                if u["kind"] == "odd":
                    nc.scalar.activation(ES[:, i % 2:i % 2 + 1], param("sink")[:, u["h"]:u["h"] + 1], ACT.Exp,
                                         bias=NM[:, s:s + 1]).then_inc(*did(f"{st}.act", f"sink {i}"))
            if 2 <= i < n + 2:
                k = i - 2
                act.wait_ge(*after(f"{st}.pe", f"turn {k}"))
                if k >= 2:
                    act.wait_ge(*after(f"{st}.pe", f"pv {k - 2}"))
                w = P * len(units[k]["turns"])
                nc.scalar.copy(PT[:, k % 2, 0:w], PS[:, 6, 0:w]).then_inc(*did(f"{st}.act", f"turned {k}"))
            if i >= 4:
                k = i - 4
                u = units[k]
                o, w = u["out"]
                act.wait_ge(*after(f"{st}.pe", f"pv {k}"))
                nc.scalar.copy(u["dst"][0], PS[o, 7, 0:w]).then_inc(*did(f"{st}.act", f"out {k}"))

    def pe_rope(pe, st, tiles, turn):
        for i, t in enumerate(tiles):
            if i >= 2:
                pe.wait_ge(*after(f"{st}.dve", f"rope sin {i - 2}"))
            o = PS[:, 4 + i % 2, :].rearrange("p (a n) -> p a n", a=2)
            nc.tensor.matmul(o, const(turn), t, start=True, stop=True
                             ).then_inc(*did(f"{st}.pe", f"rope {i}"))

    def dve_rope(dve, st, tiles, cos, sin):
        for i, t in enumerate(tiles):
            c = cos.unsqueeze(1).to_broadcast([P, 2, TOK])
            s = sin.unsqueeze(1).to_broadcast([P, 2, TOK])
            ta = TA[:, i % 2, :].rearrange("p (a n) -> p a n", a=2)
            tb = TMP[:, i % 2, :].rearrange("p (a n) -> p a n", a=2)
            o = PS[:, 4 + i % 2, :].rearrange("p (a n) -> p a n", a=2)
            nc.vector.tensor_tensor(ta, t, c, ALU.mult).then_inc(*did(f"{st}.dve", f"rope cos {i}"))
            dve.wait_ge(*after(f"{st}.pe", f"rope {i}"))
            nc.vector.tensor_tensor(tb, o, s, ALU.mult).then_inc(*did(f"{st}.dve", f"rope sin {i}"))
            dve.wait_ge(*after(f"{st}.dve", f"rope sin {i}"))
            nc.vector.tensor_tensor(t, ta, tb, ALU.add).then_inc(*did(f"{st}.dve", f"roped {i}"))

    DIFF_ROPE = [DQ[:, 0:2, :], DQ[:, 2:4, :], DK[:, 0:2, :], DK[:, 2:4, :]]
    ODD_ROPE = [OQ[:, 2 * i:2 * i + 2, :] for i in range(4)] + [OK[:, :, 0:256]]

    def ffn(n):
        return 512 if n < 3 else 256

    def pe_up(pe, n, j, it=None):
        T, m, q = ffn(n), M[f"up{n}"] + j, Q[f"up{n}"] + j
        pe_claim(pe, m, q, it)
        w = weights(m, KC, 2, P)
        for c in range(2):
            for k in range(KC):
                last = mm3(PS[:, bank(q) + c, 0:T], [v[:, k, c, :] for v in w],
                           [NH[:, k, 0:T], NL[:, k, 0:T]], k == 0, k == KC - 1)
        last.then_inc(piece_used, 1)

    def gate_tanh(act, m, q, t, T, it=None, per=4, tper=4):
        act.wait_ge(piece_used, val(m + 1, it, per))
        if t >= 2:
            act.wait_ge(ffn_mid, val(t - 1, it, tper))
        nc.scalar.activation(TA[:, q % 2, 0:T], PS[:, bank(q), 0:T], ACT.Tanh, scale=0.5
                             ).then_inc(act_tanh, 1)

    def gate_times(dve, m, q, t, T, dst, it=None, per=4, tper=4):
        dve.wait_ge(act_tanh, val(t + 1, it, tper))
        nc.vector.scalar_tensor_tensor(TB[:, q % 2, 0:T], TA[:, q % 2, 0:T], 1.0, PS[:, bank(q), 0:T],
                                       ALU.add, ALU.mult).then_inc(ffn_mid, 1)
        dve.wait_ge(ffn_mid, val(t + 1, it, tper))
        nc.vector.scalar_tensor_tensor(dst, TB[:, q % 2, 0:T], 0.5, PS[:, bank(q) + 1, 0:T],
                                       ALU.mult, ALU.mult).then_inc(evacuated, 1)

    def tanh_base(n):
        return 4 * EXPERTS + N_UP * n

    def hid_slot(p, T):
        s = 2 * (p % 2)
        return NH[:, s:s + 2, 0:T], NL[:, s:s + 2, 0:T]

    def hid_src(p, T, it):
        if it is None:
            return HID[:, 2 * p:2 * p + 2, 0:T]
        return HID[:, bass.ds(it * 8 + 2 * p, 2), 0:T]

    def act_hidden(act, n, p, it=None):
        T, m = ffn(n), M[f"down{n}"] + p
        if p < 2:
            act.wait_ge(piece_used, M[f"down{n}"])
            act.wait_ge(evacuated, Q[f"up{n}"] + N_UP)
        else:
            act.wait_ge(piece_used, val(m - 1, it))
        nc.scalar.activation(hid_slot(p, T)[0], hid_src(p, T, it), ACT.Copy).then_inc(hid_high, 1)

    def dve_hidden(dve, n, p, it=None):
        T = ffn(n)
        dve.wait_ge(hid_high, val(N_DOWN * n + p + 1, it))
        nc.vector.tensor_tensor(hid_slot(p, T)[1], hid_src(p, T, it), hid_slot(p, T)[0].bitcast(F32),
                                ALU.subtract).then_inc(hid_low, 1)

    def pe_down(pe, n, p, it=None):
        T, m = ffn(n), M[f"down{n}"] + p
        pe.wait_ge(low_made, val(m + 1, it))
        pe.wait_ge(hid_low, val(N_DOWN * n + p + 1, it))
        w = weights(m, 2, D)
        x = hid_slot(p, T)
        for k in range(2):
            for c in range(KC):
                last = mm3(PS[:, c, 0:T], [v[:, k, c * P:(c + 1) * P] for v in w],
                           [v[:, k, :] for v in x], p == 0 and k == 0, p == N_DOWN - 1 and k == 1,
                           skip_group_check=True)
        last.then_inc(piece_used, 1)

    def pe_ffn(pe, n):
        with pe.Fori(0, 5) as it:
            for j in range(4):
                pe_up(pe, n, j, it)
        for j in (20, 21):
            pe_up(pe, n, j)
        pe.wait_ge(evacuated, Q[f"up{n}"] + N_UP)
        pe_down(pe, n, 0)
        pe_down(pe, n, 1)
        with pe.Fori(0, 2) as it:
            for p in range(2, 6):
                pe_down(pe, n, p, it)
        pe_down(pe, n, 10)

    def act_ffn(act, n):
        T, m0, q0, t0 = ffn(n), M[f"up{n}"], Q[f"up{n}"], tanh_base(n)
        with act.Fori(0, 5) as it:
            for j in range(4):
                make_high(act, m0 + j + 1, it)
                gate_tanh(act, m0 + j, q0 + j, t0 + j, T, it)
        for j in (20, 21):
            make_high(act, m0 + j + 1)
            gate_tanh(act, m0 + j, q0 + j, t0 + j, T)
        d0 = M[f"down{n}"]
        act_hidden(act, n, 0)
        for p in (0, 1):
            make_high(act, d0 + p + 1)
            act_hidden(act, n, p + 1)
        with act.Fori(0, 2) as it:
            for p in range(2, 6):
                make_high(act, d0 + p + 1, it)
                act_hidden(act, n, p + 1, it)
        make_high(act, d0 + N_DOWN)

    def dve_ffn(dve, n, layer, index):
        T, m0, q0, t0 = ffn(n), M[f"up{n}"], Q[f"up{n}"], tanh_base(n)
        with dve.Fori(0, 5) as it:
            for j in range(4):
                make_low(dve, m0 + j + 1, it)
                gate_times(dve, m0 + j, q0 + j, t0 + j, T, HID[:, bass.ds(it * 4 + j, 1), 0:T]
                           .rearrange("p a n -> p (a n)"), it)
        for j in (20, 21):
            make_low(dve, m0 + j + 1)
            gate_times(dve, m0 + j, q0 + j, t0 + j, T, HID[:, j, 0:T])
        d0 = M[f"down{n}"]
        dve_hidden(dve, n, 0)
        for p in (0, 1):
            make_low(dve, d0 + p + 1)
            dve_hidden(dve, n, p + 1)
        with dve.Fori(0, 2) as it:
            for p in range(2, 6):
                make_low(dve, d0 + p + 1, it)
                dve_hidden(dve, n, p + 1, it)
        make_low(dve, d0 + N_DOWN)
        dve.wait_ge(piece_used, d0 + N_DOWN)
        for k in range(KC):
            for h in range(T // 256):
                t = slice(h * 256, h * 256 + 256)
                ins = nc.vector.scalar_tensor_tensor(X[:, k, t], PS[:, k, t], mod_col(layer, index)(k, h),
                                                     X[:, k, t], ALU.mult, ALU.add)
        ins.then_inc(*did("ffn.dve", f"residual {n}"))

    def e_m(s, j):
        return M["expert"] + 6 * s + j

    def e_q(s, j):
        return Q["expert"] + 4 * s + j

    def e_hidden(s):
        return NH[:, 4 * s:4 * s + 4, 256:512], NL[:, 4 * s:4 * s + 4, 256:512]

    def pe_experts(pe):
        with pe.Fori(0, EXPERTS // 2) as it:
            for s in range(2):
                for j in range(4):
                    m, q = e_m(s, j), e_q(s, j)
                    pe_claim(pe, m, q, it, per=12, qper=8)
                    w = weights(m, KC, 2, P)
                    for c in range(2):
                        for k in range(KC):
                            last = mm3(PS[:, bank(q) + c, 0:256], [v[:, k, c, :] for v in w],
                                       [NH[:, k, 0:256], NL[:, k, 0:256]], k == 0, k == KC - 1)
                    last.then_inc(piece_used, 1)
                for j in (4, 5):
                    m = e_m(s, j)
                    pe.wait_ge(low_made, val(m + 1, it, 12))
                    pe.wait_ge(exp_low, val(4 * s + 2 * (j - 3), it, 8))
                    w, x = weights(m, 2, D), e_hidden(s)
                    for k in range(2):
                        for c in range(KC):
                            last = mm3(PS[:, 4 + c // 2, (c % 2) * 256:(c % 2) * 256 + 256],
                                       [v[:, k, c * P:(c + 1) * P] for v in w],
                                       [v[:, 2 * (j - 4) + k, :] for v in x], False, False,
                                       skip_group_check=True)
                    last.then_inc(piece_used, 1)

    def act_experts(act):
        def high(s, j, it):
            act.wait_ge(exp_gated, val(4 * s + j + 1, it, 8))
            nc.scalar.activation(e_hidden(s)[0][:, j, :], TMP[:, j % 2, 0:256], ACT.Copy
                                 ).then_inc(exp_high, 1)
        with act.Fori(0, EXPERTS // 2) as it:
            for s in range(2):
                for j in range(4):
                    make_high(act, e_m(s, j) + 1, it, 12)
                    gate_tanh(act, e_m(s, j), e_q(s, j), 4 * s + j, 256, it, 12, 8) if s or j >= 2 else \
                        gate_tanh_first(act, s, j, it)
                    if j >= 1:
                        high(s, j - 1, it)
                make_high(act, e_m(s, 4) + 1, it, 12)
                high(s, 3, it)
                make_high(act, e_m(s, 5) + 1, it, 12)

    def gate_tanh_first(act, s, j, it):
        m, q = e_m(s, j), e_q(s, j)
        act.wait_ge(piece_used, val(m + 1, it, 12))
        nc.scalar.activation(TA[:, q % 2, 0:256], PS[:, bank(q), 0:256], ACT.Tanh, scale=0.5
                             ).then_inc(act_tanh, 1)

    def dve_experts(dve):
        def low(s, j, it):
            dve.wait_ge(exp_high, val(4 * s + j + 1, it, 8))
            nc.vector.tensor_tensor(e_hidden(s)[1][:, j, :], TMP[:, j % 2, 0:256],
                                    e_hidden(s)[0][:, j, :].bitcast(F32), ALU.subtract
                                    ).then_inc(exp_low, 1)
        with dve.Fori(0, EXPERTS // 2) as it:
            for s in range(2):
                for j in range(4):
                    make_low(dve, e_m(s, j) + 1, it, 12)
                    q = e_q(s, j)
                    gate_times(dve, e_m(s, j), q, 4 * s + j, 256, TB[:, q % 2, 256:512], it, 12, 8)
                    dve.wait_ge(evacuated, val(q + 1, it, 8))
                    nc.vector.tensor_tensor(TMP[:, j % 2, 0:256], TB[:, q % 2, 256:512],
                                            GBC[:, bass.ds(it * 2 + s, 1), :].rearrange("p a n -> p (a n)"),
                                            ALU.mult).then_inc(exp_gated, 1)
                    if j >= 1:
                        low(s, j - 1, it)
                make_low(dve, e_m(s, 4) + 1, it, 12)
                low(s, 3, it)
                make_low(dve, e_m(s, 5) + 1, it, 12)
        dve.wait_ge(piece_used, M["up0"])
        nc.vector.tensor_tensor(X[:, :, 0:256], PS[:, 4:8, :].rearrange("p b (a n) -> p (b a) n", a=2),
                                X[:, :, 0:256], ALU.add).then_inc(*did("moe.dve", "residual"))

    LG, ONG, PN = MLS[:, 0:72], MLS[:, 72:80], MLS[:, 80:88]
    RT = PB[:, 0, :]
    LM, O1, O2, W1 = RT[:, 0:64], RT[:, 64:128], RT[:, 128:192], RT[:, 192:256]
    COL = RT[:, 256:320]

    def v3(ap, b):
        return ap.rearrange("p (b n) -> p b n", b=b)

    def dve_router(dve):
        R = "moe.dve"
        step = [0]

        def then(ins, label=None):
            step[0] += 1
            name = label or f"router {step[0]}"
            ins.then_inc(*did(R, name))
            dve.wait_ge(*after(R, name))

        dve.wait_ge(*after("moe.pe", "logits"))
        lg = v3(LG, 2)
        then(nc.vector.tensor_tensor(lg, PS[:, 4, 0:72].rearrange("p (b n) -> p b n", b=2),
                                     param("b_router").unsqueeze(1).to_broadcast([P, 2, 36]), ALU.add))
        gl, el = lg[:, :, 0:4], lg[:, :, 4:36]
        gm, t4, tm = v3(COL[:, 0:2], 2), v3(COL[:, 2:10], 2), v3(COL[:, 10:12], 2)
        then(nc.vector.tensor_reduce(gm, gl, AX.X, ALU.max))
        b4 = [P, 2, 4]
        then(nc.vector.tensor_tensor(t4, gl, gm.to_broadcast(b4), ALU.is_ge))
        then(nc.vector.tensor_tensor(t4, t4, const("down4").unsqueeze(1).to_broadcast(b4), ALU.mult))
        then(nc.vector.tensor_reduce(tm, t4, AX.X, ALU.max))
        ong = v3(ONG, 2)
        then(nc.vector.tensor_tensor(ong, t4, tm.to_broadcast(b4), ALU.is_equal))
        then(nc.vector.tensor_tensor(t4, gl, gm.to_broadcast(b4), ALU.subtract), "group shifted")
        pn = v3(PN, 2)
        then(nc.vector.tensor_scalar(pn, ong, -1.0, -NEG, ALU.add, ALU.mult))
        lm = v3(LM, 2)
        for b in range(2):
            o = lm[:, b, :].rearrange("p (g e) -> p g e", g=GROUPS)
            then(nc.vector.tensor_tensor(o, el[:, b, :].rearrange("p (g e) -> p g e", g=GROUPS),
                                         pn[:, b, :].unsqueeze(2).to_broadcast([P, GROUPS, 8]), ALU.add))
        b32 = [P, 2, 32]
        v1, v2 = v3(COL[:, 12:14], 2), v3(COL[:, 14:16], 2)

        def pick(v, o):
            then(nc.vector.tensor_reduce(v, lm, AX.X, ALU.max))
            then(nc.vector.tensor_tensor(o, lm, v.to_broadcast(b32), ALU.is_ge))
            then(nc.vector.tensor_tensor(o, o, const("down32").unsqueeze(1).to_broadcast(b32), ALU.mult))
            then(nc.vector.tensor_reduce(tm, o, AX.X, ALU.max))
            then(nc.vector.tensor_tensor(o, o, tm.to_broadcast(b32), ALU.is_equal))

        o1, o2 = v3(O1, 2), v3(O2, 2)
        pick(v1, o1)
        then(nc.vector.scalar_tensor_tensor(lm, o1, 2 * NEG, lm, ALU.mult, ALU.add))
        pick(v2, o2)
        d = COL[:, 16:18]
        then(nc.vector.tensor_tensor(d, COL[:, 14:16], COL[:, 12:14], ALU.subtract), "second shifted")
        dve.wait_ge(*after("moe.act", "exps"))
        gs, w1, w2 = COL[:, 18:20], COL[:, 20:22], COL[:, 22:24]
        then(nc.vector.tensor_reduce(v3(gs, 2), v3(COL[:, 24:32], 2), AX.X, ALU.add))
        then(nc.vector.reciprocal(gs, gs))
        then(nc.vector.tensor_scalar(w1, COL[:, 32:34], 1.0, None, ALU.add))
        then(nc.vector.reciprocal(w1, w1))
        then(nc.vector.tensor_tensor(w1, w1, gs, ALU.mult))
        then(nc.vector.tensor_tensor(w2, w1, COL[:, 32:34], ALU.mult))
        then(nc.vector.tensor_tensor(o1, o1, v3(w1, 2).to_broadcast(b32), ALU.mult))
        then(nc.vector.tensor_tensor(o2, o2, v3(w2, 2).to_broadcast(b32), ALU.mult))
        then(nc.vector.tensor_tensor(v3(W1, 2), o1, o2, ALU.add), "gates")
        dve.wait_ge(*after("moe.pe", "gates turned"))
        nc.vector.tensor_copy(TA[0:32, 0, 0:256], PS[0:32, 5, 0:256]).then_inc(*did(R, "gates copied"))
        dve.wait_ge(*after(R, "gates copied"))
        nc.vector.memset(PS[:, 4:8, :], 0.0).then_inc(*did(R, "zeroed"))

    def act_router(act):
        act.wait_ge(*after("moe.dve", "second shifted"))
        nc.scalar.activation(COL[:, 24:32], COL[:, 2:10], ACT.Exp)
        nc.scalar.activation(COL[:, 32:34], COL[:, 16:18], ACT.Exp).then_inc(*did("moe.act", "exps"))
        act.wait_ge(*after("moe.dve", "gates copied"))
        act.dma_start(scratch.rearrange("(e t) -> e t", e=EXPERTS), TA[0:32, 0, 0:256]).then_inc(gate_out, 16)
        act.wait_ge(gate_out, 16)
        act.dma_start(ARENA[:, 0:EXPERTS * TOK], scratch.partition_broadcast(P)).then_inc(gate_in, 16)

    def pe_router(pe):
        for b in range(2):
            for k in range(KC):
                t = slice(b * P, (b + 1) * P)
                w = [v[:, 64:352].rearrange("p (k n) -> p k n", k=KC)[:, k, :] for v in (SWH, SWL)]
                last = mm3(PS[:, 4, b * 36:(b + 1) * 36], [NH[:, k, t], NL[:, k, t]], w, k == 0, k == KC - 1)
        last.then_inc(*did("moe.pe", "logits"))
        pe.wait_ge(*after("moe.dve", "gates"))
        for b in range(2):
            last = nc.tensor.transpose(PS[0:32, 5, b * P:(b + 1) * P], v3(W1, 2)[:, b, :], ident)
        last.then_inc(*did("moe.pe", "gates turned"))
        pe.wait_ge(*after("moe.dve", "zeroed"))

    COND = param("cond")

    def ada_place(j):
        if j < ADA_LOCAL:
            return PS[0:2, j % 2, 256:512], PS[:, 2, 256 + 4 * (j % 2):260 + 4 * (j % 2)], WORK[0:2, 1548:1804]
        return PS[0:2, 6 + j % 2, 0:256], PS[:, 6 + j % 2, 256:260], WORK[0:2, 1548:1804]

    def pe_ada_turn(pe, j):
        pe.wait_ge(low_made, ada(j) + 1)
        _, cols, row = ada_place(j)
        for c in range(2):
            last = nc.tensor.matmul(cols[:, 2 * c:2 * c + 2], row[:, c * P:(c + 1) * P], ident[0:2, 0:2],
                                    start=True, stop=True)
        last.then_inc(ada_turned, 1)

    def pe_ada(pe, js):
        for j in js:
            m = ada(j)
            pe.wait_ge(piece_loaded[m % RAW_SLOTS], 16 * (m // RAW_SLOTS + 1))
            if j >= ADA_LOCAL + 2:
                pe.wait_ge(ada_done, j - 1)
            for k in range(KC):
                last = nc.tensor.matmul(ada_place(j)[0], COND[:, 2 * k:2 * k + 2],
                                        RAW[:, m % RAW_SLOTS, 256 * k:256 * k + 256],
                                        start=k == 0, stop=k == KC - 1)
            last.then_inc(piece_used, 1)
            if j not in (0, ADA_LOCAL):
                pe_ada_turn(pe, j - 1)
            if j in (ADA_LOCAL - 1, N_ADA - 1):
                pe_ada_turn(pe, j)

    def dve_ada_columns(dve, j):
        dve.wait_ge(ada_turned, j + 1)
        l, c = divmod(2 * j, 72)
        nc.vector.tensor_tensor(MOD[:, l, c:c + 2, :], ada_place(j)[1].rearrange("p (c s) -> p c s", s=2),
                                param("ada_b")[:, 2 * j:2 * j + 2].unsqueeze(2).to_broadcast([P, 2, 2]),
                                ALU.add).then_inc(ada_done, 1)

    def dve_ada(dve, js):
        for j in js:
            if j not in (0, ADA_LOCAL):
                dve_ada_columns(dve, j - 1)
            dve.wait_ge(piece_used, ada(j) + 1)
            nc.vector.tensor_copy(ada_place(j)[2], ada_place(j)[0]).then_inc(low_made, 1)
            if j in (ADA_LOCAL - 1, N_ADA - 1):
                dve_ada_columns(dve, j)

    def dve_mod_ready(dve, done, scales, gates):
        dve.wait_ge(ada_done, done)
        for l, i in scales:
            v = MOD[:, l, 8 * i:8 * i + 8, :]
            nc.vector.tensor_scalar(v, v, 1.0, None, ALU.add)
        for l, i in gates:
            v = MOD[:, l, 8 * i:8 * i + 8, :]
            ins = nc.vector.tensor_scalar(v, v, 0.5, None, ALU.mult)
        ins.then_inc(*did("ada.dve", f"mod ready {done}"))

    LOCAL_FILL, EVEN_FILL = (1, 1), (2, 1, 1, 1)

    def fill(start, counts, turn, place):
        a = start + sum(counts) * turn + sum(counts[:place])
        return range(a, a + counts[place])

    def local_fill(i, place):
        return fill(0, LOCAL_FILL, i, place)

    def even_fill(s, place):
        return fill(ADA_LOCAL, EVEN_FILL, s, place)

    E_Q = Q["even"]
    CSTATE = WORK[:, 0:516].rearrange("p (h n) -> p h n", h=4)
    WV = WORK[:, 516:1032].rearrange("p (h n) -> p h n", h=4)
    NUM = WORK[:, 1032:1548].rearrange("p (h n) -> p h n", h=4)
    VAH = VA.rearrange("p b (h n) -> p b h n", h=4)
    LGT, GZ = MLS[:, 0:64], MLS[:, 64:128]
    CUM, TOT, REST = PT[:, 1, 0:32], PT[:, 1, 32:64], PT[:, 1, 64:96]
    AVAL, AMAX, WGT = PT[:, 1, 96:128], PT[:, 1, 128:160], PT[:, 1, 160:192]
    MSTATE = PT[:, 1, 192:196]
    MU, SML, SMX = PT[:, 1, 196:200], PT[:, 1, 200:208], PT[:, 1, 208:216]
    MNEW, DA, DAX = PT[:, 1, 216:220], PT[:, 1, 220:228], PT[:, 1, 228:236]
    DEN, RDEN = PT[:, 1, 236:240], PT[:, 1, 240:244]
    AM1 = PT[:, 1, 244:245]
    GABS, GSUM = PT[:, 1, 256:320], PT[:, 1, 320:324]
    ORDER = [(2, 3, 0, 1), (3, 2, 1, 0)]
    STEPS = [(d, i) for d in range(2) for i in range(4)]

    def gates_of(ap, k):
        return ap.rearrange("p (b d k h) -> p b d k h", b=4, d=2, k=2)[:, :, :, k, :]

    def bdh(ap):
        return ap.rearrange("p (b d h) -> p b d h", b=4, d=2)

    def heads(ap):
        return ap.rearrange("p (h n) -> p h n", h=4)

    def pe_even(pe):
        for j in range(12):
            if j in (4, 5, 10, 11):
                pe_token_major(pe, even(j), E_Q + j, 512)
            else:
                pe_feature_major(pe, even(j), E_Q + j, 512)
        for b in range(4):
            for k in range(KC):
                t = slice(b * P, (b + 1) * P)
                w = [v[:, 352 + 16 * k:352 + 16 * k + 16] for v in (SWH, SWL)]
                last = mm3(PS[:, 4, 16 * b:16 * b + 16], [NH[:, k, t], NL[:, k, t]], w, k == 0, k == KC - 1)
        last.then_inc(*did("even.pe", "gates"))
        pe.wait_ge(*after("even.dve", "gated v"))
        ws = param("sgu_ws").rearrange("p (g n) -> p g n", g=4)
        for g in range(4):
            if g >= 2:
                pe.wait_ge(*after("even.dve", f"mixed {g - 2}"))
            for b in range(4):
                last = nc.tensor.matmul(PS[:, 6 + g % 2, b * P:(b + 1) * P], VV[:, b, g * P:(g + 1) * P],
                                        ws[:, g, :], start=True, stop=True)
            last.then_inc(*did("even.pe", f"mixed {g}"))
        pe.wait_ge(*after("even.dve", "k 3"))
        for b in range(4):
            if b >= 2:
                pe.wait_ge(*after("even.act", f"keys turned {b - 2}"))
            for h in range(4):
                last = nc.tensor.transpose(PS[:, b % 2, h * P:(h + 1) * P], KT[:, h, b * P:(b + 1) * P], ident)
            last.then_inc(*did("even.pe", f"keys {b}"))
        pe.wait_ge(*after("even.dve", "log sigmoid"))
        for i, tri in enumerate((const("upto"), const("from"), ONES[:, :])):
            last = nc.tensor.matmul(PS[:, 5, 64 * i:64 * i + 64], tri, LGT, start=True, stop=True)
        last.then_inc(*did("even.pe", "cumulated"))
        pe.wait_ge(*after("even.dve", "a"))
        nc.tensor.transpose(PS[0:32, 6, 0:128], AVAL, ident).then_inc(*did("even.pe", "a turned"))
        pe.wait_ge(*after("even.dve", "a max diagonal"))
        nc.tensor.matmul(PS[:, 7, 0:32], ONES[0:32, :], TA[0:32, 0, 0:32], start=True, stop=True
                         ).then_inc(*did("even.pe", "a max"))
        for s, (d, i) in enumerate(STEPS):
            b = ORDER[d][i]
            t = slice(b * P, (b + 1) * P)
            pe.wait_ge(*after("even.dve", f"diagonal {s}"))
            if s:
                pe.wait_ge(*after("even.dve", f"state {s - 1}"))
            mask = (mask_upto, mask_from)[d]
            nc.tensor.matmul(PS[:, 0, :], ONES[:, :], TB[:, 0, :], start=True, stop=False)
            nc.tensor.matmul(heads(PS[:, 0, :]), ident, mask.unsqueeze(1).to_broadcast([P, 4, P]),
                             start=False, stop=True).then_inc(*did("even.pe", f"decay {s}"))
            for h in range(4):
                last = nc.tensor.matmul(PS[:, 1, h * P:(h + 1) * P], QT[:, h, t], KT[:, h, t],
                                        start=True, stop=True)
            last.then_inc(*did("even.pe", f"qk {s}"))
            for h in range(4):
                last = nc.tensor.matmul(PS[:, 4 + h // 2, 256 * (h % 2):256 * (h % 2) + 129],
                                        QT[:, h, t], CSTATE[:, h, :], start=True, stop=True)
            last.then_inc(*did("even.pe", f"inter {s}"))
            pe_ada(pe, even_fill(s, 0))
            pe.wait_ge(*after("even.dve", f"s {s}"))
            for h in range(4):
                last = nc.tensor.transpose(PS[:, 0, h * P:(h + 1) * P], PB[:, 0, h * P:(h + 1) * P], ident)
            last.then_inc(*did("even.pe", f"s turned {s}"))
            pe_ada(pe, even_fill(s, 1))
            pe.wait_ge(*after("even.act", f"s turned {s}"))
            for h in range(4):
                last = nc.tensor.matmul(PS[:, 2 + h // 2, 256 * (h % 2):256 * (h % 2) + 129],
                                        PT[:, 0, h * P:(h + 1) * P], VAH[:, b, h, :], start=True, stop=True)
            last.then_inc(*did("even.pe", f"intra {s}"))
            if i < 3:
                pe.wait_ge(*after("even.dve", f"weighted v {s}"))
                for h in range(4):
                    last = nc.tensor.matmul(PS[:, h // 2, 256 * (h % 2):256 * (h % 2) + 129],
                                            KTOK[:, b, h * P:(h + 1) * P], WV[:, h, :], start=True, stop=True)
                last.then_inc(*did("even.pe", f"local state {s}"))
            for place in (2, 3):
                pe_ada(pe, even_fill(s, place))
        for b in range(4):
            pe.wait_ge(*after("even.dve", f"head normed {b}"))
            if b >= 2:
                pe.wait_ge(*after("even.dve", f"head out {b - 2}"))
            for h in range(4):
                last = nc.tensor.transpose(PS[:, 6 + b % 2, h * P:(h + 1) * P],
                                           HS[:, b, h * P:(h + 1) * P], ident)
            last.then_inc(*did("even.pe", f"head turned {b}"))
        pe.wait_ge(*after("even.dve", "head low 3"))
        for j in range(12, 16):
            pe_feature_major(pe, even(j), E_Q + j, 512)

    def act_even(act):
        def tanh_of(src, dst, label, scale):
            nc.scalar.activation(dst, src, ACT.Tanh, scale=scale).then_inc(*did("even.act", label))
        for j in range(12):
            m, q = even(j), E_Q + j
            if j < 11:
                make_high(act, m + 1)
            src = PS[:, bank(q):bank(q) + 2, :]
            if j < 4:
                for c in range(2):
                    act.wait_ge(*after("even.dve", f"conv {2 * j + c}"))
                    tanh_of(TB[:, c, :], TA[:, c, :], f"qk tanh {2 * j + c}", 0.5)
            elif j in (6, 7):
                act.wait_ge(piece_used, m + 1)
                tanh_of(src, SO[:, 2 * (j - 6):2 * (j - 6) + 2, :], f"o {j}", 0.5)
            elif j >= 8:
                act.wait_ge(piece_used, m + 1)
                act.wait_ge(evacuated, q)
                nc.scalar.activation(TA[:, :, :], src, ACT.Square).then_inc(*did("even.act", f"uv square {j}"))
                act.wait_ge(*after("even.dve", f"uv inner {j}"))
                tanh_of(TB[:, :, :], TA[:, :, :], f"uv tanh {j}", GELU_C)
        act.wait_ge(*after("even.dve", "gates"))
        nc.scalar.activation(GABS, GZ, ACT.Abs).then_inc(*did("even.act", "gates abs"))
        act.wait_ge(*after("even.act", "gates abs"))
        nc.scalar.activation(GABS, GABS, ACT.Exp, scale=-1.0).then_inc(*did("even.act", "gates exp"))
        act.wait_ge(*after("even.act", "gates exp"))
        nc.scalar.activation(LGT, GABS, ACT.Ln, bias=1.0).then_inc(*did("even.act", "gates ln"))
        act.wait_ge(*after("even.dve", "uv 11"))
        for b in range(4):
            ins = nc.scalar.activation((TB, TA)[b // 2][:, b % 2, :], VV[:, b, :], ACT.Square,
                                       accum_out=GSUM[:, b:b + 1])
        ins.then_inc(*did("even.act", "gated squares"))
        for g in range(4):
            act.wait_ge(*after("even.dve", f"gated {g}"))
            nc.scalar.activation(NH[:, 4 + g, :], TB[:, g % 2, :], ACT.Copy
                                 ).then_inc(*did("even.act", f"gated high {g}"))
        for b in range(4):
            act.wait_ge(*after("even.pe", f"keys {b}"))
            nc.scalar.copy(KTOK[:, b, :], PS[:, b % 2, :]).then_inc(*did("even.act", f"keys turned {b}"))
        act.wait_ge(*after("even.dve", "a shifted"))
        nc.scalar.activation(WGT, AVAL, ACT.Exp).then_inc(*did("even.act", "a exp"))
        for s, (d, i) in enumerate(STEPS):
            act.wait_ge(*after("even.dve", f"decay shifted {s}"))
            nc.scalar.activation(TA[:, 1, :], TA[:, 0, :], ACT.Exp).then_inc(*did("even.act", f"decay {s}"))
            act.wait_ge(*after("even.dve", f"small {s}"))
            nc.scalar.activation(SMX, SML, ACT.Exp).then_inc(*did("even.act", f"small {s}"))
            act.wait_ge(*after("even.pe", f"s turned {s}"))
            nc.scalar.copy(PT[:, 0, :], PS[:, 0, :]).then_inc(*did("even.act", f"s turned {s}"))
            act.wait_ge(*after("even.dve", f"numerator {s}"))
            nc.scalar.activation(DEN.unsqueeze(2), NUM[:, :, 128:129], ACT.Abs
                                 ).then_inc(*did("even.act", f"denominator {s}"))
            if i < 3:
                act.wait_ge(*after("even.dve", f"new m {s}"))
                nc.scalar.activation(DAX, DA, ACT.Exp).then_inc(*did("even.act", f"new m {s}"))
        make_high(act, even(12))
        for b in range(4):
            act.wait_ge(*after("even.dve", f"h {len(STEPS) - 1}"))
            if b >= 2:
                act.wait_ge(*after("even.dve", f"head sum {b - 2}"))
            nc.scalar.activation(TA[:, b % 2, :], HS[:, b, :], ACT.Square
                                 ).then_inc(*did("even.act", f"head square {b}"))
        for b in range(4):
            t = slice(b * P, (b + 1) * P)
            act.wait_ge(*after("even.dve", f"head out {b}"))
            nc.scalar.activation(NH[:, 0:4, t], heads(TB[:, b % 2, :]), ACT.Copy
                                 ).then_inc(*did("even.act", f"head high {b}"))
        for j in range(12, 16):
            make_high(act, even(j) + 1)

    def dve_even(dve):
        E = "even.dve"
        conv = param("conv_w").rearrange("p (c j) -> p c j", c=KC)
        for j in range(4):
            m, q = even(j), E_Q + j
            make_low(dve, m + 1)
            dve.wait_ge(piece_used, m + 1)
            for c in range(2):
                ch = 2 * j + c
                src, dst = PS[:, bank(q) + c, :], TB[:, c, :]
                nc.vector.tensor_scalar(dst, src, conv[:, ch, 1:2], None, ALU.mult
                                        ).then_inc(*did(E, f"conv mid {ch}"))
                dve.wait_ge(*after(E, f"conv mid {ch}"))
                s2, d2 = src.rearrange("p (s t) -> p s t", s=2), dst.rearrange("p (s t) -> p s t", s=2)
                nc.vector.scalar_tensor_tensor(d2[:, :, 1:TOK], s2[:, :, 0:TOK - 1], conv[:, ch, 0:1],
                                               d2[:, :, 1:TOK], ALU.mult, ALU.add
                                               ).then_inc(*did(E, f"conv before {ch}"))
                dve.wait_ge(*after(E, f"conv before {ch}"))
                nc.vector.scalar_tensor_tensor(d2[:, :, 0:TOK - 1], s2[:, :, 1:TOK], conv[:, ch, 2:3],
                                               d2[:, :, 0:TOK - 1], ALU.mult, ALU.add
                                               ).then_inc(*did(E, f"conv {ch}"))
            for c in range(2):
                ch = 2 * j + c
                dst = (QT, KT)[ch // 4][:, ch % 4, :]
                dve.wait_ge(*after("even.act", f"qk tanh {ch}"))
                nc.vector.scalar_tensor_tensor(dst, TA[:, c, :], 1.0, TB[:, c, :], ALU.add, ALU.mult
                                               ).then_inc(*did(E, f"qk twice {ch}"))
                dve.wait_ge(*after(E, f"qk twice {ch}"))
                ins = nc.vector.tensor_scalar(dst, dst, 0.5, float(P) ** -0.5 if ch >= 4 else 1.0,
                                              ALU.mult, ALU.mult)
                if c == 0:
                    ins.then_inc(*did(E, f"half {ch}"))
                else:
                    ins.then_inc(evacuated, 1)
        dve.wait_ge(evacuated, E_Q + 4)
        nc.vector.memset(VAH[:, :, :, 128:129], 1.0).then_inc(*did(E, "k 3"))
        for j in (4, 5):
            m, q = even(j), E_Q + j
            make_low(dve, m + 1)
            dve.wait_ge(piece_used, m + 1)
            h = 2 * (j - 4)
            for i in range(2):
                src = PS[:, bank(q) + i, :].rearrange("p (b h n) -> p b h n", b=2, h=2)
                ins = nc.vector.tensor_copy(VAH[:, 2 * i:2 * i + 2, h:h + 2, 0:128], src)
            ins.then_inc(evacuated, 1)
        for j in (6, 7):
            make_low(dve, even(j) + 1)
            dve.wait_ge(*after("even.act", f"o {j}"))
            v = SO[:, 2 * (j - 6):2 * (j - 6) + 2, :]
            nc.vector.tensor_scalar(v, v, 0.5, 0.5, ALU.mult, ALU.add).then_inc(evacuated, 1)
        for j in (8, 9, 10, 11):
            m, q = even(j), E_Q + j
            if j < 11:
                make_low(dve, m + 1)
            src = PS[:, bank(q):bank(q) + 2, :]
            dve.wait_ge(*after("even.act", f"uv square {j}"))
            nc.vector.tensor_scalar(TB[:, :, :], TA[:, :, :], 0.044715, 1.0, ALU.mult, ALU.add
                                    ).then_inc(*did(E, f"uv square {j}"))
            dve.wait_ge(*after(E, f"uv square {j}"))
            nc.vector.tensor_tensor(TB[:, :, :], TB[:, :, :], src, ALU.mult
                                    ).then_inc(*did(E, f"uv inner {j}"))
            dve.wait_ge(*after("even.act", f"uv tanh {j}"))
            nc.vector.scalar_tensor_tensor(TB[:, :, :], TA[:, :, :], 1.0, src, ALU.add, ALU.mult
                                           ).then_inc(evacuated, 1)
            dve.wait_ge(evacuated, q + 1)
            if j < 10:
                c = 2 * (j - 8)
                nc.vector.tensor_scalar(UT[:, c:c + 2, :], TB[:, :, :], 0.5, None, ALU.mult
                                        ).then_inc(*did(E, f"uv {j}"))
            else:
                c = 256 * (j - 10)
                nc.vector.tensor_scalar(VV[:, :, c:c + 256],
                                        TB[:, :, :].rearrange("p a (b n) -> p (a b) n", b=2), 0.5, None,
                                        ALU.mult).then_inc(*did(E, f"uv {j}"))
            dve.wait_ge(*after(E, f"uv {j}"))
        dve.wait_ge(*after("even.pe", "gates"))
        nc.vector.tensor_tensor(GZ.rearrange("p (b n) -> p b n", b=4),
                                PS[:, 4, 0:64].rearrange("p (b n) -> p b n", b=4),
                                param("gate_b").unsqueeze(1).to_broadcast([P, 4, 16]), ALU.add
                                ).then_inc(*did(E, "gates"))
        dve.wait_ge(*after("even.act", "gates ln"))
        nc.vector.scalar_tensor_tensor(LGT, GZ, 0.0, LGT, ALU.min, ALU.subtract
                                       ).then_inc(*did(E, "log sigmoid"))
        dve.wait_ge(*after("even.act", "gated squares"))
        nc.vector.tensor_scalar(VAR[:, 0:4], GSUM, 1.0 / 512, EPS, ALU.mult, ALU.add
                                ).then_inc(*did(E, "gating var"))
        dve.wait_ge(*after("even.pool", "gating rstd"))
        for b in range(4):
            ins = nc.vector.scalar_tensor_tensor(VV[:, b, :], VV[:, b, :], RS[:, b:b + 1],
                                                 param("sgu_norm"), ALU.mult, ALU.mult)
        ins.then_inc(*did(E, "gated v"))
        sgb = heads(param("sgu_b"))
        for g in range(4):
            dve.wait_ge(*after("even.pe", f"mixed {g}"))
            tb = TB[:, g % 2, :]
            if g >= 2:
                dve.wait_ge(*after("even.act", f"gated high {g - 2}"))
            nc.vector.tensor_tensor(heads(tb), heads(PS[:, 6 + g % 2, :]),
                                    sgb[:, g, :].unsqueeze(1).to_broadcast([P, 4, P]), ALU.add
                                    ).then_inc(*did(E, f"mixed {g}"))
            dve.wait_ge(*after(E, f"mixed {g}"))
            nc.vector.tensor_tensor(tb, tb, UT[:, g, :], ALU.mult).then_inc(*did(E, f"gated {g}"))
            dve.wait_ge(*after("even.act", f"gated high {g}"))
            nc.vector.tensor_tensor(NL[:, 4 + g, :], tb, NH[:, 4 + g, :].bitcast(F32), ALU.subtract
                                    ).then_inc(*did(E, f"gated low {g}"))
        dve.wait_ge(*after("even.pe", "cumulated"))
        for d in range(2):
            nc.vector.tensor_copy(bdh(CUM)[:, :, d, :], gates_of(PS[:, 5, 64 * d:64 * d + 64], 1)[:, :, d, :])
        nc.vector.tensor_copy(bdh(TOT), gates_of(PS[:, 5, 128:192], 1)).then_inc(*did(E, "cumulated"))
        dve.wait_ge(*after(E, "cumulated"))
        nc.vector.tensor_tensor(bdh(REST), gates_of(GZ, 0), bdh(CUM), ALU.subtract).then_inc(*did(E, "rest"))
        dve.wait_ge(*after(E, "rest"))
        nc.vector.tensor_tensor(AVAL, TOT, REST, ALU.add).then_inc(*did(E, "a"))
        dve.wait_ge(*after("even.pe", "a turned"))
        nc.vector.tensor_reduce(AM1[0:32, :], PS[0:32, 6, 0:128], AX.X, ALU.max).then_inc(*did(E, "a max"))
        dve.wait_ge(*after(E, "a max"))
        nc.vector.tensor_scalar(TA[0:32, 0, 0:32], ident[0:32, 0:32], AM1[0:32, :], None, ALU.mult
                                ).then_inc(*did(E, "a max diagonal"))
        dve.wait_ge(*after("even.pe", "a max"))
        nc.vector.tensor_copy(AMAX, PS[:, 7, 0:32]).then_inc(*did(E, "a max everywhere"))
        dve.wait_ge(*after(E, "a max everywhere"))
        nc.vector.tensor_tensor(AVAL, AVAL, AMAX, ALU.subtract).then_inc(*did(E, "a shifted"))
        dve.wait_ge(*after("even.act", "a exp"))
        for s, (d, i) in enumerate(STEPS):
            b = ORDER[d][i]
            if i == 0:
                nc.vector.memset(MSTATE, 0.0)
                nc.vector.memset(WORK[:, 0:516], 0.0).then_inc(*did(E, f"start {s}"))
                dve.wait_ge(*after(E, f"start {s}"))
            cum, tot, rest, amax, wgt = (bdh(t)[:, b, d, :] for t in (CUM, TOT, REST, AMAX, WGT))
            if s:
                dve.wait_ge(*after("even.pe", f"decay {s - 1}"))
            nc.vector.tensor_tensor(heads(TB[:, 0, :]), ident.unsqueeze(1).to_broadcast([P, 4, P]),
                                    rest.unsqueeze(2).to_broadcast([P, 4, P]), ALU.mult
                                    ).then_inc(*did(E, f"diagonal {s}"))
            nc.vector.tensor_tensor(WV[:, :, :], VAH[:, b, :, :], wgt.unsqueeze(2).to_broadcast([P, 4, 129]),
                                    ALU.mult).then_inc(*did(E, f"weighted v {s}"))
            dve.wait_ge(*after("even.pe", f"decay {s}"))
            nc.vector.tensor_reduce(MU.unsqueeze(2), heads(PS[:, 0, :]), AX.X, ALU.max
                                    ).then_inc(*did(E, f"row max {s}"))
            dve.wait_ge(*after(E, f"row max {s}"))
            nc.vector.tensor_tensor(MU, MU, MSTATE, ALU.max).then_inc(*did(E, f"mu {s}"))
            dve.wait_ge(*after(E, f"mu {s}"))
            nc.vector.tensor_tensor(heads(TA[:, 0, :]), heads(PS[:, 0, :]),
                                    MU.unsqueeze(2).to_broadcast([P, 4, P]), ALU.subtract
                                    ).then_inc(*did(E, f"decay shifted {s}"))
            nc.vector.tensor_tensor(SML[:, 0:4], MSTATE, MU, ALU.subtract)
            nc.vector.scalar_tensor_tensor(SML[:, 4:8], cum, -1.0, MU, ALU.mult, ALU.subtract
                                           ).then_inc(*did(E, f"small {s}"))
            dve.wait_ge(*after("even.act", f"decay {s}"))
            dve.wait_ge(*after("even.pe", f"qk {s}"))
            nc.vector.tensor_tensor(PB[:, 0, :], PS[:, 1, :], TA[:, 1, :], ALU.mult
                                    ).then_inc(*did(E, f"s {s}"))
            dve_ada(dve, even_fill(s, 0))
            dve.wait_ge(*after("even.act", f"small {s}"))
            dve.wait_ge(*after("even.pe", f"inter {s}"))
            for k in range(2):
                hh = slice(2 * k, 2 * k + 2)
                ins = nc.vector.tensor_tensor(NUM[:, hh, :],
                                              PS[:, 4 + k, :].rearrange("p (h n) -> p h n", h=2)[:, :, 0:129],
                                              SMX[:, hh].unsqueeze(2).to_broadcast([P, 2, 129]), ALU.mult)
            ins.then_inc(*did(E, f"inter {s}"))
            dve_ada(dve, even_fill(s, 1))
            dve.wait_ge(*after(E, f"inter {s}"))
            dve.wait_ge(*after("even.pe", f"intra {s}"))
            for k in range(2):
                hh = slice(2 * k, 2 * k + 2)
                ins = nc.vector.tensor_tensor(NUM[:, hh, :],
                                              PS[:, 2 + k, :].rearrange("p (h n) -> p h n", h=2)[:, :, 0:129],
                                              NUM[:, hh, :], ALU.add)
            ins.then_inc(*did(E, f"numerator {s}"))
            dve.wait_ge(*after("even.act", f"denominator {s}"))
            nc.vector.tensor_tensor(DEN, DEN, SMX[:, 4:8], ALU.max).then_inc(*did(E, f"bounded {s}"))
            dve.wait_ge(*after(E, f"bounded {s}"))
            nc.vector.reciprocal(RDEN, DEN).then_inc(*did(E, f"recip {s}"))
            dve.wait_ge(*after(E, f"recip {s}"))
            rd = RDEN.unsqueeze(2).to_broadcast([P, 4, P])
            if d == 0:
                nc.vector.tensor_tensor(heads(HS[:, b, :]), NUM[:, :, 0:128], rd, ALU.mult
                                        ).then_inc(*did(E, f"h {s}"))
            else:
                nc.vector.tensor_tensor(heads(TB[:, 1, :]), NUM[:, :, 0:128], rd, ALU.mult
                                        ).then_inc(*did(E, f"h back {s}"))
                dve.wait_ge(*after(E, f"h back {s}"))
                nc.vector.tensor_tensor(HS[:, b, :], HS[:, b, :], TB[:, 1, :], ALU.add
                                        ).then_inc(*did(E, f"h {s}"))
            dve_ada(dve, even_fill(s, 2))
            if i < 3:
                nc.vector.tensor_tensor(DA[:, 0:4], MSTATE, tot, ALU.add).then_inc(*did(E, f"g plus m {s}"))
                dve.wait_ge(*after(E, f"g plus m {s}"))
                nc.vector.tensor_tensor(MNEW, DA[:, 0:4], amax, ALU.max).then_inc(*did(E, f"m new {s}"))
                dve.wait_ge(*after(E, f"m new {s}"))
                nc.vector.tensor_tensor(DA[:, 0:4], DA[:, 0:4], MNEW, ALU.subtract)
                nc.vector.tensor_tensor(DA[:, 4:8], amax, MNEW, ALU.subtract).then_inc(*did(E, f"new m {s}"))
                nc.vector.tensor_copy(MSTATE, MNEW)
                dve.wait_ge(*after("even.act", f"new m {s}"))
                dve.wait_ge(*after("even.pe", f"local state {s}"))
                nc.vector.tensor_tensor(CSTATE, CSTATE, DAX[:, 0:4].unsqueeze(2).to_broadcast([P, 4, 129]),
                                        ALU.mult)
                for k in range(2):
                    hh = slice(2 * k, 2 * k + 2)
                    ins = nc.vector.tensor_tensor(
                        WV[:, hh, :], PS[:, k, :].rearrange("p (h n) -> p h n", h=2)[:, :, 0:129],
                        DAX[:, 4 + 2 * k:6 + 2 * k].unsqueeze(2).to_broadcast([P, 2, 129]), ALU.mult)
                ins.then_inc(*did(E, f"new part {s}"))
                dve.wait_ge(*after(E, f"new part {s}"))
                nc.vector.tensor_tensor(CSTATE, CSTATE, WV, ALU.add).then_inc(*did(E, f"state {s}"))
                dve.wait_ge(*after(E, f"state {s}"))
            else:
                dve.wait_ge(*after(E, f"h {s}"))
                nc.vector.memset(MNEW, 0.0).then_inc(*did(E, f"state {s}"))
            dve_ada(dve, even_fill(s, 3))
        dve_mod_ready(dve, N_ADA, [(1, 1), (1, 4), (1, 7)], [(0, 8), (1, 2), (1, 8)])
        make_low(dve, even(12))
        for b in range(4):
            dve.wait_ge(*after("even.act", f"head square {b}"))
            nc.vector.tensor_reduce(GABS[:, 4 * b:4 * b + 4].unsqueeze(2), heads(TA[:, b % 2, :]), AX.X,
                                    ALU.add).then_inc(*did(E, f"head sum {b}"))
        dve.wait_ge(*after(E, "head sum 3"))
        nc.vector.tensor_scalar(VAR, GABS[:, 0:16], 1.0 / P, EPS, ALU.mult, ALU.add
                                ).then_inc(*did(E, "head var"))
        dve.wait_ge(*after("even.pool", "head rstd"))
        for b in range(4):
            nc.vector.tensor_tensor(heads(HS[:, b, :]), heads(HS[:, b, :]),
                                    RS[:, 4 * b:4 * b + 4].unsqueeze(2).to_broadcast([P, 4, P]), ALU.mult
                                    ).then_inc(*did(E, f"head normed {b}"))
        for b in range(4):
            t = slice(b * P, (b + 1) * P)
            dve.wait_ge(*after("even.pe", f"head turned {b}"))
            if b >= 2:
                dve.wait_ge(*after("even.act", f"head high {b - 2}"))
            for h in range(4):
                ins = nc.vector.scalar_tensor_tensor(TB[:, b % 2, h * P:(h + 1) * P],
                                                     PS[:, 6 + b % 2, h * P:(h + 1) * P],
                                                     param("mnorm")[:, h:h + 1], SO[:, h, t],
                                                     ALU.mult, ALU.mult)
            ins.then_inc(*did(E, f"head out {b}"))
            dve.wait_ge(*after("even.act", f"head high {b}"))
            nc.vector.tensor_tensor(NL[:, 0:4, t], heads(TB[:, b % 2, :]), NH[:, 0:4, t].bitcast(F32),
                                    ALU.subtract).then_inc(*did(E, f"head low {b}"))
        for j in range(12, 16):
            m, q = even(j), E_Q + j
            make_low(dve, m + 1)
            dve.wait_ge(piece_used, m + 1)
            for c in range(2):
                k = 2 * (j - 12) + c
                for h in range(2):
                    t = slice(h * 256, h * 256 + 256)
                    ins = nc.vector.scalar_tensor_tensor(X[:, k, t], PS[:, bank(q) + c, t],
                                                         mod_col(0, 5)(k, h), X[:, k, t], ALU.mult, ALU.add)
            ins.then_inc(evacuated, 1)
        dve.wait_ge(evacuated, E_Q + N_EVEN)

    def finish(dve):
        dve.drain()
        if upto < 7:
            dve.wait_ge(ctx_in, 16)
        nc.vector.tensor_copy(SM[:, 319:320], ZERO).then_inc(*did("end.dve", "result"))

    def evac_copy(dve, m, q, dst, scale=None, T=256):
        dve.wait_ge(piece_used, m + 1)
        src = PS[:, bank(q):bank(q) + 2, 0:T]
        if scale is None:
            nc.vector.tensor_copy(dst, src).then_inc(evacuated, 1)
        else:
            nc.vector.tensor_scalar(dst, src, scale, None, ALU.mult).then_inc(evacuated, 1)

    block = ctx.enter_context(nc.Block())

    @block.sync
    def _(sp):
        def group(src, i0, m0, n):
            n = min(n, n_pieces - m0)
            if n <= 0:
                return
            j = 0
            while m0 + j < RAW_SLOTS and j < n:
                load_piece(sp, src, i0 + j, m0 + j)
                j += 1
            if (n - j) // 4 > 1:
                with sp.Fori(0, (n - j) // 4) as it:
                    for r in range(4):
                        load_piece(sp, src, i0 + j + r, m0 + j + r, it)
                j += 4 * ((n - j) // 4)
            while j < n:
                load_piece(sp, src, i0 + j, m0 + j)
                j += 1
        group(A["w_first"], 0, M["first"], QKV_PIECES)
        group(A["w_ada"], 0, M["ada_local"], ADA_LOCAL)
        group(A["w_first"], QKV_PIECES, M["second"], N_FIRST - QKV_PIECES)
        group(A["w_expert"], 0, M["expert"], N_EXPERT)
        group(A["w_up"], 0, M["up0"], N_UP)
        group(A["w_down"], 0, M["down0"], N_DOWN)
        group(A["w_even"], 0, M["even"], EVEN_IN_PIECES)
        group(A["w_ada"], ADA_LOCAL, M["ada_even"], N_ADA - ADA_LOCAL)
        group(A["w_even"], EVEN_IN_PIECES, M["even_out"], N_EVEN - EVEN_IN_PIECES)
        for n in (1, 2):
            group(A["w_up"], N_UP * n, M[f"up{n}"], N_UP)
            group(A["w_down"], N_DOWN * n, M[f"down{n}"], N_DOWN)
        group(A["w_odd"], 0, M["odd"], N_ODD)
        group(A["w_up"], N_UP * 3, M["up3"], N_UP)
        group(A["w_down"], N_DOWN * 3, M["down3"], N_DOWN)
        sp.wait_ge(*after("end.dve", "result"))
        sp.dma_start(A["out"], X[:, :, 0:256]).then_inc(result_out, 16)
        sp.wait_ge(result_out, 16)

    @block.scalar
    def _(act):
        act.dma_start(X[:, :, 0:256], A["xT"]).then_inc(x_in, 16)
        act.dma_start(PARAM[:, :], A["params"]).then_inc(params_in, 16)
        act.dma_start(CONST[:, :], A["consts"]).then_inc(consts_in, 16)
        act.dma_start(ANGK.bitcast(I32), A["positions"]).then_inc(pos_in, 16)
        act.dma_start(X[:, :, 256:512], A["memT"]).then_inc(mem_in, 16)
        act.wait_ge(params_in, 16)
        a0 = PARAM_AT["w_fgate"][0]
        nc.scalar.activation(SWH[:, :], PARAM[:, a0:a0 + 480], ACT.Copy).then_inc(*did("set.act", "small high"))
        act.wait_ge(*after("set.dve", "sine angle"))
        nc.scalar.activation(SIND, ANG, ACT.Sin).then_inc(*did("set.act", "sine"))
        act.wait_ge(*after("set.dve", "cosine angle"))
        nc.scalar.activation(COSD, ANGR, ACT.Sin).then_inc(*did("set.act", "cosine"))
        act.wait_ge(*after("set.dve", "lambda sums"))
        nc.scalar.activation(LE, LE, ACT.Exp).then_inc(*did("set.act", "lambda exps"))
        nc.scalar.activation(TB[:, 1, 0:16], COND, ACT.Tanh, scale=0.5).then_inc(*did("set.act", "condition tanh"))
        make_high(act, 0)
        act_norm(act, 0, 256, lambda k: X[:, k, 0:256], (x_in, 16))
        act_apply(act, 0, (0,), no_shift)
        for m in range(QKV_PIECES - 1):
            make_high(act, m + 1)
        FZ, FA, FL = PB[:, 0, 0:16], PB[:, 0, 16:32], PB[:, 0, 32:48]
        act.wait_ge(*after("local.dve", "forget logits"))
        nc.scalar.activation(FA, FZ, ACT.Abs).then_inc(*did("local.act", "forget abs"))
        act.wait_ge(*after("local.act", "forget abs"))
        nc.scalar.activation(FA, FA, ACT.Exp, scale=-1.0).then_inc(*did("local.act", "forget exp"))
        act.wait_ge(*after("local.act", "forget exp"))
        nc.scalar.activation(FL, FA, ACT.Ln, bias=1.0).then_inc(*did("local.act", "forget ln"))
        act_attention(act, "local", LOCAL)
        act.wait_ge(*after("local.pe", f"pv {len(LOCAL) - 1}"))
        act.wait_ge(*after("local.act", f"out {len(LOCAL) - 1}"))
        nc.scalar.activation(SQ[:, 0:1024], YD.rearrange("p a n -> p (a n)"), ACT.Square
                             ).then_inc(*did("norm.act", "sub square"))
        act_row(act, "sub", 1024, 0)
        for k in range(4):
            act.wait_ge(*after("local.dve", f"sub scaled {k}"))
            nc.scalar.activation(NH[:, 4 + k, 256:512], TMP[:, k % 2, 0:256], ACT.Copy
                                 ).then_inc(*did("local.act", f"sub high {k}"))
        if upto < 2:
            return
        make_high(act, first(12))
        for m in range(12, 20):
            make_high(act, first(m + 1))
            act.wait_ge(piece_used, first(m) + 1)
            G = (GA, GB)[(m - 12) // 4]
            c = 2 * ((m - 12) % 4)
            nc.scalar.activation(G[:, c:c + 2, :], PS[:, bank(m):bank(m) + 2, 0:256], ACT.Tanh, scale=0.5
                                 ).then_inc(*did("gates.act", f"tanh {m}"))
        for i, m in enumerate(range(20, 24)):
            make_high(act, first(m + 1))
            if i % 2:
                act.wait_ge(*after("gates.dve", f"merged {i // 2}"))
                c = 4 * (i // 2)
                nc.scalar.activation(NH[:, c:c + 4, 0:256], MG[:, c:c + 4, :], ACT.Copy
                                     ).then_inc(*did("gates.act", f"merged high {i // 2}"))
        for m in range(24, 28):
            make_high(act, first(m + 1))
        if upto < 4:
            return
        act_norm(act, 1, 512, lambda k: X[:, k, :], (evacuated, 28), (mem_in, 16))
        act_apply(act, 1, (0, 1), no_shift)
        for m in range(28, 31):
            make_high(act, first(m + 1))
        act_attention(act, "cross", CROSS)
        make_high(act, M["expert"])
        act.wait_ge(*after("norm.act", "1 high 7"))
        act.wait_ge(*after("norm.dve", "1 scaled 7"))
        act.dma_start(X[:, :, 256:512], A["ctxT"]).then_inc(ctx_in, 16)
        if upto < 5:
            return
        act_norm(act, 2, 256, lambda k: X[:, k, 0:256], (evacuated, 32))
        act_apply(act, 2, (0,), no_shift)
        act_router(act)
        act_experts(act)
        if upto < 6:
            return
        act_norm(act, 3, 256, lambda k: X[:, k, 0:256], after("moe.dve", "residual"))
        if upto < 7:
            return
        act_norm(act, 4, 512, lambda k: X[:, k, :], after("moe.dve", "final of first"),
                 (ctx_in, 16))
        act_apply(act, 4, (0, 1), mod_col(0, 0))
        act_ffn(act, 0)
        if upto < 8:
            return
        act_norm(act, 5, 512, lambda k: X[:, k, :], after("ffn.dve", "residual 0"))
        act_apply(act, 5, (0, 1), mod_col(0, 3))
        act_even(act)
        if upto < 9:
            return
        act_norm(act, 6, 512, lambda k: X[:, k, :], (evacuated, Q["even"] + N_EVEN))
        act_apply(act, 6, (0, 1), mod_col(0, 6))
        act_ffn(act, 1)
        if upto < 10:
            return
        act_norm(act, 7, 512, lambda k: X[:, k, :], after("ffn.dve", "residual 1"))
        act_apply(act, 7, (0, 1), mod_col(1, 0))
        act_ffn(act, 2)
        if upto < 11:
            return
        act_norm(act, 8, 512, lambda k: X[:, k, :], after("ffn.dve", "residual 2"))
        act_apply(act, 8, (0, 1), mod_col(1, 3))
        for m in range(M["odd"], M["odd"] + 6):
            make_high(act, m + 1)
        act_attention(act, "odd", ODD)
        for m in range(M["odd"] + 6, M["odd"] + 10):
            make_high(act, m + 1)
        if upto < 12:
            return
        act_norm(act, 9, 256, lambda k: X[:, k, 0:256], (evacuated, Q["odd"] + N_ODD))
        act_apply(act, 9, (0,), mod_col(1, 6))
        act_ffn(act, 3)
        act_norm(act, 10, 256, lambda k: X[:, k, 0:256], after("ffn.dve", "residual 3"))

    @block.gpsimd
    def _(pool):
        nc.gpsimd.memset(NEGH, -0.5).then_inc(*did("set.pool", "exponent"))
        pool.wait_ge(*after("set.pool", "exponent"))
        pool_rstd(pool, 0, 256)
        pool_rstd(pool, "sub", 1024)
        if upto < 4:
            return
        pool_rstd(pool, 1, 512)
        if upto < 5:
            return
        pool_rstd(pool, 2, 256)
        if upto < 6:
            return
        pool_rstd(pool, 3, 256)
        if upto < 7:
            return
        pool_rstd(pool, 4, 512)
        if upto < 8:
            return
        pool_rstd(pool, 5, 512)
        pool.wait_ge(*after("even.dve", "gating var"))
        nc.gpsimd.tensor_tensor(RS[:, 0:4], VAR[:, 0:4], NEGH[:, 0:4], ALU.pow
                                ).then_inc(*did("even.pool", "gating rstd"))
        pool.wait_ge(*after("even.dve", "head var"))
        nc.gpsimd.tensor_tensor(RS, VAR, NEGH, ALU.pow).then_inc(*did("even.pool", "head rstd"))
        if upto < 9:
            return
        pool_rstd(pool, 6, 512)
        if upto < 10:
            return
        pool_rstd(pool, 7, 512)
        if upto < 11:
            return
        pool_rstd(pool, 8, 512)
        if upto < 12:
            return
        pool_rstd(pool, 9, 256)
        pool_rstd(pool, 10, 256)

    @block.tensor
    def _(pe):
        pe.wait_ge(consts_in, 16)
        pe.wait_ge(*after("set.dve", "ones"))
        pe_norm(pe, 0, 256)
        pe_applied(pe, 0)
        for m in range(12):
            (pe_token_major if m in (4, 5, 10, 11) else pe_feature_major)(pe, m, m, 256)
        pe.wait_ge(*after("set.dve", "small low"))
        for b in range(2):
            for k in range(KC):
                t = slice(b * P, (b + 1) * P)
                w = [v[:, 8 * k:8 * k + 8] for v in (SWH, SWL)]
                last = mm3(PS[:, 6, 8 * b:8 * b + 8], [NH[:, k, t], NL[:, k, t]], w, k == 0, k == KC - 1)
        last.then_inc(*did("local.pe", "forget logits"))
        pe.wait_ge(evacuated, 12)
        pe_rope(pe, "local", DIFF_ROPE, "turn_half")
        pe.wait_ge(*after("local.dve", "log forget"))
        LF = PB[:, 0, 48:64]
        nc.tensor.matmul(PS[0:8, 6, 0:128], LF[:, 0:8], const("upto"), start=True, stop=True)
        nc.tensor.matmul(PS[0:8, 6, 128:256], LF[:, 8:16], const("upto"), start=True, stop=False)
        nc.tensor.matmul(PS[0:8, 6, 128:256], LF[:, 0:8], ONES[:, :], start=False, stop=True
                         ).then_inc(*did("local.pe", "cumulated"))
        pe.wait_ge(*after("local.dve", "cumulated"))
        pe.wait_ge(*after("local.dve", "roped 3"))
        pe.wait_ge(*after("set.dve", "condition"))
        pe_attention(pe, "local", LOCAL)
        pe.wait_ge(*after("norm.act", "sub square"))
        for i in range(2):
            last = nc.tensor.matmul(PS[:, 4 + i, :], ONES[:, :], SQ[:, 512 * i:512 * i + 512],
                                    start=True, stop=True)
        last.then_inc(*did("norm.pe", "sub sum 0"))
        pe_compact(pe, "sub", 1024, 1)
        pe_broadcast(pe, "sub", 1024)
        if upto < 2:
            return
        for m in range(12, 20):
            pe_feature_major(pe, first(m), m, 256)
        pe.wait_ge(*after("local.dve", "sub low 3"))
        for i, m in enumerate(range(20, 24)):
            o = 4 * (i % 2)
            pe_feature_major(pe, first(m), m, 256, kc=4, cols=512,
                             xs=lambda k, o=o: [NH[:, o + k, 256:512], NL[:, o + k, 256:512]])
        pe.wait_ge(*after("gates.dve", "merged low 1"))
        for m in range(24, 28):
            pe_feature_major(pe, first(m), m, 256)
        if upto < 4:
            return
        pe_norm(pe, 1, 512)
        pe_applied(pe, 1)
        pe_feature_major(pe, first(28), 28, 256)
        pe_feature_major(pe, first(29), 29, 256, off=256)
        pe_token_major(pe, first(30), 30, 256, off=256)
        pe.wait_ge(evacuated, 31)
        pe_attention(pe, "cross", CROSS)
        pe.wait_ge(*after("cross.dve", f"out {len(CROSS) - 1}"))
        pe_claim(pe, first(31), 31)
        pe.wait_ge(evacuated, 31)
        w = weights(first(31), 2, D)
        for c in range(KC):
            for k in range(2):
                last = mm3(PS[:, c // 2, (c % 2) * 256:(c % 2) * 256 + 256],
                           [v[:, k, c * P:(c + 1) * P] for v in w],
                           [NH[:, k, 0:256], NL[:, k, 0:256]], k == 0, k == 1)
        last.then_inc(piece_used, 1)
        if upto < 5:
            return
        pe_norm(pe, 2, 256)
        pe_applied(pe, 2)
        pe_router(pe)
        pe.wait_ge(evacuated, 32)
        pe_experts(pe)
        if upto < 6:
            return
        pe_norm(pe, 3, 256)
        if upto < 7:
            return
        pe_norm(pe, 4, 512)
        pe_applied(pe, 4)
        pe_ffn(pe, 0)
        if upto < 8:
            return
        pe_norm(pe, 5, 512)
        pe_applied(pe, 5)
        pe_even(pe)
        if upto < 9:
            return
        pe_norm(pe, 6, 512)
        pe_applied(pe, 6)
        pe_ffn(pe, 1)
        if upto < 10:
            return
        pe_norm(pe, 7, 512)
        pe_applied(pe, 7)
        pe_ffn(pe, 2)
        if upto < 11:
            return
        pe_norm(pe, 8, 512)
        pe_applied(pe, 8)
        m0, q0 = M["odd"], Q["odd"]
        for j in range(4):
            pe_feature_major(pe, m0 + j, q0 + j, 256)
        pe_feature_major(pe, m0 + 4, q0 + 4, 512)
        pe_token_major(pe, m0 + 5, q0 + 5, 512)
        pe.wait_ge(evacuated, q0 + 6)
        pe_rope(pe, "odd", ODD_ROPE, "turn_pair")
        pe.wait_ge(*after("odd.dve", "roped 4"))
        pe_attention(pe, "odd", ODD)
        pe.wait_ge(*after("odd.dve", f"out {len(ODD) - 1}"))
        for j in range(6, 10):
            pe_feature_major(pe, m0 + j, q0 + j, 256)
        if upto < 12:
            return
        pe_norm(pe, 9, 256)
        pe_applied(pe, 9)
        pe_ffn(pe, 3)
        pe_norm(pe, 10, 256)

    @block.vector
    def _(dve):
        nc.vector.memset(ONES[:, :], 1.0)
        nc.vector.memset(ZERO, 0.0).then_inc(*did("set.dve", "ones"))
        dve.wait_ge(*after("set.dve", "ones"))
        dve.wait_ge(params_in, 16)
        a0 = PARAM_AT["w_fgate"][0]
        dve.wait_ge(*after("set.act", "small high"))
        nc.vector.tensor_tensor(SWL[:, :], PARAM[:, a0:a0 + 480], SWH[:, :].bitcast(F32), ALU.subtract
                                ).then_inc(*did("set.dve", "small low"))
        nc.vector.tensor_scalar(NSINK, param("sink"), -1.0, None, ALU.mult)
        k_step = [0]

        def chain(ins, label=None):
            k_step[0] += 1
            name = label or f"set {k_step[0]}"
            ins.then_inc(*did("set.dve", name))
            dve.wait_ge(*after("set.dve", name))
        two_pi = 2.0 * np.pi
        p1 = 6.28125
        p2 = float(np.float32(np.round((two_pi - p1) * 2 ** 20) / 2 ** 20))
        p3 = float(two_pi - p1 - p2)
        dve.wait_ge(pos_in, 16)
        dve.wait_ge(consts_in, 16)
        chain(nc.vector.tensor_copy(ANG, ANGK.bitcast(I32)))
        chain(nc.vector.tensor_scalar(ANG, ANG, const("inv_freq"), None, ALU.mult))
        for which in ("cosine", "sine"):
            turns = ANGK
            chain(nc.vector.tensor_scalar(turns, ANG, float(1.0 / two_pi), 0.25 if which == "cosine" else 0.0,
                                          ALU.mult, ALU.add))
            chain(nc.vector.tensor_scalar(turns, turns, MAGIC, None, ALU.add))
            chain(nc.vector.tensor_scalar(turns, turns, MAGIC, None, ALU.subtract))
            dst = ANGR if which == "cosine" else ANG
            chain(nc.vector.scalar_tensor_tensor(dst, turns, -p1, ANG, ALU.mult, ALU.add))
            chain(nc.vector.scalar_tensor_tensor(dst, turns, -p2, dst, ALU.mult, ALU.add))
            chain(nc.vector.scalar_tensor_tensor(dst, turns, -p3, dst, ALU.mult, ALU.add))
            if which == "cosine":
                chain(nc.vector.tensor_scalar(dst, dst, float(np.pi / 2), None, ALU.add))
            chain(nc.vector.tensor_scalar(dst, dst, 3.1415925, -3.1415925, ALU.min, ALU.max),
                  f"{which} angle")
        prod = TB[:, 0, 0:128]
        chain(nc.vector.tensor_tensor(prod, param("lam_a"), param("lam_b"), ALU.mult))
        chain(nc.vector.tensor_reduce(LE, prod.rearrange("p (a n) -> p a n", a=2), AX.X, ALU.add),
              "lambda sums")
        dve.wait_ge(*after("set.act", "lambda exps"))
        chain(nc.vector.scalar_tensor_tensor(LAM, LE[:, 0:1], LAMBDA_INIT, LE[:, 1:2], ALU.add, ALU.subtract))
        dve.wait_ge(*after("set.act", "cosine"))
        dve.wait_ge(*after("set.act", "condition tanh"))
        chain(nc.vector.scalar_tensor_tensor(COND, TB[:, 1, 0:16], 1.0, COND, ALU.add, ALU.mult))
        chain(nc.vector.tensor_scalar(COND, COND, 0.5, None, ALU.mult), "condition")

        make_low(dve, 0)
        dve_norm(dve, 0, 256)
        dve_apply(dve, 0, (0,), gain("g_mix"), no_shift)
        dests = [(FQ, .125), (FK, None), (FV, None), (DQ, .125), (DK, None), (DV, None)]
        for m in range(QKV_PIECES):
            if m + 1 < QKV_PIECES:
                make_low(dve, m + 1)
            dst, scale = dests[m // 2]
            if m in (4, 5, 10, 11):
                evac_copy(dve, m, m, dst[:, :, 256 * (m % 2):256 * (m % 2) + 256])
            else:
                evac_copy(dve, m, m, dst[:, 2 * (m % 2):2 * (m % 2) + 2, :], scale)
        FZ, FL, LF = PB[:, 0, 0:16], PB[:, 0, 32:48], PB[:, 0, 48:64]
        dve.wait_ge(*after("local.pe", "forget logits"))
        nc.vector.tensor_tensor(v3(FZ, 2), v3(PS[:, 6, 0:16], 2),
                                param("b_fgate").unsqueeze(1).to_broadcast([P, 2, 8]), ALU.add
                                ).then_inc(*did("local.dve", "forget logits"))
        dve.wait_ge(evacuated, 12)
        dve_rope(dve, "local", DIFF_ROPE, COSD, SIND)
        dve.wait_ge(*after("local.act", "forget ln"))
        nc.vector.scalar_tensor_tensor(LF, FZ, 0.0, FL, ALU.min, ALU.subtract
                                       ).then_inc(*did("local.dve", "log forget"))
        dve.wait_ge(*after("local.pe", "cumulated"))
        nc.vector.tensor_copy(C8, PS[0:8, 6, 0:256])
        nc.vector.tensor_scalar(NC8, PS[0:8, 6, 0:256], -1.0, None, ALU.mult
                                ).then_inc(*did("local.dve", "cumulated"))
        dve_attention(dve, "local", LOCAL)
        dve_ada(dve, local_fill(len(LOCAL) - 1, 1))
        dve_mod_ready(dve, ADA_LOCAL, [(0, 1), (0, 4), (0, 7)], [(0, 2)])
        dve_variance(dve, "sub", 1024, 1e-5)
        dve_diagonal(dve, "sub", 1024)
        dve.wait_ge(*after("norm.pe", "sub bcast"))
        for k in range(4):
            src = PS[:, 4 + k // 2, (k % 2) * 256:(k % 2) * 256 + 256]
            if k >= 2:
                dve.wait_ge(*after("local.act", f"sub high {k - 2}"))
            nc.vector.scalar_tensor_tensor(TMP[:, k % 2, 256:512], YD[:, k, :], param("g_sub"), src,
                                           ALU.mult, ALU.mult).then_inc(*did("local.dve", f"sub norm {k}"))
            dve.wait_ge(*after("local.dve", f"sub norm {k}"))
            nc.vector.tensor_scalar(TMP[:, k % 2, 0:256], TMP[:, k % 2, 256:512], 1.0 - LAMBDA_INIT, None,
                                    ALU.mult).then_inc(*did("local.dve", f"sub scaled {k}"))
            dve.wait_ge(*after("local.act", f"sub high {k}"))
            nc.vector.tensor_tensor(NL[:, 4 + k, 256:512], TMP[:, k % 2, 0:256],
                                    NH[:, 4 + k, 256:512].bitcast(F32), ALU.subtract
                                    ).then_inc(*did("local.dve", f"sub low {k}"))
        if upto < 2:
            nc.vector.tensor_copy(X[:, 0:4, 0:256], YD).then_inc(*did("end.dve", "result"))
            return
        make_low(dve, first(12))
        for m in range(12, 20):
            make_low(dve, first(m + 1))
            dve.wait_ge(*after("gates.act", f"tanh {m}"))
            G = (GA, GB)[(m - 12) // 4]
            c = 2 * ((m - 12) % 4)
            nc.vector.tensor_scalar(G[:, c:c + 2, :], G[:, c:c + 2, :], 0.5, 0.5, ALU.mult, ALU.add
                                    ).then_inc(evacuated, 1)
        dve.wait_ge(evacuated, 20)
        for i, m in enumerate(range(20, 24)):
            make_low(dve, first(m + 1))
            dve.wait_ge(piece_used, first(m) + 1)
            c = 4 * (i // 2)
            G = (GA, GB)[i % 2]
            src = PS[:, bank(m):bank(m) + 2, :].rearrange("p b (a n) -> p (b a) n", a=2)
            if i % 2 == 0:
                nc.vector.tensor_tensor(MG[:, c:c + 4, :], src, G[:, c:c + 4, :], ALU.mult
                                        ).then_inc(evacuated, 1)
            else:
                nc.vector.tensor_tensor(G[:, c:c + 4, :], src, G[:, c:c + 4, :], ALU.mult
                                        ).then_inc(evacuated, 1)
                dve.wait_ge(evacuated, m + 1)
                nc.vector.tensor_tensor(MG[:, c:c + 4, :], MG[:, c:c + 4, :], G[:, c:c + 4, :], ALU.add
                                        ).then_inc(*did("gates.dve", f"merged {i // 2}"))
                dve.wait_ge(*after("gates.act", f"merged high {i // 2}"))
                nc.vector.tensor_tensor(NL[:, c:c + 4, 0:256], MG[:, c:c + 4, :],
                                        NH[:, c:c + 4, 0:256].bitcast(F32), ALU.subtract
                                        ).then_inc(*did("gates.dve", f"merged low {i // 2}"))

        def residual(m0, q0, n, scale=None):
            for i in range(n):
                make_low(dve, m0 + i + 1)
                dve.wait_ge(piece_used, m0 + i + 1)
                x = X[:, 2 * i:2 * i + 2, 0:256]
                if scale is None:
                    ins = nc.vector.tensor_tensor(x, PS[:, bank(q0 + i):bank(q0 + i) + 2, 0:256], x, ALU.add)
                    ins.then_inc(evacuated, 1)
                else:
                    for c in range(2):
                        k = 2 * i + c
                        ins = nc.vector.scalar_tensor_tensor(X[:, k, 0:256], PS[:, bank(q0 + i) + c, 0:256],
                                                             scale(k, 0), X[:, k, 0:256], ALU.mult, ALU.add)
                    ins.then_inc(evacuated, 1)
            dve.wait_ge(evacuated, q0 + n)

        residual(first(24), 24, 4)
        if upto < 4:
            finish(dve)
            return
        dve_norm(dve, 1, 512)
        dve_apply(dve, 1, (0, 1), gain("g_cross", "g_mem"), no_shift)
        make_low(dve, first(29))
        evac_copy(dve, first(28), 28, CQ, .125)
        make_low(dve, first(30))
        evac_copy(dve, first(29), 29, CK)
        make_low(dve, first(31))
        evac_copy(dve, first(30), 30, CV)
        dve_attention(dve, "cross", CROSS)
        make_low(dve, M["expert"])
        dve.wait_ge(piece_used, M["expert"])
        nc.vector.tensor_tensor(X[:, :, 0:256], PS[:, 0:4, :].rearrange("p b (a n) -> p (b a) n", a=2),
                                X[:, :, 0:256], ALU.add).then_inc(evacuated, 1)
        dve.wait_ge(evacuated, 32)
        if upto < 5:
            finish(dve)
            return
        dve.wait_ge(evacuated, 32)
        dve_norm(dve, 2, 256)
        dve_apply(dve, 2, (0,), gain("g_ffn"), no_shift)
        dve_router(dve)
        dve.wait_ge(gate_in, 16)
        dve_experts(dve)
        if upto < 6:
            finish(dve)
            return
        dve.wait_ge(*after("moe.dve", "residual"))
        dve_norm(dve, 3, 256)
        for k in range(KC):
            ins = nc.vector.scalar_tensor_tensor(X[:, k, 0:256], X[:, k, 0:256], param("g_final")[:, k:k + 1],
                                                 PS[:, 4, 0:256], ALU.mult, ALU.mult)
        ins.then_inc(*did("moe.dve", "final of first"))
        if upto < 7:
            finish(dve)
            return
        dve.wait_ge(*after("ada.dve", f"mod ready {ADA_LOCAL}"))
        dve_norm(dve, 4, 512)
        dve_apply(dve, 4, (0, 1), mod_col(0, 1), mod_col(0, 0))
        dve_ffn(dve, 0, 0, 2)
        if upto < 8:
            finish(dve)
            return
        dve.wait_ge(*after("ffn.dve", "residual 0"))
        dve_norm(dve, 5, 512)
        dve_apply(dve, 5, (0, 1), mod_col(0, 4), mod_col(0, 3))
        dve_even(dve)
        if upto < 9:
            finish(dve)
            return
        dve_norm(dve, 6, 512)
        dve_apply(dve, 6, (0, 1), mod_col(0, 7), mod_col(0, 6))
        dve_ffn(dve, 1, 0, 8)
        if upto < 10:
            finish(dve)
            return
        dve.wait_ge(*after("ffn.dve", "residual 1"))
        dve.wait_ge(*after("ada.dve", f"mod ready {N_ADA}"))
        dve_norm(dve, 7, 512)
        dve_apply(dve, 7, (0, 1), mod_col(1, 1), mod_col(1, 0))
        dve_ffn(dve, 2, 1, 2)
        if upto < 11:
            finish(dve)
            return
        dve.wait_ge(*after("ffn.dve", "residual 2"))
        dve_norm(dve, 8, 512)
        dve_apply(dve, 8, (0, 1), mod_col(1, 4), mod_col(1, 3))
        m0, q0 = M["odd"], Q["odd"]
        for j in range(4):
            make_low(dve, m0 + j + 1)
            evac_copy(dve, m0 + j, q0 + j, OQ[:, 2 * j:2 * j + 2, :], .125)
        make_low(dve, m0 + 5)
        evac_copy(dve, m0 + 4, q0 + 4, OK, T=512)
        make_low(dve, m0 + 6)
        evac_copy(dve, m0 + 5, q0 + 5, OV.rearrange("p (b a) n -> p b (a n)", b=2), T=512)
        dve.wait_ge(evacuated, q0 + 6)
        dve_rope(dve, "odd", ODD_ROPE, const("cos_x"), const("sin_x"))
        dve_attention(dve, "odd", ODD)
        residual(m0 + 6, q0 + 6, 4, mod_col(1, 5))
        if upto < 12:
            finish(dve)
            return
        dve_norm(dve, 9, 256)
        dve_apply(dve, 9, (0,), mod_col(1, 7), mod_col(1, 6))
        dve_ffn(dve, 3, 1, 8)
        dve.wait_ge(*after("ffn.dve", "residual 3"))
        dve_norm(dve, 10, 256)
        for k in range(KC):
            ins = nc.vector.scalar_tensor_tensor(X[:, k, 0:256], X[:, k, 0:256],
                                                 param("final_norm")[:, k:k + 1], PS[:, 4, 0:256],
                                                 ALU.mult, ALU.mult)
        ins.then_inc(*did("end.dve", "result"))

    ctx.close()
    return steps.made


def pieces(w):
    k, n = w.shape
    return w.reshape(k // P, P, n // 256, 256).transpose(2, 1, 0, 3).reshape(n // 256, P, PIECE)


def feature_major(t):
    return np.ascontiguousarray(t.T.reshape(KC, P, -1).transpose(1, 0, 2))


def chunk_columns(v):
    return v.reshape(-1, P).T


def lay_out(I):
    w_in = I["w_in"][0]
    first = [pieces(w_in[:, 0:1536]), pieces(w_in[:, 1544:3080]), pieces(w_in[:, 3080:5128])]
    br = [I[n][0].reshape(4, P, 2, 512).transpose(2, 1, 0, 3).reshape(2, 1, P, PIECE)
          for n in ("w_branch_a", "w_branch_b")]
    first += [br[0][0], br[1][0], br[0][1], br[1][1], pieces(I["w_out"][0]), pieces(I["w_cq"][0]),
              pieces(I["w_ckv"][0]), I["w_co"][0].reshape(2, P, D).transpose(1, 0, 2).reshape(1, P, PIECE)]
    gate = I["w_exp_gate"][0].reshape(EXPERTS, KC, P, 4, 1, P)
    up = I["w_exp_up"][0].reshape(EXPERTS, KC, P, 4, 1, P)
    gu = np.concatenate([gate, up], 4).transpose(0, 3, 2, 1, 4, 5).reshape(EXPERTS, 4, P, PIECE)
    down = I["w_exp_down"][0].reshape(EXPERTS, 2, 2, P, D).transpose(0, 1, 3, 2, 4).reshape(EXPERTS, 2, P, PIECE)
    expert = np.concatenate([gu, down], 1).reshape(EXPERTS * 6, P, PIECE)
    ada = np.concatenate([pieces(w) for w in I["ada_w_2"]], 0)
    fi = I["ffn_w_in_2"].reshape(4, KC, P, 2, FF_CHUNKS, P).transpose(0, 4, 2, 1, 3, 5)
    fi = fi.reshape(4 * FF_CHUNKS, P, PIECE)
    fo = I["ffn_w_out_2"].reshape(4, N_DOWN, 2, P, D).transpose(0, 1, 3, 2, 4).reshape(4 * N_DOWN, P, PIECE)
    we = I["even_w_in_2"][0]
    even = np.concatenate([pieces(we[:, 0:2048]), pieces(we[:, 2064:3088]), pieces(I["even_w_out_2"][0])], 0)
    wq = I["odd_w_qkv_2"][0]
    order = [h for c in range(8) for h in (8 * (c // 4) + c % 4, 8 * (c // 4) + 4 + c % 4)]
    q = wq[:, 0:D].reshape(D, 16, HD)[:, order].reshape(D, D)
    wo = I["odd_w_out_2"][0].reshape(16, HD, D)[order].reshape(D, D)
    odd = np.concatenate([pieces(q), pieces(wq[:, D:D + 512]), pieces(wo)], 0)

    def rows(v):
        return np.broadcast_to(v.reshape(1, -1), (P, v.size))

    def k_major(w):
        return w.reshape(KC, P, -1).transpose(1, 0, 2).reshape(P, -1)

    f = {}
    for n in ("g_mix", "g_cross", "g_mem", "g_ffn"):
        f[n] = chunk_columns(I[n][0])
    f["g_final"], f["final_norm"] = chunk_columns(I["g_final"]), chunk_columns(I["final_norm_2"])
    f["g_sub"] = I["g_diff_sub"][0].reshape(P, 1)
    f["lam_a"] = rows(np.concatenate([I["lambda_q1"][0], I["lambda_q2"][0]]))
    f["lam_b"] = rows(np.concatenate([I["lambda_k1"][0], I["lambda_k2"][0]]))
    f["w_fgate"] = k_major(w_in[:, 1536:1544])
    f["w_router"] = k_major(np.concatenate([I["w_group"][0], I["w_expert"][0]], 1))
    f["w_gates"] = k_major(we[:, 2048:2064])
    f["b_fgate"] = rows(I["b_fgate"][0])
    f["b_router"] = rows(np.concatenate([I["b_group"][0], I["b_expert"][0]]))
    f["ada_b"] = np.concatenate([chunk_columns(v) for v in I["ada_b_2"]], 1)
    f["conv_w"] = I["mlstm_conv_2"][0].reshape(3, KC, P).transpose(2, 1, 0).reshape(P, 24)
    f["gate_b"] = rows(I["mlstm_gate_b_2"][0])
    f["mnorm"] = I["mlstm_norm_2"][0].T
    f["sgu_norm"] = rows(I["sgu_norm_2"][0])
    f["sgu_ws"] = I["sgu_ws_2"][0].transpose(2, 0, 1).reshape(P, 512)
    f["sgu_b"] = rows(I["sgu_b_2"][0])
    f["sink"] = rows(I["attn_sink_2"][0])
    f["cond"] = np.stack([I["c_2"][0].reshape(KC, P).T, I["c_ctx_2"].reshape(KC, P).T], 2).reshape(P, 16)
    params = np.concatenate([f[n] for n, _ in PARAM_FIELDS], 1)
    assert params.shape == (P, N_PARAM)
    arrays = dict(w_first=np.concatenate(first, 0), w_expert=expert, w_ada=ada, w_up=fi, w_down=fo,
                  w_even=even, w_odd=odd, params=params, consts=shape_constants(),
                  positions=np.broadcast_to(I["positions"].reshape(1, TOK).astype(np.int32), (P, TOK)),
                  xT=feature_major(I["x"][0]), memT=feature_major(I["mem"][0]),
                  ctxT=feature_major(I["ctx_2"][0]))
    return {k: np.ascontiguousarray(v) for k, v in arrays.items()}


def make_program(nc, draft, arrays, upto=99):

    def declare(nc):
        a = {k: nc.dram_tensor(k, v.shape, mybir.dt.from_np(v.dtype), kind="ExternalInput").ap()
             for k, v in arrays.items()}
        a["out"] = nc.dram_tensor("out_dram", (P, KC, TOK), F32, kind="ExternalOutput").ap()
        return a
    known = build(draft, declare(draft), None, upto)
    build(nc, declare(nc), known, upto)


def kernel(**inputs):
    import concourse.bacc as bacc
    from concourse.bass_utils import run_bass_kernel_spmd
    arrays = lay_out({k: np.asarray(v) for k, v in inputs.items()})
    nc, draft = (bacc.Bacc("TRN2", target_bir_lowering=False, num_devices=1) for _ in range(2))
    make_program(nc, draft, arrays)
    r = run_bass_kernel_spmd(nc, [arrays], core_ids=[0])
    out = np.asarray(r.results[0]["out_dram"])
    return np.ascontiguousarray(out.transpose(1, 0, 2).reshape(D, TOK).T).reshape(1, TOK, D)
```

```python
from contextlib import ExitStack

import numpy as np

import concourse.bass as bass
from concourse import mybir

F32 = mybir.dt.float32
F32R = mybir.dt.float32r
I32 = mybir.dt.int32
ALU = mybir.AluOpType
ACT = mybir.ActivationFunctionType
AX = mybir.AxisListType

P = 128
D = 1024
KC = D // P
TOK = 256
HD = 64
PIECE = 2048
RAW_SLOTS = 4
SPLIT_SLOTS = 2
EXPERTS = 32
GROUPS = 4
FF_CHUNKS = 22
NEG = -1.0e30
EPS = 1e-6
MAGIC = 1.5 * 2.0 ** 23
LAMBDA_INIT = 0.8 - 0.6 * float(np.exp(0.0))
GELU_C = float(np.sqrt(2.0 / np.pi))

BLOCKS = 2 * -(-((2 * TOK + EXPERTS * (P - 1)) // P) // 2)
N_FIRST, N_EXPERT, N_UP, N_DOWN, N_EVEN, N_ODD = 32, 6 * BLOCKS, 22, 11, 16, 10
N_ADA, ADA_LOCAL = 72, 32
QKV_PIECES, EVEN_IN_PIECES = 12, 12

PARAM_FIELDS = [("g_mix", 8), ("g_cross", 8), ("g_mem", 8), ("g_ffn", 8), ("g_final", 8),
                ("final_norm", 8), ("g_sub", 1), ("lam_a", 128), ("lam_b", 128),
                ("w_fgate", 64), ("w_router", 288), ("w_gates", 128), ("b_fgate", 8),
                ("b_router", 36), ("ada_b", 144), ("conv_w", 24), ("gate_b", 16), ("mnorm", 4),
                ("sgu_norm", 512), ("sgu_ws", 512), ("sgu_b", 512), ("sink", 16), ("cond", 16)]
CONST_FIELDS = [("ident", 128), ("mask", 384), ("upto", 128), ("from", 128), ("turn_half", 128),
                ("turn_pair", 128), ("cos_x", 256), ("sin_x", 256), ("inv_freq", 1),
                ("one_over", 2), ("down4", 4), ("down32", 32), ("iota", 2 * P)]


def columns(fields):
    at, out = 0, {}
    for name, n in fields:
        out[name] = (at, at + n)
        at += n
    return out, at


PARAM_AT, N_PARAM = columns(PARAM_FIELDS)
CONST_AT, N_CONST = columns(CONST_FIELDS)


def shape_constants():
    i = np.arange(P)
    c = {}
    c["ident"] = np.eye(P)
    zero = np.zeros((P, P))
    c["mask"] = np.concatenate([np.where(i[None, :] >= i[:, None], 0.0, NEG), zero,
                                np.where(i[None, :] <= i[:, None], 0.0, NEG)], 1)
    c["iota"] = np.broadcast_to(np.arange(2 * P), (P, 2 * P)) * 1.0
    c["upto"] = (i[:, None] <= i[None, :]) * 1.0
    c["from"] = (i[:, None] >= i[None, :]) * 1.0
    half = np.zeros((P, P))
    pair = np.zeros((P, P))
    for p in range(P):
        half[p + 32 if p % 64 < 32 else p - 32, p] = -1.0 if p % 64 < 32 else 1.0
        pair[p + 1 if p % 2 == 0 else p - 1, p] = -1.0 if p % 2 == 0 else 1.0
    c["turn_half"], c["turn_pair"] = half, pair
    t = np.arange(TOK)
    freq = (np.float32(10000.0) ** (-np.arange(16, dtype=np.float32) / np.float32(16))).astype(np.float32)
    ang = np.concatenate([(t // 64).astype(np.float32)[:, None] * freq,
                          (t % 64).astype(np.float32)[:, None] * freq], 1)
    which = (i % 64) // 2
    c["cos_x"] = np.cos(ang.astype(np.float64))[:, which].T
    c["sin_x"] = np.sin(ang.astype(np.float64))[:, which].T
    inv = np.float32(10000.0) ** (-np.arange(32, dtype=np.float32) * np.float32(2.0) / np.float32(64))
    c["inv_freq"] = inv[i % 32][:, None]
    c["one_over"] = np.broadcast_to([1.0 / D, 1.0 / P], (P, 2))
    c["down4"] = np.broadcast_to(np.arange(4, 0, -1), (P, 4))
    c["down32"] = np.broadcast_to(np.arange(32, 0, -1), (P, 32))
    return np.concatenate([np.asarray(c[n], np.float32) for n, _ in CONST_FIELDS], 1)


class Steps:

    def __init__(self, known):
        self.known, self.made, self.sems, self.count = known, {}, {}, {}
        self.make = None

    def sem(self, key):
        if key not in self.sems:
            self.sems[key] = self.make(key)
        return self.sems[key]

    def did(self, key, label):
        self.count[key] = self.count.get(key, 0) + 1
        assert (key, label) not in self.made, (key, label)
        self.made[(key, label)] = self.count[key]
        return self.sem(key), 1

    def after(self, key, label):
        if self.known is None:
            return self.sem(key), 1
        return self.sem(key), self.known[(key, label)]


def build(nc, A, known=None, upto=99):
    ctx = ExitStack()
    steps = Steps(known)
    did, after = steps.did, steps.after

    def sb(name, shape, dt=F32):
        return ctx.enter_context(nc.sbuf_tensor(name, shape, dt))

    def sem(name):
        return ctx.enter_context(nc.semaphore(name))

    steps.make = sem
    PS = ctx.enter_context(nc.psum_tensor("PS", [P, 8, 512], F32))
    X = sb("X", [P, KC, 512])
    NH = sb("NH", [P, KC, 512], F32R)
    NL = sb("NL", [P, KC, 512], F32R)
    RAW = sb("RAW", [P, RAW_SLOTS, PIECE])
    SH = sb("SH", [P, SPLIT_SLOTS, PIECE], F32R)
    SL = sb("SL", [P, SPLIT_SLOTS, PIECE], F32R)
    PARAM = sb("PARAM", [P, N_PARAM])
    CONST = sb("CONST", [P, N_CONST])
    ONES = sb("ONES", [P, P])
    SWH = sb("SWH", [P, 480], F32R)
    SWL = sb("SWL", [P, 480], F32R)
    WORK = sb("WORK", [P, 2048])
    TA = sb("TA", [P, 2, 512])
    TB = sb("TB", [P, 2, 512])
    PB = sb("PB", [P, 2, 512])
    PT = sb("PT", [P, 2, 512])
    MOD = sb("MOD", [P, 2, 72, 2])
    SM = sb("SM", [P, 264])
    with nc.sbuf_tensor("ARENA", [P, 12304], F32) as ARENA:
        pass
    EXP_R = sb("EXP_R", [P, 7168], F32R)

    sm_at = [0]

    def small(n):
        a = sm_at[0]
        sm_at[0] += n
        assert sm_at[0] <= 262
        return SM[:, a:a + n]

    def param(name):
        a, b = PARAM_AT[name]
        return PARAM[:, a:b]

    def const(name):
        a, b = CONST_AT[name]
        return CONST[:, a:b]

    ident = const("ident")
    mask_from, mask_upto = const("mask")[:, 0:128], const("mask")[:, 256:384]
    SQ = WORK[:, 0:1024]
    TMP = WORK[:, 1024:2048].rearrange("p (a n) -> p a n", a=2)
    ROW = TA[0:1, :, :].rearrange("p a n -> p (a n)")

    def arena(at, *shape):
        n = int(np.prod(shape))
        v = ARENA[:, at:at + n]
        if len(shape) == 2:
            return v.rearrange("p (a b) -> p a b", a=shape[0])
        if len(shape) == 3:
            return v.rearrange("p (a b c) -> p a b c", a=shape[0], b=shape[1])
        return v

    FQ, FK, FV = arena(0, 4, 256), arena(1024, 4, 256), arena(2048, 2, 512)
    DQ, DK, DV = arena(3072, 4, 256), arena(4096, 4, 256), arena(5120, 2, 512)
    YD = arena(6144, 4, 256)
    COSD, SIND, ANG, ANGR = arena(7168, 256), arena(7424, 256), arena(7680, 256), arena(7936, 256)
    ANGK = arena(8192, 256)
    GA, GB, MG = arena(0, 8, 256), arena(2048, 8, 256), arena(4096, 8, 256)
    CQ, CK, CV = arena(0, 2, 256), arena(512, 2, 256), arena(1024, 2, 256)
    HID = arena(0, FF_CHUNKS, 512)
    QT, KT, KTOK = arena(0, 4, 512), arena(2048, 4, 512), arena(4096, 4, 512)
    VV = arena(4096, 4, 512)
    VA = arena(6144, 4, 4 * 129)
    SO, UT, HS = arena(8208, 4, 512), arena(10256, 4, 512), arena(10256, 4, 512)
    OQ, OK, OV = arena(0, 8, 256), arena(2048, 2, 512), arena(3072, 4, 256)
    C8, NC8 = TB[0:8, 0, 0:256], TB[0:8, 0, 256:512]

    NEGH, VAR, RS = small(16), small(16), small(16)
    ZERO = small(1)
    NM, RSUM, RI, ES = small(4), small(4), small(4), small(2)
    LAM, LE = small(1), small(2)
    NSINK = small(16)
    MLS = small(128)

    piece_loaded = [sem(f"piece_loaded{i}") for i in range(RAW_SLOTS)]
    high_made, low_made, piece_used = sem("high_made"), sem("low_made"), sem("piece_used")
    evacuated = sem("evacuated")
    params_in, consts_in, x_in, pos_in, mem_in, ctx_in = (
        sem(n) for n in ("params_in", "consts_in", "x_in", "pos_in", "mem_in", "ctx_in"))
    result_out = sem("result_out")
    hid_high, hid_low = sem("hid_high"), sem("hid_low")
    aux_made, aux_high, aux_done = sem("aux_made"), sem("aux_high"), sem("aux_done")
    y_high, scattered = sem("y_high"), sem("scattered")
    sel_step, sel_made, sel_gated = sem("sel_step"), sem("sel_made"), sem("sel_gated")
    act_tanh = sem("act_tanh")
    ffn_mid = sem("ffn_mid")
    ada_turned, ada_done = sem("ada_turned"), sem("ada_done")

    M = {}
    at = 0
    for name, n in (("first", QKV_PIECES), ("ada_local", ADA_LOCAL), ("second", N_FIRST - QKV_PIECES),
                    ("expert", N_EXPERT), ("up0", N_UP), ("down0", N_DOWN), ("even", EVEN_IN_PIECES),
                    ("ada_even", N_ADA - ADA_LOCAL), ("even_out", N_EVEN - EVEN_IN_PIECES),
                    ("up1", N_UP), ("down1", N_DOWN), ("up2", N_UP), ("down2", N_DOWN),
                    ("odd", N_ODD), ("up3", N_UP), ("down3", N_DOWN)):
        M[name] = at
        at += n
    N_PIECES = at
    Q = {"first": 0, "expert": N_FIRST}
    Q["up0"] = Q["expert"] + N_EXPERT
    Q["even"] = Q["up0"] + N_UP
    Q["up1"] = Q["even"] + N_EVEN
    Q["up2"] = Q["up1"] + N_UP
    Q["odd"] = Q["up2"] + N_UP
    Q["up3"] = Q["odd"] + N_ODD
    n_pieces = {1: M["second"], 2: M["second"] + 12, 3: M["second"] + 16, 4: M["expert"],
                5: M["up0"] + 1, 7: M["even"] + 1, 8: M["up1"] + 1,
                9: M["up2"] + 1, 10: M["odd"] + 1, 11: M["up3"] + 1}.get(upto, N_PIECES)

    def first(i):
        return M["first"] + i if i < QKV_PIECES else M["second"] + i - QKV_PIECES

    def even(i):
        return M["even"] + i if i < EVEN_IN_PIECES else M["even_out"] + i - EVEN_IN_PIECES

    def ada(j):
        return M["ada_local"] + j if j < ADA_LOCAL else M["ada_even"] + j - ADA_LOCAL

    def unsplit_before(m):
        return sum(ada(j) < m for j in (range(N_ADA)))

    def val(c, it=None, per=4):
        return c if it is None else it * per + c

    def load_piece(sp, src, index, m, it=None, per=4, i_per=4):
        if m >= RAW_SLOTS:
            sp.wait_ge(low_made, val(2 * (m - RAW_SLOTS + 1), it, 2 * per))
        if it is None:
            s = src[index]
        else:
            s = src[bass.ds(it * i_per + index, 1)].rearrange("a p n -> p (a n)")
        sp.dma_start(RAW[:, m % RAW_SLOTS, :], s).then_inc(piece_loaded[m % RAW_SLOTS], 16)

    HALVES = [slice(0, PIECE // 2), slice(PIECE // 2, PIECE)]

    def make_high(act, m, it=None, per=4):
        if m >= n_pieces:
            return
        act.wait_ge(piece_loaded[m % RAW_SLOTS], val(16 * (m // RAW_SLOTS + 1), it, 16 * per // RAW_SLOTS))
        if m >= SPLIT_SLOTS:
            act.wait_ge(piece_used, val(m - SPLIT_SLOTS + 1, it, per))
        for h in HALVES:
            nc.scalar.activation(SH[:, m % SPLIT_SLOTS, h], RAW[:, m % RAW_SLOTS, h], ACT.Copy
                                 ).then_inc(high_made, 1)

    def make_low(dve, m, it=None, per=4):
        if m >= n_pieces:
            return
        for i, h in enumerate(HALVES):
            dve.wait_ge(high_made, val(2 * (m - unsplit_before(m)) + i + 1, it, 2 * per))
            nc.vector.tensor_tensor(SL[:, m % SPLIT_SLOTS, h], RAW[:, m % RAW_SLOTS, h],
                                    SH[:, m % SPLIT_SLOTS, h].bitcast(F32), ALU.subtract
                                    ).then_inc(low_made, 1)

    def weights(m, a, b, c=None):
        if c is None:
            return [t[:, m % SPLIT_SLOTS, :].rearrange("p (a b) -> p a b", a=a) for t in (SH, SL)]
        return [t[:, m % SPLIT_SLOTS, :].rearrange("p (a b c) -> p a b c", a=a, b=b) for t in (SH, SL)]

    def mm3(out, w, x, start, stop, **kw):
        nc.tensor.matmul(out, w[0], x[0], start=start, stop=False, **kw)
        nc.tensor.matmul(out, w[0], x[1], start=False, stop=False, **kw)
        return nc.tensor.matmul(out, w[1], x[0], start=False, stop=stop, **kw)

    def bank(q):
        return 2 * (q % 2)

    def pe_half(pe, m, half, it=None, per=4):
        pe.wait_ge(low_made, val(2 * m + half + 1, it, 2 * per))

    def pe_claim(pe, m, q, it=None, per=4, qper=4, half=1):
        pe_half(pe, m, half, it, per)
        if q is not None and q >= 2:
            pe.wait_ge(evacuated, val(q - 1, it, qper))

    def pe_feature_major(pe, m, q, T, xs=None, kc=KC, cols=256, off=0, norm=None, **loop):
        pe_claim(pe, m, q, **loop)
        w = weights(m, kc, cols)
        n = cols // P
        per_bank = n // 2
        order = [(c, k) for c in range(n) for k in range(kc)]
        if norm is not None:
            order = [(c, k) for k in range(kc) for c in range(n)]
        for c, k in order:
            o = PS[:, bank(q) + c // per_bank, (c % per_bank) * T:(c % per_bank) * T + T]
            if norm is not None and c == 0:
                pe.wait_ge(*after("norm.dve", f"{norm} low {k}"))
            x = xs(k) if xs else [NH[:, k, off:off + T], NL[:, k, off:off + T]]
            last = mm3(o, [v[:, k, c * P:(c + 1) * P] for v in w], x, k == 0, k == kc - 1)
        last.then_inc(piece_used, 1)

    def pe_token_major(pe, m, q, T, off=0):
        pe_claim(pe, m, q)
        w = weights(m, KC, 256)
        per_bank = T // P // 2
        for b in range(T // P):
            o = PS[:, bank(q) + b // per_bank, (b % per_bank) * 256:(b % per_bank) * 256 + 256]
            for k in range(KC):
                t = slice(off + b * P, off + (b + 1) * P)
                last = mm3(o, [NH[:, k, t], NL[:, k, t]], [v[:, k, :] for v in w], k == 0, k == KC - 1)
        last.then_inc(piece_used, 1)

    TAIL = [4, 5, 6, 7, 0, 1, 2, 3]

    def act_squares(act, n, src, T, *ready):
        for r in ready:
            if isinstance(r, tuple):
                act.wait_ge(*r)
        for k in range(KC):
            for r in ready:
                if not isinstance(r, tuple):
                    act.wait_ge(*r(TAIL[k]))
            if k >= 2:
                act.wait_ge(*after("norm.pe", f"{n} sum {k - 2}"))
            nc.scalar.activation(SQ[:, (k % 2) * 512:(k % 2) * 512 + T], src(TAIL[k]), ACT.Square
                                 ).then_inc(*did("norm.act", f"{n} square {k}"))

    def pe_sums(pe, n, T):
        for k in range(KC):
            pe.wait_ge(*after("norm.act", f"{n} square {k}"))
            nc.tensor.matmul(PS[:, 4, 0:T], ONES[:, :], SQ[:, (k % 2) * 512:(k % 2) * 512 + T],
                             start=k == 0, stop=k == KC - 1).then_inc(*did("norm.pe", f"{n} sum {k}"))

    def act_row(act, n, T, last):
        act.wait_ge(*after("norm.pe", f"{n} sum {last}"))
        for i in range(0, T, 512):
            w = min(512, T - i)
            ins = nc.scalar.copy(ROW[:, i:i + w], PS[0:1, 4 + i // 512, 0:w])
        ins.then_inc(*did("norm.act", f"{n} row"))

    def pe_compact(pe, n, T, width):
        pe.wait_ge(*after("norm.act", f"{n} row"))
        for j in range(T // P):
            last = nc.tensor.matmul(PS[:, 6, j:j + 1], ROW[:, j * P:(j + 1) * P],
                                    const("one_over")[0:1, width:width + 1], start=True, stop=True)
        last.then_inc(*did("norm.pe", f"{n} compact"))

    def dve_variance(dve, n, T, eps):
        dve.wait_ge(*after("norm.pe", f"{n} compact"))
        nc.vector.tensor_scalar(VAR[:, 0:T // P], PS[:, 6, 0:T // P], eps, None, ALU.add
                                ).then_inc(*did("norm.dve", f"{n} var"))

    def pool_rstd(pool, n, T):
        pool.wait_ge(*after("norm.dve", f"{n} var"))
        nc.gpsimd.tensor_tensor(RS[:, 0:T // P], VAR[:, 0:T // P], NEGH[:, 0:T // P], ALU.pow
                                ).then_inc(*did("norm.pool", f"{n} rstd"))

    def dve_diagonal(dve, n, T):
        dve.wait_ge(*after("norm.pool", f"{n} rstd"))
        J = T // P
        nc.vector.tensor_tensor(SQ[:, 0:T].rearrange("p (j n) -> p j n", j=J),
                                ident.unsqueeze(1).to_broadcast([P, J, P]),
                                RS[:, 0:J].unsqueeze(2).to_broadcast([P, J, P]), ALU.mult
                                ).then_inc(*did("norm.dve", f"{n} diag"))

    def pe_broadcast(pe, n, T):
        pe.wait_ge(*after("norm.dve", f"{n} diag"))
        for i in range(0, T, 512):
            w = min(512, T - i)
            last = nc.tensor.matmul(PS[:, 4 + i // 512, 0:w], ONES[:, :], SQ[:, i:i + w],
                                    start=True, stop=True)
        last.then_inc(*did("norm.pe", f"{n} bcast"))

    def act_norm(act, n, T, src, *ready):
        act_squares(act, n, src, T, *ready)
        act_row(act, n, T, KC - 1)

    def pe_norm(pe, n, T):
        pe_sums(pe, n, T)
        pe_compact(pe, n, T, 0)
        pe_broadcast(pe, n, T)

    def dve_norm(dve, n, T):
        dve_variance(dve, n, T, EPS)
        dve_diagonal(dve, n, T)
        dve.wait_ge(*after("norm.pe", f"{n} bcast"))

    def dve_apply(dve, n, halves, mul, add):
        def low(k):
            dve.wait_ge(*after("norm.act", f"{n} high {k}"))
            for h in halves:
                t = slice(h * 256, h * 256 + 256)
                ins = nc.vector.scalar_tensor_tensor(NL[:, k, t], TMP[:, k % 2, t], add(k, h),
                                                     NH[:, k, t].bitcast(F32), ALU.add, ALU.subtract)
            ins.then_inc(*did("norm.dve", f"{n} low {k}"))
        for k in range(KC):
            if k >= 2:
                dve.wait_ge(*after("norm.dve", f"{n} low {k - 2}"))
            for h in halves:
                t = slice(h * 256, h * 256 + 256)
                ins = nc.vector.scalar_tensor_tensor(TMP[:, k % 2, t], X[:, k, t], mul(k, h),
                                                     PS[:, 4, t], ALU.mult, ALU.mult)
            ins.then_inc(*did("norm.dve", f"{n} scaled {k}"))
            if k >= 1:
                low(k - 1)
        low(KC - 1)

    def act_apply(act, n, halves, add):
        for k in range(KC):
            act.wait_ge(*after("norm.dve", f"{n} scaled {k}"))
            for h in halves:
                t = slice(h * 256, h * 256 + 256)
                ins = nc.scalar.activation(NH[:, k, t], TMP[:, k % 2, t], ACT.Identity, bias=add(k, h))
            ins.then_inc(*did("norm.act", f"{n} high {k}"))

    def pe_applied(pe, n):
        pe.wait_ge(*after("norm.dve", f"{n} low {KC - 1}"))

    def gain(*names):
        return lambda k, h: param(names[h])[:, k:k + 1]

    def no_shift(k, h):
        return ZERO

    def mod_col(layer, index):
        return lambda k, h: MOD[:, layer, 8 * index + k, h:h + 1]

    def fox_unit(h):
        pb, c = slice(64 * (h % 2), 64 * (h % 2) + 64), h // 2
        return dict(kind="fox", segs=[(0, 128), (128, 256)], h=h, pb=pb, c=c,
                    turns=[(0, 0), (128, 128), (256, 256)],
                    pv=[(FV[:, 0, h * 64:h * 64 + 64], 0, 128, 0, True, True),
                        (FV[:, 0, h * 64:h * 64 + 64], 128, 128, 128, True, False),
                        (FV[:, 1, h * 64:h * 64 + 64], 256, 128, 128, False, True)],
                    out=(pb, 256), dst=(NH[pb, c, 256:512], NL[pb, c, 256:512]))

    def diff_unit(h, qb):
        w = P * (qb + 1)
        return dict(kind="diff", segs=[(0, w), (w, w)], h=h, qb=qb, w=w,
                    turns=[(P * j, P * j) for j in range(qb + 1)],
                    pv=[(DV[:, j, h * P:(h + 1) * P], P * j, P, 0, j == 0, j == qb)
                        for j in range(qb + 1)],
                    out=(slice(0, P), P), dst=(YD[:, h, qb * P:(qb + 1) * P],))

    def cross_unit(h):
        pb, c = slice(64 * (h % 2), 64 * (h % 2) + 64), h // 2
        return dict(kind="cross", segs=[(0, 256), (256, 256)], h=h, pb=pb, c=c,
                    turns=[(qb * 256 + kb * P, kb * 256 + qb * P) for qb in range(2) for kb in range(2)],
                    pv=[(CV[:, kb, h * 64:h * 64 + 64], kb * 256, 256, 0, kb == 0, kb == 1)
                        for kb in range(2)],
                    out=(pb, 256), dst=(NH[pb, c, 0:256], NL[pb, c, 0:256]))

    def odd_unit(c, side, qb):
        kv = 2 * (c // 4) + side
        pb = slice(64 * side, 64 * side + 64)
        t = slice(qb * P, (qb + 1) * P)
        return dict(kind="odd", segs=[(0, 512)], h=4 * kv + c % 4, pb=pb, c=c, kc=c // 4, qb=qb,
                    turns=[(P * j, P * j) for j in range(4)],
                    pv=[(OV[:, j, kv * 64:kv * 64 + 64], P * j, P, 0, j == 0, j == 3) for j in range(4)],
                    out=(pb, P), dst=(NH[pb, c, t], NL[pb, c, t]))

    LOCAL = [fox_unit(h) for h in range(8)] + [diff_unit(h, qb) for h in range(4) for qb in range(2)]
    CROSS = [cross_unit(h) for h in range(4)]
    ODD = [odd_unit(c, side, qb) for c in range(8) for side in range(2) for qb in range(2)]

    def pe_scores(pe, u, b):
        if u["kind"] == "fox":
            for qb, (c0, w) in enumerate(u["segs"]):
                o = PS[:, b, c0:c0 + w]
                pick = ident[0:8, u["h"]:u["h"] + 1]
                q = slice(qb * P, (qb + 1) * P)
                nc.tensor.matmul(o, FQ[u["pb"], u["c"], q], FK[u["pb"], u["c"], 0:w], start=True, stop=False)
                nc.tensor.matmul(o, ident, const("mask")[:, 384 - w:384], start=False, stop=False)
                nc.tensor.matmul(o, C8[:, q], pick.to_broadcast([8, w]), start=False, stop=False)
                last = nc.tensor.matmul(o, pick.to_broadcast([8, P]), NC8[:, 0:w], start=False, stop=True)
        elif u["kind"] == "diff":
            for r, (c0, w) in enumerate(u["segs"]):
                o = PS[:, b, c0:c0 + w]
                pb = slice(64 * r, 64 * r + 64)
                nc.tensor.matmul(o, DQ[pb, u["h"], u["qb"] * P:(u["qb"] + 1) * P], DK[pb, u["h"], 0:w],
                                 start=True, stop=False)
                last = nc.tensor.matmul(o, ident, const("mask")[:, 384 - w:384], start=False, stop=True)
                if r == 0:
                    last.then_inc(*did("local.pe", f"first half {u['h']} {u['qb']}"))
                    pe.wait_ge(*after("local.pe", f"first half {u['h']} {u['qb']}"))
        elif u["kind"] == "cross":
            for qb, (c0, w) in enumerate(u["segs"]):
                last = nc.tensor.matmul(PS[:, b, c0:c0 + w], CQ[u["pb"], u["c"], qb * P:(qb + 1) * P],
                                        CK[u["pb"], u["c"], :], start=True, stop=True)
        else:
            t = slice(u["qb"] * P, (u["qb"] + 1) * P)
            m0 = 128 if u["qb"] == 0 else 0
            nc.tensor.matmul(PS[:, b, 0:256], OQ[u["pb"], u["c"], t], OK[u["pb"], u["kc"], 0:256],
                             start=True, stop=False)
            nc.tensor.matmul(PS[:, b, 0:256], ident, const("mask")[:, m0:m0 + 256], start=False, stop=True)
            last = nc.tensor.matmul(PS[:, b, 256:512], OQ[u["pb"], u["c"], t], OK[u["pb"], u["kc"], 256:512],
                                    start=True, stop=True)
        return last

    def pe_attention(pe, st, units):
        n = len(units)
        for i in range(n + 3):
            if i < n:
                if i >= 2:
                    pe.wait_ge(*after(f"{st}.act", f"exp {i - 2}"))
                pe_scores(pe, units[i], 4 + i % 2).then_inc(*did(f"{st}.pe", f"scores {i}"))
                if st == "local":
                    pe_ada(pe, local_fill(i, 0))
            if 2 <= i < n + 2:
                u = i - 2
                pe.wait_ge(*after(f"{st}.dve", f"scaled {u}"))
                if u >= 1:
                    pe.wait_ge(*after(f"{st}.act", f"turned {u - 1}"))
                for p0, t0 in units[u]["turns"]:
                    last = nc.tensor.transpose(PS[:, 6, t0:t0 + P], PB[:, u % 2, p0:p0 + P], ident)
                last.then_inc(*did(f"{st}.pe", f"turn {u}"))
            if i >= 3:
                u = i - 3
                pe.wait_ge(*after(f"{st}.act", f"turned {u}"))
                if u >= 1:
                    last_reader = "act" if units[u - 1]["kind"] == "diff" else "dve"
                    pe.wait_ge(*after(f"{st}.{last_reader}", f"out {u - 1}"))
                o = units[u]["out"][0]
                for v, p0, w, o0, start, stop in units[u]["pv"]:
                    last = nc.tensor.matmul(PS[o, 7, o0:o0 + w], v, PT[:, u % 2, p0:p0 + w],
                                            start=start, stop=stop)
                last.then_inc(*did(f"{st}.pe", f"pv {u}"))
            if i < n and st == "local":
                pe_ada(pe, local_fill(i, 1))

    def dve_attention(dve, st, units):
        n = len(units)
        for i in range(n + 4):
            if i < n:
                u, s = units[i], 2 * (i % 2)
                dve.wait_ge(*after(f"{st}.pe", f"scores {i}"))
                for j, (c0, w) in enumerate(u["segs"]):
                    ins = nc.vector.tensor_reduce(NM[:, s + j:s + j + 1], PS[:, 4 + i % 2, c0:c0 + w],
                                                  AX.X, ALU.max, negate=True)
                ins.then_inc(*did(f"{st}.dve", f"max {i}"))
                if i and st == "local":
                    dve_ada(dve, local_fill(i - 1, 1))
                if u["kind"] == "odd":
                    dve.wait_ge(*after(f"{st}.dve", f"max {i}"))
                    nc.vector.tensor_tensor(NM[:, s:s + 1], NM[:, s:s + 1], NSINK[:, u["h"]:u["h"] + 1],
                                            ALU.min).then_inc(*did(f"{st}.dve", f"shift {i}"))
            if 1 <= i <= n:
                k = i - 1
                u, s = units[k], 2 * (k % 2)
                dve.wait_ge(*after(f"{st}.act", f"exp {k}"))
                m = len(u["segs"])
                total = RSUM[:, s:s + m]
                if u["kind"] == "odd":
                    dve.wait_ge(*after(f"{st}.act", f"sink {k}"))
                    nc.vector.tensor_tensor(total, total, ES[:, k % 2:k % 2 + 1], ALU.add
                                            ).then_inc(*did(f"{st}.dve", f"total {k}"))
                    dve.wait_ge(*after(f"{st}.dve", f"total {k}"))
                nc.vector.reciprocal(RI[:, s:s + m], total).then_inc(*did(f"{st}.dve", f"recip {k}"))
                dve.wait_ge(*after(f"{st}.dve", f"recip {k}"))
                if u["kind"] == "diff":
                    w = u["w"]
                    nc.vector.tensor_scalar(PB[:, k % 2, w:2 * w], PB[:, k % 2, w:2 * w], RI[:, s + 1:s + 2],
                                            LAM, ALU.mult, ALU.mult
                                            ).then_inc(*did(f"{st}.dve", f"second {k}"))
                    dve.wait_ge(*after(f"{st}.dve", f"second {k}"))
                    ins = nc.vector.scalar_tensor_tensor(PB[:, k % 2, 0:w], PB[:, k % 2, 0:w], RI[:, s:s + 1],
                                                         PB[:, k % 2, w:2 * w], ALU.mult, ALU.subtract)
                else:
                    for j, (c0, w) in enumerate(u["segs"]):
                        ins = nc.vector.tensor_scalar(PB[:, k % 2, c0:c0 + w], PB[:, k % 2, c0:c0 + w],
                                                      RI[:, s + j:s + j + 1], None, ALU.mult)
                ins.then_inc(*did(f"{st}.dve", f"scaled {k}"))
            if i >= 4:
                k = i - 4
                u = units[k]
                o, w = u["out"]
                if u["kind"] != "diff":
                    dve.wait_ge(*after(f"{st}.act", f"out {k}"))
                if u["kind"] != "diff":
                    nc.vector.tensor_tensor(u["dst"][1], PS[o, 7, 0:w], u["dst"][0].bitcast(F32),
                                            ALU.subtract).then_inc(*did(f"{st}.dve", f"out {k}"))
            if i < n and st == "local":
                dve_ada(dve, local_fill(i, 0))

    def act_attention(act, st, units):
        n = len(units)
        for i in range(n + 4):
            if i < n:
                u, s = units[i], 2 * (i % 2)
                act.wait_ge(*after(f"{st}.dve", (f"shift {i}" if u["kind"] == "odd" else f"max {i}")))
                if i >= 2:
                    act.wait_ge(*after(f"{st}.pe", f"turn {i - 2}"))
                for j, (c0, w) in enumerate(u["segs"]):
                    ins = nc.scalar.activation(PB[:, i % 2, c0:c0 + w], PS[:, 4 + i % 2, c0:c0 + w], ACT.Exp,
                                               bias=NM[:, s + j:s + j + 1],
                                               accum_out=RSUM[:, s + j:s + j + 1])
                ins.then_inc(*did(f"{st}.act", f"exp {i}"))
                if u["kind"] == "odd":
                    nc.scalar.activation(ES[:, i % 2:i % 2 + 1], param("sink")[:, u["h"]:u["h"] + 1], ACT.Exp,
                                         bias=NM[:, s:s + 1]).then_inc(*did(f"{st}.act", f"sink {i}"))
            if 2 <= i < n + 2:
                k = i - 2
                act.wait_ge(*after(f"{st}.pe", f"turn {k}"))
                if k >= 2:
                    act.wait_ge(*after(f"{st}.pe", f"pv {k - 2}"))
                w = P * len(units[k]["turns"])
                nc.scalar.copy(PT[:, k % 2, 0:w], PS[:, 6, 0:w]).then_inc(*did(f"{st}.act", f"turned {k}"))
            if i >= 4:
                k = i - 4
                u = units[k]
                o, w = u["out"]
                act.wait_ge(*after(f"{st}.pe", f"pv {k}"))
                nc.scalar.copy(u["dst"][0], PS[o, 7, 0:w]).then_inc(*did(f"{st}.act", f"out {k}"))

    def pe_rope(pe, st, tiles, turn):
        for i, t in enumerate(tiles):
            if i >= 2:
                pe.wait_ge(*after(f"{st}.dve", f"rope sin {i - 2}"))
            o = PS[:, 4 + i % 2, :].rearrange("p (a n) -> p a n", a=2)
            nc.tensor.matmul(o, const(turn), t, start=True, stop=True
                             ).then_inc(*did(f"{st}.pe", f"rope {i}"))

    def dve_rope(dve, st, tiles, cos, sin):
        for i, t in enumerate(tiles):
            c = cos.unsqueeze(1).to_broadcast([P, 2, TOK])
            s = sin.unsqueeze(1).to_broadcast([P, 2, TOK])
            ta = TA[:, i % 2, :].rearrange("p (a n) -> p a n", a=2)
            tb = TMP[:, i % 2, :].rearrange("p (a n) -> p a n", a=2)
            o = PS[:, 4 + i % 2, :].rearrange("p (a n) -> p a n", a=2)
            nc.vector.tensor_tensor(ta, t, c, ALU.mult).then_inc(*did(f"{st}.dve", f"rope cos {i}"))
            dve.wait_ge(*after(f"{st}.pe", f"rope {i}"))
            nc.vector.tensor_tensor(tb, o, s, ALU.mult).then_inc(*did(f"{st}.dve", f"rope sin {i}"))
            dve.wait_ge(*after(f"{st}.dve", f"rope sin {i}"))
            nc.vector.tensor_tensor(t, ta, tb, ALU.add).then_inc(*did(f"{st}.dve", f"roped {i}"))

    DIFF_ROPE = [DQ[:, 0:2, :], DQ[:, 2:4, :], DK[:, 0:2, :], DK[:, 2:4, :]]
    ODD_ROPE = [OQ[:, 2 * i:2 * i + 2, :] for i in range(4)] + [OK[:, :, 0:256]]

    FFN_NORM = (4, 6, 7, 9)

    def ffn(n):
        return 512 if n < 3 else 256

    def pe_up(pe, n, j, it=None):
        T, m, q = ffn(n), M[f"up{n}"] + j, Q[f"up{n}"] + j
        pe_claim(pe, m, q, it)
        w = weights(m, KC, 2, P)
        if j == 0:
            order = [(c, k) for k in range(KC) for c in range(2)]
        else:
            order = [(c, k) for c in range(2) for k in range(KC)]
        for c, k in order:
            if j == 0 and c == 0:
                pe.wait_ge(*after("norm.dve", f"{FFN_NORM[n]} low {k}"))
            last = mm3(PS[:, bank(q) + c, 0:T], [v[:, k, c, :] for v in w],
                       [NH[:, k, 0:T], NL[:, k, 0:T]], k == 0, k == KC - 1)
        last.then_inc(piece_used, 1)

    def gate_tanh(act, m, q, t, T, it=None, per=4, tper=4):
        act.wait_ge(piece_used, val(m + 1, it, per))
        if t >= 2:
            act.wait_ge(ffn_mid, val(t - 1, it, tper))
        nc.scalar.activation(TA[:, q % 2, 0:T], PS[:, bank(q), 0:T], ACT.Tanh, scale=0.5
                             ).then_inc(act_tanh, 1)

    def gate_times(dve, m, q, t, T, dst, it=None, per=4, tper=4):
        dve.wait_ge(act_tanh, val(t + 1, it, tper))
        nc.vector.scalar_tensor_tensor(TB[:, q % 2, 0:T], TA[:, q % 2, 0:T], 1.0, PS[:, bank(q), 0:T],
                                       ALU.add, ALU.mult).then_inc(ffn_mid, 1)
        dve.wait_ge(ffn_mid, val(t + 1, it, tper))
        nc.vector.scalar_tensor_tensor(dst, TB[:, q % 2, 0:T], 0.5, PS[:, bank(q) + 1, 0:T],
                                       ALU.mult, ALU.mult).then_inc(evacuated, 1)

    def tanh_base(n):
        return 4 * BLOCKS + N_UP * n

    def hid_slot(p, T):
        s = 2 * (p % 2)
        return NH[:, s:s + 2, 0:T], NL[:, s:s + 2, 0:T]

    def hid_src(p, T, it):
        if it is None:
            return HID[:, 2 * p:2 * p + 2, 0:T]
        return HID[:, bass.ds(it * 8 + 2 * p, 2), 0:T]

    def act_hidden(act, n, p, it=None):
        T, m = ffn(n), M[f"down{n}"] + p
        if p < 2:
            act.wait_ge(piece_used, M[f"down{n}"])
            act.wait_ge(evacuated, Q[f"up{n}"] + N_UP)
        else:
            act.wait_ge(piece_used, val(m - 1, it))
        nc.scalar.activation(hid_slot(p, T)[0], hid_src(p, T, it), ACT.Copy).then_inc(hid_high, 1)

    def dve_hidden(dve, n, p, it=None):
        T = ffn(n)
        dve.wait_ge(hid_high, val(N_DOWN * n + p + 1, it))
        nc.vector.tensor_tensor(hid_slot(p, T)[1], hid_src(p, T, it), hid_slot(p, T)[0].bitcast(F32),
                                ALU.subtract).then_inc(hid_low, 1)

    def pe_down(pe, n, p, it=None):
        T, m = ffn(n), M[f"down{n}"] + p
        pe.wait_ge(hid_low, val(N_DOWN * n + p + 1, it))
        w = weights(m, 2, D)
        x = hid_slot(p, T)
        if p < N_DOWN - 1:
            for k in range(2):
                pe_half(pe, m, k, it)
                for c in range(KC):
                    last = mm3(PS[:, c, 0:T], [v[:, k, c * P:(c + 1) * P] for v in w],
                               [v[:, k, :] for v in x], p == 0 and k == 0, False, skip_group_check=True)
        else:
            pe_half(pe, m, 1)
            for c in TAIL:
                for k in range(2):
                    last = mm3(PS[:, c, 0:T], [v[:, k, c * P:(c + 1) * P] for v in w],
                               [v[:, k, :] for v in x], False, k == 1, skip_group_check=True)
                if c != TAIL[-1]:
                    last.then_inc(*did("ffn.pe", f"out {n} {c}"))
        last.then_inc(piece_used, 1)

    def pe_ffn(pe, n):
        with pe.Fori(0, 5) as it:
            for j in range(4):
                pe_up(pe, n, j, it)
        for j in (20, 21):
            pe_up(pe, n, j)
        pe.wait_ge(evacuated, Q[f"up{n}"] + N_UP)
        pe_down(pe, n, 0)
        pe_down(pe, n, 1)
        with pe.Fori(0, 2) as it:
            for p in range(2, 6):
                pe_down(pe, n, p, it)
        pe_down(pe, n, 10)

    def act_ffn(act, n):
        T, m0, q0, t0 = ffn(n), M[f"up{n}"], Q[f"up{n}"], tanh_base(n)
        with act.Fori(0, 5) as it:
            for j in range(4):
                make_high(act, m0 + j + 1, it)
                gate_tanh(act, m0 + j, q0 + j, t0 + j, T, it)
        for j in (20, 21):
            make_high(act, m0 + j + 1)
            gate_tanh(act, m0 + j, q0 + j, t0 + j, T)
        d0 = M[f"down{n}"]
        act_hidden(act, n, 0)
        for p in (0, 1):
            make_high(act, d0 + p + 1)
            act_hidden(act, n, p + 1)
        with act.Fori(0, 2) as it:
            for p in range(2, 6):
                make_high(act, d0 + p + 1, it)
                act_hidden(act, n, p + 1, it)
        make_high(act, d0 + N_DOWN)

    def dve_ffn(dve, n, layer, index):
        T, m0, q0, t0 = ffn(n), M[f"up{n}"], Q[f"up{n}"], tanh_base(n)
        with dve.Fori(0, 5) as it:
            for j in range(4):
                make_low(dve, m0 + j + 1, it)
                gate_times(dve, m0 + j, q0 + j, t0 + j, T, HID[:, bass.ds(it * 4 + j, 1), 0:T]
                           .rearrange("p a n -> p (a n)"), it)
        for j in (20, 21):
            make_low(dve, m0 + j + 1)
            gate_times(dve, m0 + j, q0 + j, t0 + j, T, HID[:, j, 0:T])
        d0 = M[f"down{n}"]
        dve_hidden(dve, n, 0)
        for p in (0, 1):
            make_low(dve, d0 + p + 1)
            dve_hidden(dve, n, p + 1)
        with dve.Fori(0, 2) as it:
            for p in range(2, 6):
                make_low(dve, d0 + p + 1, it)
                dve_hidden(dve, n, p + 1, it)
        make_low(dve, d0 + N_DOWN)
        for k in TAIL:
            if k == TAIL[-1]:
                dve.wait_ge(piece_used, d0 + N_DOWN)
            else:
                dve.wait_ge(*after("ffn.pe", f"out {n} {k}"))
            for h in range(T // 256):
                t = slice(h * 256, h * 256 + 256)
                ins = nc.vector.scalar_tensor_tensor(X[:, k, t], PS[:, k, t], mod_col(layer, index)(k, h),
                                                     X[:, k, t], ALU.mult, ALU.add)
            ins.then_inc(*did("ffn.dve", f"residual {n} {k}"))

    EXPERT_ORDER = [(s, j) for s in range(2) for j in range(4)] + [(s, 4 + p) for s in range(2) for p in range(2)]
    AUX = ["slots 0", "slots 1", "hidden 0", "gather 0", "gather 1", "hidden 1", "gather 2", "gather 3"]
    SELR = EXP_R[:, 0:512].rearrange("p (t n) -> p t n", t=2)
    SELT = EXP_R[:, 512:1024].rearrange("p (s n) -> p s n", s=2)
    HTH = EXP_R[:, 1024:2048].rearrange("p (s f n) -> p s f n", s=2, f=4)
    HTL = EXP_R[:, 2048:3072].rearrange("p (s f n) -> p s f n", s=2, f=4)
    YH = EXP_R[:, 3072:5120].rearrange("p (s n) -> p s n", s=2)
    YL = EXP_R[:, 5120:7168].rearrange("p (s n) -> p s n", s=2)
    SG = arena(7168, 2, 256)
    SG1, SG2 = arena(7680, 2, 256), arena(8192, 2, 256)
    HSL = arena(8704, 2, 512)
    CMP = ARENA[0:1, 9728:9728 + BLOCKS * EXPERTS].rearrange("p (b e) -> p b e", b=BLOCKS)
    BLOCK_EXPERT = ARENA[0:1, 10944:10944 + BLOCKS].bitcast(I32)
    BLOCK_F = ARENA[0:1, 11008:11008 + BLOCKS]
    DEST, GSLOT = ARENA[:, 11072:11076], ARENA[:, 11076:11078]

    def e_m(s, j):
        return M["expert"] + EXPERT_ORDER.index((s, j))

    def e_q(s, j):
        return Q["expert"] + EXPERT_ORDER.index((s, j))

    def aux(name):
        return 4 + AUX.index(name)

    def aux_highs(name):
        return 4 + sum(not n.startswith("slots") for n in AUX[:AUX.index(name) + 1])

    def aux_out(a):
        return PS[:, 2 + a % 2, :]

    def pe_gather(pe, r, a, it=None):
        pe.wait_ge(sel_made, 1 if it is None else val(2, it, 1))
        if a >= 2 or it is not None:
            pe.wait_ge(aux_done, val(a - 1, it, 8))
        for c in (2 * r, 2 * r + 1):
            o = aux_out(a)[:, 256 * (c % 2):256 * (c % 2) + 256]
            for tb in range(2):
                t = slice(256 + tb * P, 256 + (tb + 1) * P)
                nc.tensor.matmul(o, NH[:, c, t], SELR[:, tb, :], start=tb == 0, stop=False)
                last = nc.tensor.matmul(o, NL[:, c, t], SELR[:, tb, :], start=False, stop=tb == 1)
        last.then_inc(aux_made, 1)

    def pe_experts(pe):
        def up(s, j, it):
            m, q = e_m(s, j), e_q(s, j)
            pe_claim(pe, m, q, it, per=12, qper=12, half=0)
            w, t = weights(m, KC, 256), slice(s * P, (s + 1) * P)
            for k in range(KC):
                if k == KC // 2:
                    pe_half(pe, m, 1, it, 12)
                last = mm3(PS[:, q % 2, 0:256], [NH[:, k, t], NL[:, k, t]], [v[:, k, :] for v in w],
                           k == 0, k == KC - 1)
            last.then_inc(piece_used, 1)

        def hidden(s, it):
            a = aux(f"hidden {s}")
            pe.wait_ge(evacuated, val(e_q(s, 3) + 1, it, 12))
            pe.wait_ge(aux_done, val(a - 1, it, 8))
            for f in range(4):
                last = nc.tensor.transpose(aux_out(a)[:, f * P:(f + 1) * P], HSL[:, s, f * P:(f + 1) * P], ident)
            last.then_inc(aux_made, 1)

        def down(s, p, it):
            m, q = e_m(s, 4 + p), e_q(s, 4 + p)
            pe_claim(pe, m, q, it, per=12, qper=12, half=0)
            if p == 0:
                pe.wait_ge(aux_done, val(aux(f"hidden {s}") + 1, it, 8))
            w = weights(m, 4, 512)
            for f in range(4):
                if f == 2:
                    pe_half(pe, m, 1, it, 12)
                last = mm3(PS[:, q % 2, :], [HTH[:, s, f, :], HTL[:, s, f, :]], [v[:, f, :] for v in w],
                           f == 0, f == 3)
            last.then_inc(piece_used, 1)

        def scatter(s, it):
            pe.wait_ge(evacuated, val(e_q(s, 5) + 1, it, 12))
            for c in range(KC):
                o = PS[:, 4 + c // 2, (c % 2) * 256:(c % 2) * 256 + 256]
                for y in (YH, YL):
                    last = nc.tensor.matmul(o, y[:, s, c * P:(c + 1) * P], SELT[:, s, :], start=False,
                                            stop=False, skip_group_check=True)
            last.then_inc(scattered, 1)

        for r in range(4):
            pe_gather(pe, r, r)
        with pe.Fori(0, BLOCKS // 2) as it:
            for s in range(2):
                a = aux(f"slots {s}")
                pe.wait_ge(sel_made, val(1, it, 1))
                pe.wait_ge(aux_done, val(a - 1, it, 8))
                for tb in range(2):
                    last = nc.tensor.transpose(aux_out(a)[:, tb * P:(tb + 1) * P],
                                               SG[:, tb, s * P:(s + 1) * P], ident)
                last.then_inc(aux_made, 1)
            pe.wait_ge(aux_done, val(4, it, 8))
            for j in range(4):
                up(0, j, it)
            up(1, 0, it)
            hidden(0, it)
            for j in range(1, 4):
                up(1, j, it)
            for r in range(2):
                pe_gather(pe, r, aux(f"gather {r}"), it)
            down(0, 0, it)
            hidden(1, it)
            down(0, 1, it)
            down(1, 0, it)
            scatter(0, it)
            down(1, 1, it)
            for r in range(2, 4):
                pe_gather(pe, r, aux(f"gather {r}"), it)
            scatter(1, it)

    def gathered(t, r):
        return t[:, 2 * r:2 * r + 2, 0:256]

    def flat(t, s):
        return t[:, s, :, :].rearrange("p f n -> p (f n)")

    def psum_pairs(a):
        return aux_out(a).rearrange("p (c n) -> p c n", c=2)

    def act_gather(act, r, a, it=None):
        act.wait_ge(aux_made, val(a + 1, it, 8))
        nc.scalar.activation(gathered(NH, r), psum_pairs(a), ACT.Copy).then_inc(aux_high, 1)

    def dve_gather(dve, r, a, highs, it=None):
        dve.wait_ge(aux_high, val(highs, it, 6))
        nc.vector.tensor_tensor(gathered(NL, r), psum_pairs(a), gathered(NH, r).bitcast(F32), ALU.subtract
                                ).then_inc(aux_done, 1)

    def act_experts(act):
        def hidden(s, it):
            a = aux(f"hidden {s}")
            act.wait_ge(aux_made, val(a + 1, it, 8))
            nc.scalar.activation(flat(HTH, s), aux_out(a), ACT.Copy).then_inc(aux_high, 1)

        def up(s, j, it):
            m, q = e_m(s, j), e_q(s, j)
            make_high(act, m + 1, it, 12)
            act.wait_ge(piece_used, val(m + 1, it, 12))
            act.wait_ge(evacuated, val(q - 1, it, 12))
            nc.scalar.activation(TA[:, q % 2, 0:P], PS[:, q % 2, 0:P], ACT.Tanh, scale=0.5
                                 ).then_inc(act_tanh, 1)

        def down(s, p, it):
            m, q = e_m(s, 4 + p), e_q(s, 4 + p)
            make_high(act, m + 1, it, 12)
            act.wait_ge(piece_used, val(m + 1, it, 12))
            nc.scalar.activation(YH[:, s, 512 * p:512 * p + 512], PS[:, q % 2, :], ACT.Copy
                                 ).then_inc(y_high, 1)

        for r in range(4):
            act_gather(act, r, r)
        make_high(act, M["expert"])
        with act.Fori(0, BLOCKS // 2) as it:
            for j in range(4):
                up(0, j, it)
            up(1, 0, it)
            hidden(0, it)
            for j in range(1, 4):
                up(1, j, it)
            for r in range(2):
                act_gather(act, r, aux(f"gather {r}"), it)
            down(0, 0, it)
            hidden(1, it)
            down(0, 1, it)
            down(1, 0, it)
            down(1, 1, it)
            for r in range(2, 4):
                act_gather(act, r, aux(f"gather {r}"), it)

    def dve_experts(dve):
        def slots(s, it):
            a = aux(f"slots {s}")
            dve.wait_ge(aux_made, val(a + 1, it, 8))
            src = aux_out(a)[:, 0:256]
            nc.vector.tensor_reduce(GSLOT[:, s:s + 1], src, AX.X, ALU.add)
            nc.vector.tensor_scalar(SELT[:, s, :], src, 0.0, None, ALU.is_gt).then_inc(aux_done, 1)

        def hidden(s, it):
            n = f"hidden {s}"
            dve.wait_ge(aux_high, val(aux_highs(n), it, 6))
            nc.vector.tensor_tensor(flat(HTL, s), aux_out(aux(n)), flat(HTH, s).bitcast(F32), ALU.subtract
                                    ).then_inc(aux_done, 1)

        def up(s, j, it):
            m, q, t = e_m(s, j), e_q(s, j), 4 * s + j
            make_low(dve, m + 1, it, 12)
            dve.wait_ge(act_tanh, val(t + 1, it, 8))
            nc.vector.scalar_tensor_tensor(TB[:, q % 2, 0:P], TA[:, q % 2, 0:P], 1.0, PS[:, q % 2, 0:P],
                                           ALU.add, ALU.mult).then_inc(ffn_mid, 1)
            dve.wait_ge(ffn_mid, val(t + 1, it, 8))
            nc.vector.tensor_scalar(TB[:, q % 2, P:2 * P], TB[:, q % 2, 0:P], GSLOT[:, s:s + 1], 0.5,
                                    ALU.mult, ALU.mult).then_inc(sel_gated, 1)
            dve.wait_ge(sel_gated, val(t + 1, it, 8))
            nc.vector.tensor_tensor(HSL[:, s, j * P:(j + 1) * P], TB[:, q % 2, P:2 * P],
                                    PS[:, q % 2, P:2 * P], ALU.mult).then_inc(evacuated, 1)

        def down(s, p, it):
            m, q = e_m(s, 4 + p), e_q(s, 4 + p)
            make_low(dve, m + 1, it, 12)
            dve.wait_ge(y_high, val(2 * s + p + 1, it, 4))
            h = slice(512 * p, 512 * p + 512)
            nc.vector.tensor_tensor(YL[:, s, h], PS[:, q % 2, :], YH[:, s, h].bitcast(F32), ALU.subtract
                                    ).then_inc(evacuated, 1)

        for part in range(3):
            select(dve, 0, part)
        for r in range(4):
            dve_gather(dve, r, r, r + 1)
        make_low(dve, M["expert"])
        with dve.Fori(0, BLOCKS // 2) as it:
            for s in range(2):
                slots(s, it)
            for j in range(4):
                up(0, j, it)
                if j < 3:
                    select(dve, 1, j, it)
            up(1, 0, it)
            hidden(0, it)
            for j in range(1, 4):
                up(1, j, it)
            for r in range(2):
                dve_gather(dve, r, aux(f"gather {r}"), aux_highs(f"gather {r}"), it)
            down(0, 0, it)
            hidden(1, it)
            down(0, 1, it)
            down(1, 0, it)
            down(1, 1, it)
            for r in range(2, 4):
                dve_gather(dve, r, aux(f"gather {r}"), aux_highs(f"gather {r}"), it)
        dve.wait_ge(scattered, BLOCKS)
        nc.vector.tensor_tensor(X[:, :, 0:256], PS[:, 4:8, :].rearrange("p b (a n) -> p (b a) n", a=2),
                                X[:, :, 0:256], ALU.add).then_inc(*did("moe.dve", "residual"))

    def select(dve, n, part, it=None):
        if part == 0:
            for tb in range(2):
                for k, g in enumerate((SG1, SG2)):
                    c = 2 * k + tb
                    ins = nc.vector.tensor_scalar(g[:, tb, :], const("iota"), DEST[:, c:c + 1],
                                                  WSEL[:, c:c + 1], ALU.is_equal, ALU.mult)
            ins.then_inc(sel_step, 1)
        elif part == 1:
            dve.wait_ge(sel_step, val(2 * n + 1, it, 2))
            nc.vector.tensor_scalar(DEST, DEST, float(2 * P), None, ALU.subtract)
            nc.vector.tensor_tensor(SG, SG1, SG2, ALU.add).then_inc(sel_step, 1)
        else:
            dve.wait_ge(sel_step, val(2 * n + 2, it, 2))
            nc.vector.tensor_scalar(SELR, SG, 0.0, None, ALU.is_gt).then_inc(sel_made, 1)

    LG, ONG, PN = MLS[:, 0:72], MLS[:, 72:80], MLS[:, 80:88]
    RT = PB[:, 0, :]
    LM, O1, O2, MASK = RT[:, 0:64], RT[:, 64:128], RT[:, 128:192], RT[:, 192:256]
    NBLK, ENDS = RT[:, 320:352], (RT[:, 352:384], RT[:, 384:416])
    WSEL = RT[:, 416:420]
    COL = RT[:, 256:320]

    def v3(ap, b):
        return ap.rearrange("p (b n) -> p b n", b=b)

    def dve_router(dve):
        R = "moe.dve"
        step = [0]

        def then(ins, label=None):
            step[0] += 1
            name = label or f"router {step[0]}"
            ins.then_inc(*did(R, name))
            dve.wait_ge(*after(R, name))

        dve.wait_ge(*after("moe.pe", "logits"))
        lg = v3(LG, 2)
        then(nc.vector.tensor_tensor(lg, PS[:, 4, 0:72].rearrange("p (b n) -> p b n", b=2),
                                     param("b_router").unsqueeze(1).to_broadcast([P, 2, 36]), ALU.add))
        gl, el = lg[:, :, 0:4], lg[:, :, 4:36]
        gm, t4, tm = v3(COL[:, 0:2], 2), v3(COL[:, 2:10], 2), v3(COL[:, 10:12], 2)
        then(nc.vector.tensor_reduce(gm, gl, AX.X, ALU.max))
        b4 = [P, 2, 4]
        then(nc.vector.tensor_tensor(t4, gl, gm.to_broadcast(b4), ALU.is_ge))
        then(nc.vector.tensor_tensor(t4, t4, const("down4").unsqueeze(1).to_broadcast(b4), ALU.mult))
        then(nc.vector.tensor_reduce(tm, t4, AX.X, ALU.max))
        ong = v3(ONG, 2)
        then(nc.vector.tensor_tensor(ong, t4, tm.to_broadcast(b4), ALU.is_equal))
        then(nc.vector.tensor_tensor(t4, gl, gm.to_broadcast(b4), ALU.subtract), "group shifted")
        pn = v3(PN, 2)
        then(nc.vector.tensor_scalar(pn, ong, -1.0, -NEG, ALU.add, ALU.mult))
        lm = v3(LM, 2)
        for b in range(2):
            o = lm[:, b, :].rearrange("p (g e) -> p g e", g=GROUPS)
            then(nc.vector.tensor_tensor(o, el[:, b, :].rearrange("p (g e) -> p g e", g=GROUPS),
                                         pn[:, b, :].unsqueeze(2).to_broadcast([P, GROUPS, 8]), ALU.add))
        b32 = [P, 2, 32]
        v1, v2 = v3(COL[:, 12:14], 2), v3(COL[:, 14:16], 2)

        def pick(v, o):
            then(nc.vector.tensor_reduce(v, lm, AX.X, ALU.max))
            then(nc.vector.tensor_tensor(o, lm, v.to_broadcast(b32), ALU.is_ge))
            then(nc.vector.tensor_tensor(o, o, const("down32").unsqueeze(1).to_broadcast(b32), ALU.mult))
            then(nc.vector.tensor_reduce(tm, o, AX.X, ALU.max))
            then(nc.vector.tensor_tensor(o, o, tm.to_broadcast(b32), ALU.is_equal))

        o1, o2 = v3(O1, 2), v3(O2, 2)
        pick(v1, o1)
        then(nc.vector.scalar_tensor_tensor(lm, o1, 2 * NEG, lm, ALU.mult, ALU.add))
        pick(v2, o2)
        d = COL[:, 16:18]
        then(nc.vector.tensor_tensor(d, COL[:, 14:16], COL[:, 12:14], ALU.subtract), "second shifted")
        dve.wait_ge(*after("moe.act", "exps"))
        gs, w1, w2 = COL[:, 18:20], COL[:, 20:22], COL[:, 22:24]
        then(nc.vector.tensor_reduce(v3(gs, 2), v3(COL[:, 24:32], 2), AX.X, ALU.add))
        then(nc.vector.reciprocal(gs, gs))
        then(nc.vector.tensor_scalar(w1, COL[:, 32:34], 1.0, None, ALU.add))
        then(nc.vector.reciprocal(w1, w1))
        then(nc.vector.tensor_tensor(w1, w1, gs, ALU.mult))
        then(nc.vector.tensor_tensor(w2, w1, COL[:, 32:34], ALU.mult))
        for k in range(2):
            then(nc.vector.tensor_copy(WSEL[:, 2 * k:2 * k + 2], (w1, w2)[k]))
        then(nc.vector.tensor_tensor(v3(MASK, 2), o1, o2, ALU.add), "mask")
        dve.wait_ge(*after("moe.pe", "ranks"))
        then(nc.vector.tensor_scalar(NBLK, PS[:, 5, 64:96], 0.0, None, ALU.is_gt))
        then(nc.vector.scalar_tensor_tensor(NBLK, PS[:, 5, 64:96], float(P), NBLK, ALU.is_gt, ALU.add))
        a, b = ENDS
        then(nc.vector.tensor_copy(a, NBLK))
        for d in (1, 2, 4, 8, 16):
            then(nc.vector.tensor_copy(b[:, 0:d], a[:, 0:d]))
            then(nc.vector.tensor_tensor(b[:, d:EXPERTS], a[:, d:EXPERTS], a[:, 0:EXPERTS - d], ALU.add))
            a, b = b, a
        then(nc.vector.tensor_tensor(CMP, a[0:1, :].unsqueeze(1).to_broadcast([1, BLOCKS, EXPERTS]),
                                     const("iota")[0:1, 0:BLOCKS].unsqueeze(2).to_broadcast([1, BLOCKS, EXPERTS]),
                                     ALU.is_le))
        then(nc.vector.tensor_reduce(BLOCK_F.unsqueeze(2), CMP, AX.X, ALU.add))
        then(nc.vector.tensor_scalar(BLOCK_F, BLOCK_F, float(EXPERTS - 1), None, ALU.min))
        then(nc.vector.tensor_copy(BLOCK_EXPERT, BLOCK_F), "block experts")
        then(nc.vector.tensor_tensor(b, a, NBLK, ALU.subtract))
        then(nc.vector.scalar_tensor_tensor(lm, b.unsqueeze(1).to_broadcast(b32), float(P),
                                            v3(PS[:, 5, 0:64], 2), ALU.mult, ALU.add))
        for k, o in enumerate((o1, o2)):
            then(nc.vector.tensor_tensor(o, o, lm, ALU.mult))
            then(nc.vector.tensor_reduce(v3(DEST[:, 2 * k:2 * k + 2], 2), o, AX.X, ALU.add))
        then(nc.vector.tensor_scalar(DEST, DEST, 1.0, None, ALU.subtract), "slots")
        for i in range(4):
            dve.wait_ge(*after("moe.pe", f"token major {i}"))
            nc.vector.tensor_copy(NL[:, 2 * i:2 * i + 2, 256:512], psum_bank(2 * (i % 2) + 1)
                                  ).then_inc(*did(R, f"token major {i}"))
        nc.vector.memset(PS[:, 4:8, :], 0.0).then_inc(*did(R, "zeroed"))

    def act_router(act):
        act.wait_ge(*after("moe.dve", "second shifted"))
        nc.scalar.activation(COL[:, 24:32], COL[:, 2:10], ACT.Exp)
        nc.scalar.activation(COL[:, 32:34], COL[:, 16:18], ACT.Exp).then_inc(*did("moe.act", "exps"))
        for i in range(4):
            act.wait_ge(*after("moe.pe", f"token major {i}"))
            nc.scalar.activation(NH[:, 2 * i:2 * i + 2, 256:512], psum_bank(2 * (i % 2)), ACT.Copy
                                 ).then_inc(*did("moe.act", f"token major {i}"))

    def psum_bank(b):
        return PS[:, b, :].rearrange("p (c n) -> p c n", c=2)

    def pe_router(pe):
        for b in range(2):
            for k in range(KC):
                t = slice(b * P, (b + 1) * P)
                w = [v[:, 64:352].rearrange("p (k n) -> p k n", k=KC)[:, k, :] for v in (SWH, SWL)]
                last = mm3(PS[:, 4, b * 36:(b + 1) * 36], [NH[:, k, t], NL[:, k, t]], w, k == 0, k == KC - 1)
        last.then_inc(*did("moe.pe", "logits"))
        for i in range(4):
            if i >= 2:
                pe.wait_ge(*after("moe.dve", f"token major {i - 2}"))
                pe.wait_ge(*after("moe.act", f"token major {i - 2}"))
            for part, t in enumerate((NH, NL)):
                for c in range(2):
                    for b in range(2):
                        o = 256 * c + P * b
                        last = nc.tensor.transpose(PS[:, 2 * (i % 2) + part, o:o + P],
                                                   t[:, 2 * i + c, b * P:(b + 1) * P].bitcast(F32), ident)
            last.then_inc(*did("moe.pe", f"token major {i}"))
            if i == 1:
                pe.wait_ge(*after("moe.dve", "mask"))
                m = v3(MASK, 2)
                nc.tensor.matmul(PS[:, 5, 0:32], const("upto"), m[:, 0, :], start=True, stop=True)
                nc.tensor.matmul(PS[:, 5, 32:64], const("upto"), m[:, 1, :], start=True, stop=False)
                nc.tensor.matmul(PS[:, 5, 32:64], ONES[:, :], m[:, 0, :], start=False, stop=True)
                nc.tensor.matmul(PS[:, 5, 64:96], ONES[:, :], m[:, 0, :], start=True, stop=False)
                nc.tensor.matmul(PS[:, 5, 64:96], ONES[:, :], m[:, 1, :], start=False, stop=True
                                 ).then_inc(*did("moe.pe", "ranks"))
        pe.wait_ge(*after("moe.dve", "zeroed"))
        pe.wait_ge(*after("moe.act", "token major 3"))

    COND = param("cond")

    def ada_place(j):
        if j < ADA_LOCAL:
            return PS[0:2, j % 2, 256:512], PS[:, 2, 256 + 4 * (j % 2):260 + 4 * (j % 2)], WORK[0:2, 1548:1804]
        return PS[0:2, 6 + j % 2, 0:256], PS[:, 6 + j % 2, 256:260], WORK[0:2, 1548:1804]

    def pe_ada_turn(pe, j):
        pe.wait_ge(low_made, 2 * (ada(j) + 1))
        _, cols, row = ada_place(j)
        for c in range(2):
            last = nc.tensor.matmul(cols[:, 2 * c:2 * c + 2], row[:, c * P:(c + 1) * P], ident[0:2, 0:2],
                                    start=True, stop=True)
        last.then_inc(ada_turned, 1)

    def pe_ada(pe, js):
        for j in js:
            m = ada(j)
            pe.wait_ge(piece_loaded[m % RAW_SLOTS], 16 * (m // RAW_SLOTS + 1))
            if j >= ADA_LOCAL + 2:
                pe.wait_ge(ada_done, j - 1)
            for k in range(KC):
                last = nc.tensor.matmul(ada_place(j)[0], COND[:, 2 * k:2 * k + 2],
                                        RAW[:, m % RAW_SLOTS, 256 * k:256 * k + 256],
                                        start=k == 0, stop=k == KC - 1)
            last.then_inc(piece_used, 1)
            if j not in (0, ADA_LOCAL):
                pe_ada_turn(pe, j - 1)
            if j in (ADA_LOCAL - 1, N_ADA - 1):
                pe_ada_turn(pe, j)

    def dve_ada_columns(dve, j):
        dve.wait_ge(ada_turned, j + 1)
        l, c = divmod(2 * j, 72)
        nc.vector.tensor_tensor(MOD[:, l, c:c + 2, :], ada_place(j)[1].rearrange("p (c s) -> p c s", s=2),
                                param("ada_b")[:, 2 * j:2 * j + 2].unsqueeze(2).to_broadcast([P, 2, 2]),
                                ALU.add).then_inc(ada_done, 1)

    def dve_ada(dve, js):
        for j in js:
            if j not in (0, ADA_LOCAL):
                dve_ada_columns(dve, j - 1)
            dve.wait_ge(piece_used, ada(j) + 1)
            nc.vector.tensor_copy(ada_place(j)[2], ada_place(j)[0]).then_inc(low_made, 2)
            if j in (ADA_LOCAL - 1, N_ADA - 1):
                dve_ada_columns(dve, j)

    def dve_mod_ready(dve, done, scales, gates):
        dve.wait_ge(ada_done, done)
        for l, i in scales:
            v = MOD[:, l, 8 * i:8 * i + 8, :]
            nc.vector.tensor_scalar(v, v, 1.0, None, ALU.add)
        for l, i in gates:
            v = MOD[:, l, 8 * i:8 * i + 8, :]
            ins = nc.vector.tensor_scalar(v, v, 0.5, None, ALU.mult)
        ins.then_inc(*did("ada.dve", f"mod ready {done}"))

    LOCAL_FILL, EVEN_FILL = (1, 1), (2, 1, 1, 1)

    def fill(start, counts, turn, place):
        a = start + sum(counts) * turn + sum(counts[:place])
        return range(a, a + counts[place])

    def local_fill(i, place):
        return fill(0, LOCAL_FILL, i, place)

    def even_fill(s, place):
        return fill(ADA_LOCAL, EVEN_FILL, s, place)

    E_Q = Q["even"]
    CSTATE = WORK[:, 0:516].rearrange("p (h n) -> p h n", h=4)
    WV = WORK[:, 516:1032].rearrange("p (h n) -> p h n", h=4)
    NUM = WORK[:, 1032:1548].rearrange("p (h n) -> p h n", h=4)
    VAH = VA.rearrange("p b (h n) -> p b h n", h=4)
    LGT, GZ = MLS[:, 0:64], MLS[:, 64:128]
    CUM, TOT, REST = PT[:, 1, 0:32], PT[:, 1, 32:64], PT[:, 1, 64:96]
    AVAL, AMAX, WGT = PT[:, 1, 96:128], PT[:, 1, 128:160], PT[:, 1, 160:192]
    MSTATE = PT[:, 1, 192:196]
    MU, SML, SMX = PT[:, 1, 196:200], PT[:, 1, 200:208], PT[:, 1, 208:216]
    MNEW, DA, DAX = PT[:, 1, 216:220], PT[:, 1, 220:228], PT[:, 1, 228:236]
    DEN, RDEN = PT[:, 1, 236:240], PT[:, 1, 240:244]
    AM1 = PT[:, 1, 244:245]
    GABS, GSUM = PT[:, 1, 256:320], PT[:, 1, 320:324]
    ORDER = [(2, 3, 0, 1), (3, 2, 1, 0)]
    STEPS = [(d, i) for d in range(2) for i in range(4)]

    def gates_of(ap, k):
        return ap.rearrange("p (b d k h) -> p b d k h", b=4, d=2, k=2)[:, :, :, k, :]

    def bdh(ap):
        return ap.rearrange("p (b d h) -> p b d h", b=4, d=2)

    def heads(ap):
        return ap.rearrange("p (h n) -> p h n", h=4)

    def pe_even(pe):
        for j in range(12):
            if j in (4, 5, 10, 11):
                pe_token_major(pe, even(j), E_Q + j, 512)
            else:
                pe_feature_major(pe, even(j), E_Q + j, 512, norm=5 if j == 0 else None)
        for b in range(4):
            for k in range(KC):
                t = slice(b * P, (b + 1) * P)
                w = [v[:, 352 + 16 * k:352 + 16 * k + 16] for v in (SWH, SWL)]
                last = mm3(PS[:, 4, 16 * b:16 * b + 16], [NH[:, k, t], NL[:, k, t]], w, k == 0, k == KC - 1)
        last.then_inc(*did("even.pe", "gates"))
        pe.wait_ge(*after("even.dve", "gated v"))
        ws = param("sgu_ws").rearrange("p (g n) -> p g n", g=4)
        for g in range(4):
            if g >= 2:
                pe.wait_ge(*after("even.dve", f"mixed {g - 2}"))
            for b in range(4):
                last = nc.tensor.matmul(PS[:, 6 + g % 2, b * P:(b + 1) * P], VV[:, b, g * P:(g + 1) * P],
                                        ws[:, g, :], start=True, stop=True)
            last.then_inc(*did("even.pe", f"mixed {g}"))
        pe.wait_ge(*after("even.dve", "k 3"))
        for b in range(4):
            if b >= 2:
                pe.wait_ge(*after("even.act", f"keys turned {b - 2}"))
            for h in range(4):
                last = nc.tensor.transpose(PS[:, b % 2, h * P:(h + 1) * P], KT[:, h, b * P:(b + 1) * P], ident)
            last.then_inc(*did("even.pe", f"keys {b}"))
        pe.wait_ge(*after("even.dve", "log sigmoid"))
        for i, tri in enumerate((const("upto"), const("from"), ONES[:, :])):
            last = nc.tensor.matmul(PS[:, 5, 64 * i:64 * i + 64], tri, LGT, start=True, stop=True)
        last.then_inc(*did("even.pe", "cumulated"))
        pe.wait_ge(*after("even.dve", "a"))
        nc.tensor.transpose(PS[0:32, 6, 0:128], AVAL, ident).then_inc(*did("even.pe", "a turned"))
        pe.wait_ge(*after("even.dve", "a max diagonal"))
        nc.tensor.matmul(PS[:, 7, 0:32], ONES[0:32, :], TA[0:32, 0, 0:32], start=True, stop=True
                         ).then_inc(*did("even.pe", "a max"))
        for s, (d, i) in enumerate(STEPS):
            b = ORDER[d][i]
            t = slice(b * P, (b + 1) * P)
            pe.wait_ge(*after("even.dve", f"diagonal {s}"))
            if s:
                pe.wait_ge(*after("even.dve", f"state {s - 1}"))
            mask = (mask_upto, mask_from)[d]
            nc.tensor.matmul(PS[:, 0, :], ONES[:, :], TB[:, 0, :], start=True, stop=False)
            nc.tensor.matmul(heads(PS[:, 0, :]), ident, mask.unsqueeze(1).to_broadcast([P, 4, P]),
                             start=False, stop=True).then_inc(*did("even.pe", f"decay {s}"))
            for h in range(4):
                last = nc.tensor.matmul(PS[:, 1, h * P:(h + 1) * P], QT[:, h, t], KT[:, h, t],
                                        start=True, stop=True)
            last.then_inc(*did("even.pe", f"qk {s}"))
            for h in range(4):
                last = nc.tensor.matmul(PS[:, 4 + h // 2, 256 * (h % 2):256 * (h % 2) + 129],
                                        QT[:, h, t], CSTATE[:, h, :], start=True, stop=True)
            last.then_inc(*did("even.pe", f"inter {s}"))
            pe_ada(pe, even_fill(s, 0))
            pe.wait_ge(*after("even.dve", f"s {s}"))
            for h in range(4):
                last = nc.tensor.transpose(PS[:, 0, h * P:(h + 1) * P], PB[:, 0, h * P:(h + 1) * P], ident)
            last.then_inc(*did("even.pe", f"s turned {s}"))
            pe_ada(pe, even_fill(s, 1))
            pe.wait_ge(*after("even.act", f"s turned {s}"))
            for h in range(4):
                last = nc.tensor.matmul(PS[:, 2 + h // 2, 256 * (h % 2):256 * (h % 2) + 129],
                                        PT[:, 0, h * P:(h + 1) * P], VAH[:, b, h, :], start=True, stop=True)
            last.then_inc(*did("even.pe", f"intra {s}"))
            if i < 3:
                pe.wait_ge(*after("even.dve", f"weighted v {s}"))
                for h in range(4):
                    last = nc.tensor.matmul(PS[:, h // 2, 256 * (h % 2):256 * (h % 2) + 129],
                                            KTOK[:, b, h * P:(h + 1) * P], WV[:, h, :], start=True, stop=True)
                last.then_inc(*did("even.pe", f"local state {s}"))
            for place in (2, 3):
                pe_ada(pe, even_fill(s, place))
        for b in range(4):
            pe.wait_ge(*after("even.dve", f"head normed {b}"))
            if b >= 2:
                pe.wait_ge(*after("even.dve", f"head out {b - 2}"))
            for h in range(4):
                last = nc.tensor.transpose(PS[:, 6 + b % 2, h * P:(h + 1) * P],
                                           HS[:, b, h * P:(h + 1) * P], ident)
            last.then_inc(*did("even.pe", f"head turned {b}"))
        pe.wait_ge(*after("even.dve", "head low 3"))
        for j in range(12, 16):
            pe_feature_major(pe, even(j), E_Q + j, 512)

    def act_even(act):
        def tanh_of(src, dst, label, scale):
            nc.scalar.activation(dst, src, ACT.Tanh, scale=scale).then_inc(*did("even.act", label))
        for j in range(12):
            m, q = even(j), E_Q + j
            if j < 11:
                make_high(act, m + 1)
            src = PS[:, bank(q):bank(q) + 2, :]
            if j < 4:
                for c in range(2):
                    act.wait_ge(*after("even.dve", f"conv {2 * j + c}"))
                    tanh_of(TB[:, c, :], TA[:, c, :], f"qk tanh {2 * j + c}", 0.5)
            elif j in (6, 7):
                act.wait_ge(piece_used, m + 1)
                tanh_of(src, SO[:, 2 * (j - 6):2 * (j - 6) + 2, :], f"o {j}", 0.5)
            elif j >= 8:
                act.wait_ge(piece_used, m + 1)
                act.wait_ge(evacuated, q)
                nc.scalar.activation(TA[:, :, :], src, ACT.Square).then_inc(*did("even.act", f"uv square {j}"))
                act.wait_ge(*after("even.dve", f"uv inner {j}"))
                tanh_of(TB[:, :, :], TA[:, :, :], f"uv tanh {j}", GELU_C)
        act.wait_ge(*after("even.dve", "gates"))
        nc.scalar.activation(GABS, GZ, ACT.Abs).then_inc(*did("even.act", "gates abs"))
        act.wait_ge(*after("even.act", "gates abs"))
        nc.scalar.activation(GABS, GABS, ACT.Exp, scale=-1.0).then_inc(*did("even.act", "gates exp"))
        act.wait_ge(*after("even.act", "gates exp"))
        nc.scalar.activation(LGT, GABS, ACT.Ln, bias=1.0).then_inc(*did("even.act", "gates ln"))
        act.wait_ge(*after("even.dve", "uv 11"))
        for b in range(4):
            ins = nc.scalar.activation((TB, TA)[b // 2][:, b % 2, :], VV[:, b, :], ACT.Square,
                                       accum_out=GSUM[:, b:b + 1])
        ins.then_inc(*did("even.act", "gated squares"))
        for g in range(4):
            act.wait_ge(*after("even.dve", f"gated {g}"))
            nc.scalar.activation(NH[:, 4 + g, :], TB[:, g % 2, :], ACT.Copy
                                 ).then_inc(*did("even.act", f"gated high {g}"))
        for b in range(4):
            act.wait_ge(*after("even.pe", f"keys {b}"))
            nc.scalar.copy(KTOK[:, b, :], PS[:, b % 2, :]).then_inc(*did("even.act", f"keys turned {b}"))
        act.wait_ge(*after("even.dve", "a shifted"))
        nc.scalar.activation(WGT, AVAL, ACT.Exp).then_inc(*did("even.act", "a exp"))
        for s, (d, i) in enumerate(STEPS):
            act.wait_ge(*after("even.dve", f"decay shifted {s}"))
            nc.scalar.activation(TA[:, 1, :], TA[:, 0, :], ACT.Exp).then_inc(*did("even.act", f"decay {s}"))
            act.wait_ge(*after("even.dve", f"small {s}"))
            nc.scalar.activation(SMX, SML, ACT.Exp).then_inc(*did("even.act", f"small {s}"))
            act.wait_ge(*after("even.pe", f"s turned {s}"))
            nc.scalar.copy(PT[:, 0, :], PS[:, 0, :]).then_inc(*did("even.act", f"s turned {s}"))
            act.wait_ge(*after("even.dve", f"numerator {s}"))
            nc.scalar.activation(DEN.unsqueeze(2), NUM[:, :, 128:129], ACT.Abs
                                 ).then_inc(*did("even.act", f"denominator {s}"))
            if i < 3:
                act.wait_ge(*after("even.dve", f"new m {s}"))
                nc.scalar.activation(DAX, DA, ACT.Exp).then_inc(*did("even.act", f"new m {s}"))
        make_high(act, even(12))
        for b in range(4):
            act.wait_ge(*after("even.dve", f"h {len(STEPS) - 1}"))
            if b >= 2:
                act.wait_ge(*after("even.dve", f"head sum {b - 2}"))
            nc.scalar.activation(TA[:, b % 2, :], HS[:, b, :], ACT.Square
                                 ).then_inc(*did("even.act", f"head square {b}"))
        for b in range(4):
            t = slice(b * P, (b + 1) * P)
            act.wait_ge(*after("even.dve", f"head out {b}"))
            nc.scalar.activation(NH[:, 0:4, t], heads(TB[:, b % 2, :]), ACT.Copy
                                 ).then_inc(*did("even.act", f"head high {b}"))
        for j in range(12, 16):
            make_high(act, even(j) + 1)

    def dve_even(dve):
        E = "even.dve"
        conv = param("conv_w").rearrange("p (c j) -> p c j", c=KC)
        for j in range(4):
            m, q = even(j), E_Q + j
            make_low(dve, m + 1)
            dve.wait_ge(piece_used, m + 1)
            for c in range(2):
                ch = 2 * j + c
                src, dst = PS[:, bank(q) + c, :], TB[:, c, :]
                nc.vector.tensor_scalar(dst, src, conv[:, ch, 1:2], None, ALU.mult
                                        ).then_inc(*did(E, f"conv mid {ch}"))
                dve.wait_ge(*after(E, f"conv mid {ch}"))
                s2, d2 = src.rearrange("p (s t) -> p s t", s=2), dst.rearrange("p (s t) -> p s t", s=2)
                nc.vector.scalar_tensor_tensor(d2[:, :, 1:TOK], s2[:, :, 0:TOK - 1], conv[:, ch, 0:1],
                                               d2[:, :, 1:TOK], ALU.mult, ALU.add
                                               ).then_inc(*did(E, f"conv before {ch}"))
                dve.wait_ge(*after(E, f"conv before {ch}"))
                nc.vector.scalar_tensor_tensor(d2[:, :, 0:TOK - 1], s2[:, :, 1:TOK], conv[:, ch, 2:3],
                                               d2[:, :, 0:TOK - 1], ALU.mult, ALU.add
                                               ).then_inc(*did(E, f"conv {ch}"))
            for c in range(2):
                ch = 2 * j + c
                dst = (QT, KT)[ch // 4][:, ch % 4, :]
                dve.wait_ge(*after("even.act", f"qk tanh {ch}"))
                nc.vector.scalar_tensor_tensor(dst, TA[:, c, :], 1.0, TB[:, c, :], ALU.add, ALU.mult
                                               ).then_inc(*did(E, f"qk twice {ch}"))
                dve.wait_ge(*after(E, f"qk twice {ch}"))
                ins = nc.vector.tensor_scalar(dst, dst, 0.5, float(P) ** -0.5 if ch >= 4 else 1.0,
                                              ALU.mult, ALU.mult)
                if c == 0:
                    ins.then_inc(*did(E, f"half {ch}"))
                else:
                    ins.then_inc(evacuated, 1)
        dve.wait_ge(evacuated, E_Q + 4)
        nc.vector.memset(VAH[:, :, :, 128:129], 1.0).then_inc(*did(E, "k 3"))
        for j in (4, 5):
            m, q = even(j), E_Q + j
            make_low(dve, m + 1)
            dve.wait_ge(piece_used, m + 1)
            h = 2 * (j - 4)
            for i in range(2):
                src = PS[:, bank(q) + i, :].rearrange("p (b h n) -> p b h n", b=2, h=2)
                ins = nc.vector.tensor_copy(VAH[:, 2 * i:2 * i + 2, h:h + 2, 0:128], src)
            ins.then_inc(evacuated, 1)
        for j in (6, 7):
            make_low(dve, even(j) + 1)
            dve.wait_ge(*after("even.act", f"o {j}"))
            v = SO[:, 2 * (j - 6):2 * (j - 6) + 2, :]
            nc.vector.tensor_scalar(v, v, 0.5, 0.5, ALU.mult, ALU.add).then_inc(evacuated, 1)
        for j in (8, 9, 10, 11):
            m, q = even(j), E_Q + j
            if j < 11:
                make_low(dve, m + 1)
            src = PS[:, bank(q):bank(q) + 2, :]
            dve.wait_ge(*after("even.act", f"uv square {j}"))
            nc.vector.tensor_scalar(TB[:, :, :], TA[:, :, :], 0.044715, 1.0, ALU.mult, ALU.add
                                    ).then_inc(*did(E, f"uv square {j}"))
            dve.wait_ge(*after(E, f"uv square {j}"))
            nc.vector.tensor_tensor(TB[:, :, :], TB[:, :, :], src, ALU.mult
                                    ).then_inc(*did(E, f"uv inner {j}"))
            dve.wait_ge(*after("even.act", f"uv tanh {j}"))
            nc.vector.scalar_tensor_tensor(TB[:, :, :], TA[:, :, :], 1.0, src, ALU.add, ALU.mult
                                           ).then_inc(evacuated, 1)
            dve.wait_ge(evacuated, q + 1)
            if j < 10:
                c = 2 * (j - 8)
                nc.vector.tensor_scalar(UT[:, c:c + 2, :], TB[:, :, :], 0.5, None, ALU.mult
                                        ).then_inc(*did(E, f"uv {j}"))
            else:
                c = 256 * (j - 10)
                nc.vector.tensor_scalar(VV[:, :, c:c + 256],
                                        TB[:, :, :].rearrange("p a (b n) -> p (a b) n", b=2), 0.5, None,
                                        ALU.mult).then_inc(*did(E, f"uv {j}"))
            dve.wait_ge(*after(E, f"uv {j}"))
        dve.wait_ge(*after("even.pe", "gates"))
        nc.vector.tensor_tensor(GZ.rearrange("p (b n) -> p b n", b=4),
                                PS[:, 4, 0:64].rearrange("p (b n) -> p b n", b=4),
                                param("gate_b").unsqueeze(1).to_broadcast([P, 4, 16]), ALU.add
                                ).then_inc(*did(E, "gates"))
        dve.wait_ge(*after("even.act", "gates ln"))
        nc.vector.scalar_tensor_tensor(LGT, GZ, 0.0, LGT, ALU.min, ALU.subtract
                                       ).then_inc(*did(E, "log sigmoid"))
        dve.wait_ge(*after("even.act", "gated squares"))
        nc.vector.tensor_scalar(VAR[:, 0:4], GSUM, 1.0 / 512, EPS, ALU.mult, ALU.add
                                ).then_inc(*did(E, "gating var"))
        dve.wait_ge(*after("even.pool", "gating rstd"))
        for b in range(4):
            ins = nc.vector.scalar_tensor_tensor(VV[:, b, :], VV[:, b, :], RS[:, b:b + 1],
                                                 param("sgu_norm"), ALU.mult, ALU.mult)
        ins.then_inc(*did(E, "gated v"))
        sgb = heads(param("sgu_b"))
        for g in range(4):
            dve.wait_ge(*after("even.pe", f"mixed {g}"))
            tb = TB[:, g % 2, :]
            if g >= 2:
                dve.wait_ge(*after("even.act", f"gated high {g - 2}"))
            nc.vector.tensor_tensor(heads(tb), heads(PS[:, 6 + g % 2, :]),
                                    sgb[:, g, :].unsqueeze(1).to_broadcast([P, 4, P]), ALU.add
                                    ).then_inc(*did(E, f"mixed {g}"))
            dve.wait_ge(*after(E, f"mixed {g}"))
            nc.vector.tensor_tensor(tb, tb, UT[:, g, :], ALU.mult).then_inc(*did(E, f"gated {g}"))
            dve.wait_ge(*after("even.act", f"gated high {g}"))
            nc.vector.tensor_tensor(NL[:, 4 + g, :], tb, NH[:, 4 + g, :].bitcast(F32), ALU.subtract
                                    ).then_inc(*did(E, f"gated low {g}"))
        dve.wait_ge(*after("even.pe", "cumulated"))
        for d in range(2):
            nc.vector.tensor_copy(bdh(CUM)[:, :, d, :], gates_of(PS[:, 5, 64 * d:64 * d + 64], 1)[:, :, d, :])
        nc.vector.tensor_copy(bdh(TOT), gates_of(PS[:, 5, 128:192], 1)).then_inc(*did(E, "cumulated"))
        dve.wait_ge(*after(E, "cumulated"))
        nc.vector.tensor_tensor(bdh(REST), gates_of(GZ, 0), bdh(CUM), ALU.subtract).then_inc(*did(E, "rest"))
        dve.wait_ge(*after(E, "rest"))
        nc.vector.tensor_tensor(AVAL, TOT, REST, ALU.add).then_inc(*did(E, "a"))
        dve.wait_ge(*after("even.pe", "a turned"))
        nc.vector.tensor_reduce(AM1[0:32, :], PS[0:32, 6, 0:128], AX.X, ALU.max).then_inc(*did(E, "a max"))
        dve.wait_ge(*after(E, "a max"))
        nc.vector.tensor_scalar(TA[0:32, 0, 0:32], ident[0:32, 0:32], AM1[0:32, :], None, ALU.mult
                                ).then_inc(*did(E, "a max diagonal"))
        dve.wait_ge(*after("even.pe", "a max"))
        nc.vector.tensor_copy(AMAX, PS[:, 7, 0:32]).then_inc(*did(E, "a max everywhere"))
        dve.wait_ge(*after(E, "a max everywhere"))
        nc.vector.tensor_tensor(AVAL, AVAL, AMAX, ALU.subtract).then_inc(*did(E, "a shifted"))
        dve.wait_ge(*after("even.act", "a exp"))
        for s, (d, i) in enumerate(STEPS):
            b = ORDER[d][i]
            if i == 0:
                nc.vector.memset(MSTATE, 0.0)
                nc.vector.memset(WORK[:, 0:516], 0.0).then_inc(*did(E, f"start {s}"))
                dve.wait_ge(*after(E, f"start {s}"))
            cum, tot, rest, amax, wgt = (bdh(t)[:, b, d, :] for t in (CUM, TOT, REST, AMAX, WGT))
            if s:
                dve.wait_ge(*after("even.pe", f"decay {s - 1}"))
            nc.vector.tensor_tensor(heads(TB[:, 0, :]), ident.unsqueeze(1).to_broadcast([P, 4, P]),
                                    rest.unsqueeze(2).to_broadcast([P, 4, P]), ALU.mult
                                    ).then_inc(*did(E, f"diagonal {s}"))
            nc.vector.tensor_tensor(WV[:, :, :], VAH[:, b, :, :], wgt.unsqueeze(2).to_broadcast([P, 4, 129]),
                                    ALU.mult).then_inc(*did(E, f"weighted v {s}"))
            dve.wait_ge(*after("even.pe", f"decay {s}"))
            nc.vector.tensor_reduce(MU.unsqueeze(2), heads(PS[:, 0, :]), AX.X, ALU.max
                                    ).then_inc(*did(E, f"row max {s}"))
            dve.wait_ge(*after(E, f"row max {s}"))
            nc.vector.tensor_tensor(MU, MU, MSTATE, ALU.max).then_inc(*did(E, f"mu {s}"))
            dve.wait_ge(*after(E, f"mu {s}"))
            nc.vector.tensor_tensor(heads(TA[:, 0, :]), heads(PS[:, 0, :]),
                                    MU.unsqueeze(2).to_broadcast([P, 4, P]), ALU.subtract
                                    ).then_inc(*did(E, f"decay shifted {s}"))
            nc.vector.tensor_tensor(SML[:, 0:4], MSTATE, MU, ALU.subtract)
            nc.vector.scalar_tensor_tensor(SML[:, 4:8], cum, -1.0, MU, ALU.mult, ALU.subtract
                                           ).then_inc(*did(E, f"small {s}"))
            dve.wait_ge(*after("even.act", f"decay {s}"))
            dve.wait_ge(*after("even.pe", f"qk {s}"))
            nc.vector.tensor_tensor(PB[:, 0, :], PS[:, 1, :], TA[:, 1, :], ALU.mult
                                    ).then_inc(*did(E, f"s {s}"))
            dve_ada(dve, even_fill(s, 0))
            dve.wait_ge(*after("even.act", f"small {s}"))
            dve.wait_ge(*after("even.pe", f"inter {s}"))
            for k in range(2):
                hh = slice(2 * k, 2 * k + 2)
                ins = nc.vector.tensor_tensor(NUM[:, hh, :],
                                              PS[:, 4 + k, :].rearrange("p (h n) -> p h n", h=2)[:, :, 0:129],
                                              SMX[:, hh].unsqueeze(2).to_broadcast([P, 2, 129]), ALU.mult)
            ins.then_inc(*did(E, f"inter {s}"))
            dve_ada(dve, even_fill(s, 1))
            dve.wait_ge(*after(E, f"inter {s}"))
            dve.wait_ge(*after("even.pe", f"intra {s}"))
            for k in range(2):
                hh = slice(2 * k, 2 * k + 2)
                ins = nc.vector.tensor_tensor(NUM[:, hh, :],
                                              PS[:, 2 + k, :].rearrange("p (h n) -> p h n", h=2)[:, :, 0:129],
                                              NUM[:, hh, :], ALU.add)
            ins.then_inc(*did(E, f"numerator {s}"))
            dve.wait_ge(*after("even.act", f"denominator {s}"))
            nc.vector.tensor_tensor(DEN, DEN, SMX[:, 4:8], ALU.max).then_inc(*did(E, f"bounded {s}"))
            dve.wait_ge(*after(E, f"bounded {s}"))
            nc.vector.reciprocal(RDEN, DEN).then_inc(*did(E, f"recip {s}"))
            dve.wait_ge(*after(E, f"recip {s}"))
            rd = RDEN.unsqueeze(2).to_broadcast([P, 4, P])
            if d == 0:
                nc.vector.tensor_tensor(heads(HS[:, b, :]), NUM[:, :, 0:128], rd, ALU.mult
                                        ).then_inc(*did(E, f"h {s}"))
            else:
                nc.vector.tensor_tensor(heads(TB[:, 1, :]), NUM[:, :, 0:128], rd, ALU.mult
                                        ).then_inc(*did(E, f"h back {s}"))
                dve.wait_ge(*after(E, f"h back {s}"))
                nc.vector.tensor_tensor(HS[:, b, :], HS[:, b, :], TB[:, 1, :], ALU.add
                                        ).then_inc(*did(E, f"h {s}"))
            dve_ada(dve, even_fill(s, 2))
            if i < 3:
                nc.vector.tensor_tensor(DA[:, 0:4], MSTATE, tot, ALU.add).then_inc(*did(E, f"g plus m {s}"))
                dve.wait_ge(*after(E, f"g plus m {s}"))
                nc.vector.tensor_tensor(MNEW, DA[:, 0:4], amax, ALU.max).then_inc(*did(E, f"m new {s}"))
                dve.wait_ge(*after(E, f"m new {s}"))
                nc.vector.tensor_tensor(DA[:, 0:4], DA[:, 0:4], MNEW, ALU.subtract)
                nc.vector.tensor_tensor(DA[:, 4:8], amax, MNEW, ALU.subtract).then_inc(*did(E, f"new m {s}"))
                nc.vector.tensor_copy(MSTATE, MNEW)
                dve.wait_ge(*after("even.act", f"new m {s}"))
                dve.wait_ge(*after("even.pe", f"local state {s}"))
                nc.vector.tensor_tensor(CSTATE, CSTATE, DAX[:, 0:4].unsqueeze(2).to_broadcast([P, 4, 129]),
                                        ALU.mult)
                for k in range(2):
                    hh = slice(2 * k, 2 * k + 2)
                    ins = nc.vector.tensor_tensor(
                        WV[:, hh, :], PS[:, k, :].rearrange("p (h n) -> p h n", h=2)[:, :, 0:129],
                        DAX[:, 4 + 2 * k:6 + 2 * k].unsqueeze(2).to_broadcast([P, 2, 129]), ALU.mult)
                ins.then_inc(*did(E, f"new part {s}"))
                dve.wait_ge(*after(E, f"new part {s}"))
                nc.vector.tensor_tensor(CSTATE, CSTATE, WV, ALU.add).then_inc(*did(E, f"state {s}"))
                dve.wait_ge(*after(E, f"state {s}"))
            else:
                dve.wait_ge(*after(E, f"h {s}"))
                nc.vector.memset(MNEW, 0.0).then_inc(*did(E, f"state {s}"))
            dve_ada(dve, even_fill(s, 3))
        dve_mod_ready(dve, N_ADA, [(1, 1), (1, 4), (1, 7)], [(0, 8), (1, 2), (1, 8)])
        make_low(dve, even(12))
        for b in range(4):
            dve.wait_ge(*after("even.act", f"head square {b}"))
            nc.vector.tensor_reduce(GABS[:, 4 * b:4 * b + 4].unsqueeze(2), heads(TA[:, b % 2, :]), AX.X,
                                    ALU.add).then_inc(*did(E, f"head sum {b}"))
        dve.wait_ge(*after(E, "head sum 3"))
        nc.vector.tensor_scalar(VAR, GABS[:, 0:16], 1.0 / P, EPS, ALU.mult, ALU.add
                                ).then_inc(*did(E, "head var"))
        dve.wait_ge(*after("even.pool", "head rstd"))
        for b in range(4):
            nc.vector.tensor_tensor(heads(HS[:, b, :]), heads(HS[:, b, :]),
                                    RS[:, 4 * b:4 * b + 4].unsqueeze(2).to_broadcast([P, 4, P]), ALU.mult
                                    ).then_inc(*did(E, f"head normed {b}"))
        for b in range(4):
            t = slice(b * P, (b + 1) * P)
            dve.wait_ge(*after("even.pe", f"head turned {b}"))
            if b >= 2:
                dve.wait_ge(*after("even.act", f"head high {b - 2}"))
            for h in range(4):
                ins = nc.vector.scalar_tensor_tensor(TB[:, b % 2, h * P:(h + 1) * P],
                                                     PS[:, 6 + b % 2, h * P:(h + 1) * P],
                                                     param("mnorm")[:, h:h + 1], SO[:, h, t],
                                                     ALU.mult, ALU.mult)
            ins.then_inc(*did(E, f"head out {b}"))
            dve.wait_ge(*after("even.act", f"head high {b}"))
            nc.vector.tensor_tensor(NL[:, 0:4, t], heads(TB[:, b % 2, :]), NH[:, 0:4, t].bitcast(F32),
                                    ALU.subtract).then_inc(*did(E, f"head low {b}"))
        for j in range(12, 16):
            m, q = even(j), E_Q + j
            make_low(dve, m + 1)
            dve.wait_ge(piece_used, m + 1)
            for c in range(2):
                k = 2 * (j - 12) + c
                for h in range(2):
                    t = slice(h * 256, h * 256 + 256)
                    ins = nc.vector.scalar_tensor_tensor(X[:, k, t], PS[:, bank(q) + c, t],
                                                         mod_col(0, 5)(k, h), X[:, k, t], ALU.mult, ALU.add)
            ins.then_inc(evacuated, 1)
        dve.wait_ge(evacuated, E_Q + N_EVEN)

    def finish(dve):
        dve.drain()
        if upto < 7:
            dve.wait_ge(ctx_in, 16)
        nc.vector.tensor_copy(SM[:, 263:264], ZERO).then_inc(*did("end.dve", "result"))

    def evac_copy(dve, m, q, dst, scale=None, T=256):
        dve.wait_ge(piece_used, m + 1)
        src = PS[:, bank(q):bank(q) + 2, 0:T]
        if scale is None:
            nc.vector.tensor_copy(dst, src).then_inc(evacuated, 1)
        else:
            nc.vector.tensor_scalar(dst, src, scale, None, ALU.mult).then_inc(evacuated, 1)

    block = ctx.enter_context(nc.Block())

    @block.sync
    def _(sp):
        def group(src, i0, m0, n):
            n = min(n, n_pieces - m0)
            if n <= 0:
                return
            j = 0
            while m0 + j < RAW_SLOTS and j < n:
                load_piece(sp, src, i0 + j, m0 + j)
                j += 1
            if (n - j) // 4 > 1:
                with sp.Fori(0, (n - j) // 4) as it:
                    for r in range(4):
                        load_piece(sp, src, i0 + j + r, m0 + j + r, it)
                j += 4 * ((n - j) // 4)
            while j < n:
                load_piece(sp, src, i0 + j, m0 + j)
                j += 1
        group(A["w_first"], 0, M["first"], QKV_PIECES)
        group(A["w_ada"], 0, M["ada_local"], ADA_LOCAL)
        group(A["w_first"], QKV_PIECES, M["second"], N_FIRST - QKV_PIECES)
        sp.wait_ge(*after("moe.dve", "block experts"))
        if upto >= 5:
            with sp.Fori(0, BLOCKS // 2) as it:
                e = [sp.value_load(BLOCK_EXPERT[0:1, bass.ds(it * 2 + s, 1)], min_val=0, max_val=EXPERTS - 1)
                     for s in range(2)]
                for r, (s, j) in enumerate(EXPERT_ORDER):
                    m = M["expert"] + r
                    sp.wait_ge(low_made, val(2 * (m - RAW_SLOTS + 1), it, 24))
                    sp.dma_start(RAW[:, m % RAW_SLOTS, :],
                                 A["w_expert"][bass.ds(e[s] * 6 + j, 1)].rearrange("a p n -> p (a n)")
                                 ).then_inc(piece_loaded[m % RAW_SLOTS], 16)
        group(A["w_up"], 0, M["up0"], N_UP)
        group(A["w_down"], 0, M["down0"], N_DOWN)
        group(A["w_even"], 0, M["even"], EVEN_IN_PIECES)
        group(A["w_ada"], ADA_LOCAL, M["ada_even"], N_ADA - ADA_LOCAL)
        group(A["w_even"], EVEN_IN_PIECES, M["even_out"], N_EVEN - EVEN_IN_PIECES)
        for n in (1, 2):
            group(A["w_up"], N_UP * n, M[f"up{n}"], N_UP)
            group(A["w_down"], N_DOWN * n, M[f"down{n}"], N_DOWN)
        group(A["w_odd"], 0, M["odd"], N_ODD)
        group(A["w_up"], N_UP * 3, M["up3"], N_UP)
        group(A["w_down"], N_DOWN * 3, M["down3"], N_DOWN)
        sp.wait_ge(*after("end.dve", "result"))
        sp.dma_start(A["out"], X[:, :, 0:256]).then_inc(result_out, 16)
        sp.wait_ge(result_out, 16)

    @block.scalar
    def _(act):
        act.dma_start(X[:, :, 0:256], A["xT"]).then_inc(x_in, 16)
        act.dma_start(PARAM[:, :], A["params"]).then_inc(params_in, 16)
        act.dma_start(CONST[:, :], A["consts"]).then_inc(consts_in, 16)
        act.dma_start(ANGK.bitcast(I32), A["positions"]).then_inc(pos_in, 16)
        act.dma_start(X[:, :, 256:512], A["memT"]).then_inc(mem_in, 16)
        act.wait_ge(params_in, 16)
        a0 = PARAM_AT["w_fgate"][0]
        nc.scalar.activation(SWH[:, :], PARAM[:, a0:a0 + 480], ACT.Copy).then_inc(*did("set.act", "small high"))
        act.wait_ge(*after("set.dve", "sine angle"))
        nc.scalar.activation(SIND, ANG, ACT.Sin).then_inc(*did("set.act", "sine"))
        act.wait_ge(*after("set.dve", "cosine angle"))
        nc.scalar.activation(COSD, ANGR, ACT.Sin).then_inc(*did("set.act", "cosine"))
        act.wait_ge(*after("set.dve", "lambda sums"))
        nc.scalar.activation(LE, LE, ACT.Exp).then_inc(*did("set.act", "lambda exps"))
        nc.scalar.activation(TB[:, 1, 0:16], COND, ACT.Tanh, scale=0.5).then_inc(*did("set.act", "condition tanh"))
        make_high(act, 0)
        act_norm(act, 0, 256, lambda k: X[:, k, 0:256], (x_in, 16))
        act_apply(act, 0, (0,), no_shift)
        for m in range(QKV_PIECES - 1):
            make_high(act, m + 1)
        FZ, FA, FL = PB[:, 0, 0:16], PB[:, 0, 16:32], PB[:, 0, 32:48]
        act.wait_ge(*after("local.dve", "forget logits"))
        nc.scalar.activation(FA, FZ, ACT.Abs).then_inc(*did("local.act", "forget abs"))
        act.wait_ge(*after("local.act", "forget abs"))
        nc.scalar.activation(FA, FA, ACT.Exp, scale=-1.0).then_inc(*did("local.act", "forget exp"))
        act.wait_ge(*after("local.act", "forget exp"))
        nc.scalar.activation(FL, FA, ACT.Ln, bias=1.0).then_inc(*did("local.act", "forget ln"))
        act_attention(act, "local", LOCAL)
        act.wait_ge(*after("local.pe", f"pv {len(LOCAL) - 1}"))
        act.wait_ge(*after("local.act", f"out {len(LOCAL) - 1}"))
        nc.scalar.activation(SQ[:, 0:1024], YD.rearrange("p a n -> p (a n)"), ACT.Square
                             ).then_inc(*did("norm.act", "sub square"))
        act_row(act, "sub", 1024, 0)
        for k in range(4):
            act.wait_ge(*after("local.dve", f"sub scaled {k}"))
            nc.scalar.activation(NH[:, 4 + k, 256:512], TMP[:, k % 2, 0:256], ACT.Copy
                                 ).then_inc(*did("local.act", f"sub high {k}"))
        if upto < 2:
            return
        make_high(act, first(12))
        for m in range(12, 20):
            make_high(act, first(m + 1))
            act.wait_ge(piece_used, first(m) + 1)
            G = (GA, GB)[(m - 12) // 4]
            c = 2 * ((m - 12) % 4)
            nc.scalar.activation(G[:, c:c + 2, :], PS[:, bank(m):bank(m) + 2, 0:256], ACT.Tanh, scale=0.5
                                 ).then_inc(*did("gates.act", f"tanh {m}"))
        for i, m in enumerate(range(20, 24)):
            make_high(act, first(m + 1))
            if i % 2:
                act.wait_ge(*after("gates.dve", f"merged {i // 2}"))
                c = 4 * (i // 2)
                nc.scalar.activation(NH[:, c:c + 4, 0:256], MG[:, c:c + 4, :], ACT.Copy
                                     ).then_inc(*did("gates.act", f"merged high {i // 2}"))
        for m in range(24, 28):
            make_high(act, first(m + 1))
        if upto < 4:
            return
        act_norm(act, 1, 512, lambda k: X[:, k, :], (evacuated, 28), (mem_in, 16))
        act_apply(act, 1, (0, 1), no_shift)
        for m in range(28, 31):
            make_high(act, first(m + 1))
        act_attention(act, "cross", CROSS)
        act.wait_ge(*after("norm.act", "1 high 7"))
        act.wait_ge(*after("norm.dve", "1 scaled 7"))
        act.dma_start(X[:, :, 256:512], A["ctxT"]).then_inc(ctx_in, 16)
        if upto < 5:
            return
        act_norm(act, 2, 256, lambda k: X[:, k, 0:256], (evacuated, 32))
        act_apply(act, 2, (0,), no_shift)
        act_router(act)
        act_experts(act)
        if upto < 6:
            return
        act_norm(act, 3, 256, lambda k: X[:, k, 0:256], after("moe.dve", "residual"))
        if upto < 7:
            return
        act_norm(act, 4, 512, lambda k: X[:, k, :], after("moe.dve", "final of first"),
                 (ctx_in, 16))
        act_apply(act, 4, (0, 1), mod_col(0, 0))
        act_ffn(act, 0)
        if upto < 8:
            return
        act_norm(act, 5, 512, lambda k: X[:, k, :], (lambda k: after("ffn.dve", f"residual 0 {k}")))
        act_apply(act, 5, (0, 1), mod_col(0, 3))
        act_even(act)
        if upto < 9:
            return
        act_norm(act, 6, 512, lambda k: X[:, k, :], (evacuated, Q["even"] + N_EVEN))
        act_apply(act, 6, (0, 1), mod_col(0, 6))
        act_ffn(act, 1)
        if upto < 10:
            return
        act_norm(act, 7, 512, lambda k: X[:, k, :], (lambda k: after("ffn.dve", f"residual 1 {k}")))
        act_apply(act, 7, (0, 1), mod_col(1, 0))
        act_ffn(act, 2)
        if upto < 11:
            return
        act_norm(act, 8, 512, lambda k: X[:, k, :], (lambda k: after("ffn.dve", f"residual 2 {k}")))
        act_apply(act, 8, (0, 1), mod_col(1, 3))
        for m in range(M["odd"], M["odd"] + 6):
            make_high(act, m + 1)
        act_attention(act, "odd", ODD)
        for m in range(M["odd"] + 6, M["odd"] + 10):
            make_high(act, m + 1)
        if upto < 12:
            return
        act_norm(act, 9, 256, lambda k: X[:, k, 0:256], (evacuated, Q["odd"] + N_ODD))
        act_apply(act, 9, (0,), mod_col(1, 6))
        act_ffn(act, 3)
        act_norm(act, 10, 256, lambda k: X[:, k, 0:256], (lambda k: after("ffn.dve", f"residual 3 {k}")))

    @block.gpsimd
    def _(pool):
        nc.gpsimd.memset(NEGH, -0.5).then_inc(*did("set.pool", "exponent"))
        pool.wait_ge(*after("set.pool", "exponent"))
        pool_rstd(pool, 0, 256)
        pool_rstd(pool, "sub", 1024)
        if upto < 4:
            return
        pool_rstd(pool, 1, 512)
        if upto < 5:
            return
        pool_rstd(pool, 2, 256)
        if upto < 6:
            return
        pool_rstd(pool, 3, 256)
        if upto < 7:
            return
        pool_rstd(pool, 4, 512)
        if upto < 8:
            return
        pool_rstd(pool, 5, 512)
        pool.wait_ge(*after("even.dve", "gating var"))
        nc.gpsimd.tensor_tensor(RS[:, 0:4], VAR[:, 0:4], NEGH[:, 0:4], ALU.pow
                                ).then_inc(*did("even.pool", "gating rstd"))
        pool.wait_ge(*after("even.dve", "head var"))
        nc.gpsimd.tensor_tensor(RS, VAR, NEGH, ALU.pow).then_inc(*did("even.pool", "head rstd"))
        if upto < 9:
            return
        pool_rstd(pool, 6, 512)
        if upto < 10:
            return
        pool_rstd(pool, 7, 512)
        if upto < 11:
            return
        pool_rstd(pool, 8, 512)
        if upto < 12:
            return
        pool_rstd(pool, 9, 256)
        pool_rstd(pool, 10, 256)

    @block.tensor
    def _(pe):
        pe.wait_ge(consts_in, 16)
        pe.wait_ge(*after("set.dve", "ones"))
        pe_norm(pe, 0, 256)
        pe_feature_major(pe, 0, 0, 256, norm=0)
        for m in range(1, 12):
            (pe_token_major if m in (4, 5, 10, 11) else pe_feature_major)(pe, m, m, 256)
        pe.wait_ge(*after("set.dve", "small low"))
        for b in range(2):
            for k in range(KC):
                t = slice(b * P, (b + 1) * P)
                w = [v[:, 8 * k:8 * k + 8] for v in (SWH, SWL)]
                last = mm3(PS[:, 6, 8 * b:8 * b + 8], [NH[:, k, t], NL[:, k, t]], w, k == 0, k == KC - 1)
        last.then_inc(*did("local.pe", "forget logits"))
        pe.wait_ge(evacuated, 12)
        pe_rope(pe, "local", DIFF_ROPE, "turn_half")
        pe.wait_ge(*after("local.dve", "log forget"))
        LF = PB[:, 0, 48:64]
        nc.tensor.matmul(PS[0:8, 6, 0:128], LF[:, 0:8], const("upto"), start=True, stop=True)
        nc.tensor.matmul(PS[0:8, 6, 128:256], LF[:, 8:16], const("upto"), start=True, stop=False)
        nc.tensor.matmul(PS[0:8, 6, 128:256], LF[:, 0:8], ONES[:, :], start=False, stop=True
                         ).then_inc(*did("local.pe", "cumulated"))
        pe.wait_ge(*after("local.dve", "cumulated"))
        pe.wait_ge(*after("local.dve", "roped 3"))
        pe.wait_ge(*after("set.dve", "condition"))
        pe_attention(pe, "local", LOCAL)
        pe.wait_ge(*after("norm.act", "sub square"))
        for i in range(2):
            last = nc.tensor.matmul(PS[:, 4 + i, :], ONES[:, :], SQ[:, 512 * i:512 * i + 512],
                                    start=True, stop=True)
        last.then_inc(*did("norm.pe", "sub sum 0"))
        pe_compact(pe, "sub", 1024, 1)
        pe_broadcast(pe, "sub", 1024)
        if upto < 2:
            return
        for m in range(12, 20):
            pe_feature_major(pe, first(m), m, 256)
        pe.wait_ge(*after("local.dve", "sub low 3"))
        for i, m in enumerate(range(20, 24)):
            o = 4 * (i % 2)
            pe_feature_major(pe, first(m), m, 256, kc=4, cols=512,
                             xs=lambda k, o=o: [NH[:, o + k, 256:512], NL[:, o + k, 256:512]])
        pe.wait_ge(*after("gates.dve", "merged low 1"))
        for m in range(24, 28):
            pe_feature_major(pe, first(m), m, 256)
        if upto < 4:
            return
        pe_norm(pe, 1, 512)
        pe_feature_major(pe, first(28), 28, 256, norm=1)
        pe_feature_major(pe, first(29), 29, 256, off=256)
        pe_token_major(pe, first(30), 30, 256, off=256)
        pe.wait_ge(evacuated, 31)
        pe_attention(pe, "cross", CROSS)
        pe.wait_ge(*after("cross.dve", f"out {len(CROSS) - 1}"))
        pe_claim(pe, first(31), 31)
        pe.wait_ge(evacuated, 31)
        w = weights(first(31), 2, D)
        for c in range(KC):
            for k in range(2):
                last = mm3(PS[:, c // 2, (c % 2) * 256:(c % 2) * 256 + 256],
                           [v[:, k, c * P:(c + 1) * P] for v in w],
                           [NH[:, k, 0:256], NL[:, k, 0:256]], k == 0, k == 1)
        last.then_inc(piece_used, 1)
        if upto < 5:
            return
        pe_norm(pe, 2, 256)
        pe_applied(pe, 2)
        pe_router(pe)
        pe.wait_ge(evacuated, 32)
        pe_experts(pe)
        if upto < 6:
            return
        pe_norm(pe, 3, 256)
        if upto < 7:
            return
        pe_norm(pe, 4, 512)
        pe_ffn(pe, 0)
        if upto < 8:
            return
        pe_norm(pe, 5, 512)
        pe_even(pe)
        if upto < 9:
            return
        pe_norm(pe, 6, 512)
        pe_ffn(pe, 1)
        if upto < 10:
            return
        pe_norm(pe, 7, 512)
        pe_ffn(pe, 2)
        if upto < 11:
            return
        pe_norm(pe, 8, 512)
        m0, q0 = M["odd"], Q["odd"]
        for j in range(4):
            pe_feature_major(pe, m0 + j, q0 + j, 256, norm=8 if j == 0 else None)
        pe_feature_major(pe, m0 + 4, q0 + 4, 512)
        pe_token_major(pe, m0 + 5, q0 + 5, 512)
        pe.wait_ge(evacuated, q0 + 6)
        pe_rope(pe, "odd", ODD_ROPE, "turn_pair")
        pe.wait_ge(*after("odd.dve", "roped 4"))
        pe_attention(pe, "odd", ODD)
        pe.wait_ge(*after("odd.dve", f"out {len(ODD) - 1}"))
        for j in range(6, 10):
            pe_feature_major(pe, m0 + j, q0 + j, 256)
        if upto < 12:
            return
        pe_norm(pe, 9, 256)
        pe_ffn(pe, 3)
        pe_norm(pe, 10, 256)

    @block.vector
    def _(dve):
        nc.vector.memset(ONES[:, :], 1.0)
        nc.vector.memset(ZERO, 0.0).then_inc(*did("set.dve", "ones"))
        dve.wait_ge(*after("set.dve", "ones"))
        dve.wait_ge(params_in, 16)
        a0 = PARAM_AT["w_fgate"][0]
        dve.wait_ge(*after("set.act", "small high"))
        nc.vector.tensor_tensor(SWL[:, :], PARAM[:, a0:a0 + 480], SWH[:, :].bitcast(F32), ALU.subtract
                                ).then_inc(*did("set.dve", "small low"))
        nc.vector.tensor_scalar(NSINK, param("sink"), -1.0, None, ALU.mult)
        k_step = [0]

        def chain(ins, label=None):
            k_step[0] += 1
            name = label or f"set {k_step[0]}"
            ins.then_inc(*did("set.dve", name))
            dve.wait_ge(*after("set.dve", name))
        two_pi = 2.0 * np.pi
        p1 = 6.28125
        p2 = float(np.float32(np.round((two_pi - p1) * 2 ** 20) / 2 ** 20))
        p3 = float(two_pi - p1 - p2)
        dve.wait_ge(pos_in, 16)
        dve.wait_ge(consts_in, 16)
        chain(nc.vector.tensor_copy(ANG, ANGK.bitcast(I32)))
        chain(nc.vector.tensor_scalar(ANG, ANG, const("inv_freq"), None, ALU.mult))
        for which in ("cosine", "sine"):
            turns = ANGK
            chain(nc.vector.tensor_scalar(turns, ANG, float(1.0 / two_pi), 0.25 if which == "cosine" else 0.0,
                                          ALU.mult, ALU.add))
            chain(nc.vector.tensor_scalar(turns, turns, MAGIC, None, ALU.add))
            chain(nc.vector.tensor_scalar(turns, turns, MAGIC, None, ALU.subtract))
            dst = ANGR if which == "cosine" else ANG
            chain(nc.vector.scalar_tensor_tensor(dst, turns, -p1, ANG, ALU.mult, ALU.add))
            chain(nc.vector.scalar_tensor_tensor(dst, turns, -p2, dst, ALU.mult, ALU.add))
            chain(nc.vector.scalar_tensor_tensor(dst, turns, -p3, dst, ALU.mult, ALU.add))
            if which == "cosine":
                chain(nc.vector.tensor_scalar(dst, dst, float(np.pi / 2), None, ALU.add))
            chain(nc.vector.tensor_scalar(dst, dst, 3.1415925, -3.1415925, ALU.min, ALU.max),
                  f"{which} angle")
        prod = TB[:, 0, 0:128]
        chain(nc.vector.tensor_tensor(prod, param("lam_a"), param("lam_b"), ALU.mult))
        chain(nc.vector.tensor_reduce(LE, prod.rearrange("p (a n) -> p a n", a=2), AX.X, ALU.add),
              "lambda sums")
        dve.wait_ge(*after("set.act", "lambda exps"))
        chain(nc.vector.scalar_tensor_tensor(LAM, LE[:, 0:1], LAMBDA_INIT, LE[:, 1:2], ALU.add, ALU.subtract))
        dve.wait_ge(*after("set.act", "cosine"))
        dve.wait_ge(*after("set.act", "condition tanh"))
        chain(nc.vector.scalar_tensor_tensor(COND, TB[:, 1, 0:16], 1.0, COND, ALU.add, ALU.mult))
        chain(nc.vector.tensor_scalar(COND, COND, 0.5, None, ALU.mult), "condition")

        make_low(dve, 0)
        dve_norm(dve, 0, 256)
        dve_apply(dve, 0, (0,), gain("g_mix"), no_shift)
        dests = [(FQ, .125), (FK, None), (FV, None), (DQ, .125), (DK, None), (DV, None)]
        for m in range(QKV_PIECES):
            if m + 1 < QKV_PIECES:
                make_low(dve, m + 1)
            dst, scale = dests[m // 2]
            if m in (4, 5, 10, 11):
                evac_copy(dve, m, m, dst[:, :, 256 * (m % 2):256 * (m % 2) + 256])
            else:
                evac_copy(dve, m, m, dst[:, 2 * (m % 2):2 * (m % 2) + 2, :], scale)
        FZ, FL, LF = PB[:, 0, 0:16], PB[:, 0, 32:48], PB[:, 0, 48:64]
        dve.wait_ge(*after("local.pe", "forget logits"))
        nc.vector.tensor_tensor(v3(FZ, 2), v3(PS[:, 6, 0:16], 2),
                                param("b_fgate").unsqueeze(1).to_broadcast([P, 2, 8]), ALU.add
                                ).then_inc(*did("local.dve", "forget logits"))
        dve.wait_ge(evacuated, 12)
        dve_rope(dve, "local", DIFF_ROPE, COSD, SIND)
        dve.wait_ge(*after("local.act", "forget ln"))
        nc.vector.scalar_tensor_tensor(LF, FZ, 0.0, FL, ALU.min, ALU.subtract
                                       ).then_inc(*did("local.dve", "log forget"))
        dve.wait_ge(*after("local.pe", "cumulated"))
        nc.vector.tensor_copy(C8, PS[0:8, 6, 0:256])
        nc.vector.tensor_scalar(NC8, PS[0:8, 6, 0:256], -1.0, None, ALU.mult
                                ).then_inc(*did("local.dve", "cumulated"))
        dve_attention(dve, "local", LOCAL)
        dve_ada(dve, local_fill(len(LOCAL) - 1, 1))
        dve_mod_ready(dve, ADA_LOCAL, [(0, 1), (0, 4), (0, 7)], [(0, 2)])
        dve_variance(dve, "sub", 1024, 1e-5)
        dve_diagonal(dve, "sub", 1024)
        dve.wait_ge(*after("norm.pe", "sub bcast"))
        for k in range(4):
            src = PS[:, 4 + k // 2, (k % 2) * 256:(k % 2) * 256 + 256]
            if k >= 2:
                dve.wait_ge(*after("local.act", f"sub high {k - 2}"))
            nc.vector.scalar_tensor_tensor(TMP[:, k % 2, 256:512], YD[:, k, :], param("g_sub"), src,
                                           ALU.mult, ALU.mult).then_inc(*did("local.dve", f"sub norm {k}"))
            dve.wait_ge(*after("local.dve", f"sub norm {k}"))
            nc.vector.tensor_scalar(TMP[:, k % 2, 0:256], TMP[:, k % 2, 256:512], 1.0 - LAMBDA_INIT, None,
                                    ALU.mult).then_inc(*did("local.dve", f"sub scaled {k}"))
            dve.wait_ge(*after("local.act", f"sub high {k}"))
            nc.vector.tensor_tensor(NL[:, 4 + k, 256:512], TMP[:, k % 2, 0:256],
                                    NH[:, 4 + k, 256:512].bitcast(F32), ALU.subtract
                                    ).then_inc(*did("local.dve", f"sub low {k}"))
        if upto < 2:
            nc.vector.tensor_copy(X[:, 0:4, 0:256], YD).then_inc(*did("end.dve", "result"))
            return
        make_low(dve, first(12))
        for m in range(12, 20):
            make_low(dve, first(m + 1))
            dve.wait_ge(*after("gates.act", f"tanh {m}"))
            G = (GA, GB)[(m - 12) // 4]
            c = 2 * ((m - 12) % 4)
            nc.vector.tensor_scalar(G[:, c:c + 2, :], G[:, c:c + 2, :], 0.5, 0.5, ALU.mult, ALU.add
                                    ).then_inc(evacuated, 1)
        dve.wait_ge(evacuated, 20)
        for i, m in enumerate(range(20, 24)):
            make_low(dve, first(m + 1))
            dve.wait_ge(piece_used, first(m) + 1)
            c = 4 * (i // 2)
            G = (GA, GB)[i % 2]
            src = PS[:, bank(m):bank(m) + 2, :].rearrange("p b (a n) -> p (b a) n", a=2)
            if i % 2 == 0:
                nc.vector.tensor_tensor(MG[:, c:c + 4, :], src, G[:, c:c + 4, :], ALU.mult
                                        ).then_inc(evacuated, 1)
            else:
                nc.vector.tensor_tensor(G[:, c:c + 4, :], src, G[:, c:c + 4, :], ALU.mult
                                        ).then_inc(evacuated, 1)
                dve.wait_ge(evacuated, m + 1)
                nc.vector.tensor_tensor(MG[:, c:c + 4, :], MG[:, c:c + 4, :], G[:, c:c + 4, :], ALU.add
                                        ).then_inc(*did("gates.dve", f"merged {i // 2}"))
                dve.wait_ge(*after("gates.act", f"merged high {i // 2}"))
                nc.vector.tensor_tensor(NL[:, c:c + 4, 0:256], MG[:, c:c + 4, :],
                                        NH[:, c:c + 4, 0:256].bitcast(F32), ALU.subtract
                                        ).then_inc(*did("gates.dve", f"merged low {i // 2}"))

        def residual(m0, q0, n, scale=None):
            for i in range(n):
                make_low(dve, m0 + i + 1)
                dve.wait_ge(piece_used, m0 + i + 1)
                x = X[:, 2 * i:2 * i + 2, 0:256]
                if scale is None:
                    ins = nc.vector.tensor_tensor(x, PS[:, bank(q0 + i):bank(q0 + i) + 2, 0:256], x, ALU.add)
                    ins.then_inc(evacuated, 1)
                else:
                    for c in range(2):
                        k = 2 * i + c
                        ins = nc.vector.scalar_tensor_tensor(X[:, k, 0:256], PS[:, bank(q0 + i) + c, 0:256],
                                                             scale(k, 0), X[:, k, 0:256], ALU.mult, ALU.add)
                    ins.then_inc(evacuated, 1)
            dve.wait_ge(evacuated, q0 + n)

        residual(first(24), 24, 4)
        if upto < 4:
            finish(dve)
            return
        dve_norm(dve, 1, 512)
        dve_apply(dve, 1, (0, 1), gain("g_cross", "g_mem"), no_shift)
        make_low(dve, first(29))
        evac_copy(dve, first(28), 28, CQ, .125)
        make_low(dve, first(30))
        evac_copy(dve, first(29), 29, CK)
        make_low(dve, first(31))
        evac_copy(dve, first(30), 30, CV)
        dve_attention(dve, "cross", CROSS)
        dve.wait_ge(piece_used, M["expert"])
        nc.vector.tensor_tensor(X[:, :, 0:256], PS[:, 0:4, :].rearrange("p b (a n) -> p (b a) n", a=2),
                                X[:, :, 0:256], ALU.add).then_inc(evacuated, 1)
        dve.wait_ge(evacuated, 32)
        if upto < 5:
            finish(dve)
            return
        dve.wait_ge(evacuated, 32)
        dve_norm(dve, 2, 256)
        dve_apply(dve, 2, (0,), gain("g_ffn"), no_shift)
        dve_router(dve)
        dve_experts(dve)
        if upto < 6:
            finish(dve)
            return
        dve.wait_ge(*after("moe.dve", "residual"))
        dve_norm(dve, 3, 256)
        for k in range(KC):
            ins = nc.vector.scalar_tensor_tensor(X[:, k, 0:256], X[:, k, 0:256], param("g_final")[:, k:k + 1],
                                                 PS[:, 4, 0:256], ALU.mult, ALU.mult)
        ins.then_inc(*did("moe.dve", "final of first"))
        if upto < 7:
            finish(dve)
            return
        dve.wait_ge(*after("ada.dve", f"mod ready {ADA_LOCAL}"))
        dve_norm(dve, 4, 512)
        dve_apply(dve, 4, (0, 1), mod_col(0, 1), mod_col(0, 0))
        dve_ffn(dve, 0, 0, 2)
        if upto < 8:
            finish(dve)
            return
        dve.wait_ge(*after("ffn.dve", f"residual 0 {TAIL[-1]}"))
        dve_norm(dve, 5, 512)
        dve_apply(dve, 5, (0, 1), mod_col(0, 4), mod_col(0, 3))
        dve_even(dve)
        if upto < 9:
            finish(dve)
            return
        dve_norm(dve, 6, 512)
        dve_apply(dve, 6, (0, 1), mod_col(0, 7), mod_col(0, 6))
        dve_ffn(dve, 1, 0, 8)
        if upto < 10:
            finish(dve)
            return
        dve.wait_ge(*after("ffn.dve", f"residual 1 {TAIL[-1]}"))
        dve.wait_ge(*after("ada.dve", f"mod ready {N_ADA}"))
        dve_norm(dve, 7, 512)
        dve_apply(dve, 7, (0, 1), mod_col(1, 1), mod_col(1, 0))
        dve_ffn(dve, 2, 1, 2)
        if upto < 11:
            finish(dve)
            return
        dve.wait_ge(*after("ffn.dve", f"residual 2 {TAIL[-1]}"))
        dve_norm(dve, 8, 512)
        dve_apply(dve, 8, (0, 1), mod_col(1, 4), mod_col(1, 3))
        m0, q0 = M["odd"], Q["odd"]
        for j in range(4):
            make_low(dve, m0 + j + 1)
            evac_copy(dve, m0 + j, q0 + j, OQ[:, 2 * j:2 * j + 2, :], .125)
        make_low(dve, m0 + 5)
        evac_copy(dve, m0 + 4, q0 + 4, OK, T=512)
        make_low(dve, m0 + 6)
        evac_copy(dve, m0 + 5, q0 + 5, OV.rearrange("p (b a) n -> p b (a n)", b=2), T=512)
        dve.wait_ge(evacuated, q0 + 6)
        dve_rope(dve, "odd", ODD_ROPE, const("cos_x"), const("sin_x"))
        dve_attention(dve, "odd", ODD)
        residual(m0 + 6, q0 + 6, 4, mod_col(1, 5))
        if upto < 12:
            finish(dve)
            return
        dve_norm(dve, 9, 256)
        dve_apply(dve, 9, (0,), mod_col(1, 7), mod_col(1, 6))
        dve_ffn(dve, 3, 1, 8)
        dve.wait_ge(*after("ffn.dve", f"residual 3 {TAIL[-1]}"))
        dve_norm(dve, 10, 256)
        for k in range(KC):
            ins = nc.vector.scalar_tensor_tensor(X[:, k, 0:256], X[:, k, 0:256],
                                                 param("final_norm")[:, k:k + 1], PS[:, 4, 0:256],
                                                 ALU.mult, ALU.mult)
        ins.then_inc(*did("end.dve", "result"))

    ctx.close()
    return steps.made


def pieces(w):
    k, n = w.shape
    return w.reshape(k // P, P, n // 256, 256).transpose(2, 1, 0, 3).reshape(n // 256, P, PIECE)


def feature_major(t):
    return np.ascontiguousarray(t.T.reshape(KC, P, -1).transpose(1, 0, 2))


def chunk_columns(v):
    return v.reshape(-1, P).T


def lay_out(I):
    w_in = I["w_in"][0]
    first = [pieces(w_in[:, 0:1536]), pieces(w_in[:, 1544:3080]), pieces(w_in[:, 3080:5128])]
    br = [I[n][0].reshape(4, P, 2, 512).transpose(2, 1, 0, 3).reshape(2, 1, P, PIECE)
          for n in ("w_branch_a", "w_branch_b")]
    first += [br[0][0], br[1][0], br[0][1], br[1][1], pieces(I["w_out"][0]), pieces(I["w_cq"][0]),
              pieces(I["w_ckv"][0]), I["w_co"][0].reshape(2, P, D).transpose(1, 0, 2).reshape(1, P, PIECE)]
    gate = I["w_exp_gate"][0].reshape(EXPERTS, KC, P, 4, 1, P)
    up = I["w_exp_up"][0].reshape(EXPERTS, KC, P, 4, 1, P)
    gu = np.concatenate([gate, up], 4).transpose(0, 3, 2, 1, 4, 5).reshape(EXPERTS, 4, P, PIECE)
    down = I["w_exp_down"][0].reshape(EXPERTS, 4, P, 2, 512).transpose(0, 3, 2, 1, 4).reshape(EXPERTS, 2, P, PIECE)
    expert = np.concatenate([gu, down], 1).reshape(EXPERTS * 6, P, PIECE)
    ada = np.concatenate([pieces(w) for w in I["ada_w_2"]], 0)
    fi = I["ffn_w_in_2"].reshape(4, KC, P, 2, FF_CHUNKS, P).transpose(0, 4, 2, 1, 3, 5)
    fi = fi.reshape(4 * FF_CHUNKS, P, PIECE)
    fo = I["ffn_w_out_2"].reshape(4, N_DOWN, 2, P, D).transpose(0, 1, 3, 2, 4).reshape(4 * N_DOWN, P, PIECE)
    we = I["even_w_in_2"][0]
    even = np.concatenate([pieces(we[:, 0:2048]), pieces(we[:, 2064:3088]), pieces(I["even_w_out_2"][0])], 0)
    wq = I["odd_w_qkv_2"][0]
    order = [h for c in range(8) for h in (8 * (c // 4) + c % 4, 8 * (c // 4) + 4 + c % 4)]
    q = wq[:, 0:D].reshape(D, 16, HD)[:, order].reshape(D, D)
    wo = I["odd_w_out_2"][0].reshape(16, HD, D)[order].reshape(D, D)
    odd = np.concatenate([pieces(q), pieces(wq[:, D:D + 512]), pieces(wo)], 0)

    def rows(v):
        return np.broadcast_to(v.reshape(1, -1), (P, v.size))

    def k_major(w):
        return w.reshape(KC, P, -1).transpose(1, 0, 2).reshape(P, -1)

    f = {}
    for n in ("g_mix", "g_cross", "g_mem", "g_ffn"):
        f[n] = chunk_columns(I[n][0])
    f["g_final"], f["final_norm"] = chunk_columns(I["g_final"]), chunk_columns(I["final_norm_2"])
    f["g_sub"] = I["g_diff_sub"][0].reshape(P, 1)
    f["lam_a"] = rows(np.concatenate([I["lambda_q1"][0], I["lambda_q2"][0]]))
    f["lam_b"] = rows(np.concatenate([I["lambda_k1"][0], I["lambda_k2"][0]]))
    f["w_fgate"] = k_major(w_in[:, 1536:1544])
    f["w_router"] = k_major(np.concatenate([I["w_group"][0], I["w_expert"][0]], 1))
    f["w_gates"] = k_major(we[:, 2048:2064])
    f["b_fgate"] = rows(I["b_fgate"][0])
    f["b_router"] = rows(np.concatenate([I["b_group"][0], I["b_expert"][0]]))
    f["ada_b"] = np.concatenate([chunk_columns(v) for v in I["ada_b_2"]], 1)
    f["conv_w"] = I["mlstm_conv_2"][0].reshape(3, KC, P).transpose(2, 1, 0).reshape(P, 24)
    f["gate_b"] = rows(I["mlstm_gate_b_2"][0])
    f["mnorm"] = I["mlstm_norm_2"][0].T
    f["sgu_norm"] = rows(I["sgu_norm_2"][0])
    f["sgu_ws"] = I["sgu_ws_2"][0].transpose(2, 0, 1).reshape(P, 512)
    f["sgu_b"] = rows(I["sgu_b_2"][0])
    f["sink"] = rows(I["attn_sink_2"][0])
    f["cond"] = np.stack([I["c_2"][0].reshape(KC, P).T, I["c_ctx_2"].reshape(KC, P).T], 2).reshape(P, 16)
    params = np.concatenate([f[n] for n, _ in PARAM_FIELDS], 1)
    assert params.shape == (P, N_PARAM)
    arrays = dict(w_first=np.concatenate(first, 0), w_expert=expert, w_ada=ada, w_up=fi, w_down=fo,
                  w_even=even, w_odd=odd, params=params, consts=shape_constants(),
                  positions=np.broadcast_to(I["positions"].reshape(1, TOK).astype(np.int32), (P, TOK)),
                  xT=feature_major(I["x"][0]), memT=feature_major(I["mem"][0]),
                  ctxT=feature_major(I["ctx_2"][0]))
    return {k: np.ascontiguousarray(v) for k, v in arrays.items()}


def make_program(nc, draft, arrays, upto=99):

    def declare(nc):
        a = {k: nc.dram_tensor(k, v.shape, mybir.dt.from_np(v.dtype), kind="ExternalInput").ap()
             for k, v in arrays.items()}
        a["out"] = nc.dram_tensor("out_dram", (P, KC, TOK), F32, kind="ExternalOutput").ap()
        return a
    known = build(draft, declare(draft), None, upto)
    build(nc, declare(nc), known, upto)


def kernel(**inputs):
    import concourse.bacc as bacc
    from concourse.bass_utils import run_bass_kernel_spmd
    arrays = lay_out({k: np.asarray(v) for k, v in inputs.items()})
    nc, draft = (bacc.Bacc("TRN2", target_bir_lowering=False, num_devices=1) for _ in range(2))
    make_program(nc, draft, arrays)
    r = run_bass_kernel_spmd(nc, [arrays], core_ids=[0])
    out = np.asarray(r.results[0]["out_dram"])
    return np.ascontiguousarray(out.transpose(1, 0, 2).reshape(D, TOK).T).reshape(1, TOK, D)
```
